# Optimizing a Trainium2 kernel written in Bass

```python
import jax, jax.numpy as jnp
from jax import lax
import numpy as np

D_MODEL = 1024
BATCH = 1
SEQ = 512
DEPTH = 2
DEC_BATCH = 8
DEC_SEQ = 8
PAST_LEN = 2048
PAGE_SIZE = 128

N_MIXERS = 2
N_ATTN_LAYERS = (DEPTH + N_MIXERS - 1) // N_MIXERS
N_REC_LAYERS = DEPTH // N_MIXERS
N_HEADS = 16
QK_NOPE = 64
QK_ROPE = 32
V_HEAD = 64
Q_LORA = 512
KV_LORA = 256
ROPE_THETA = 10000.0
SOFTMAX_SCALE = (QK_NOPE + QK_ROPE) ** -0.5
Q_BLOCK = 128
LRU_WIDTH = D_MODEL
N_LRU_BLOCKS = 8
LRU_BLOCK = LRU_WIDTH // N_LRU_BLOCKS
LRU_C = 8.0
REC_CONV_W = 4
D_FF = 3 * D_MODEL
FFN_CONV_W = 3
EPS = 1e-6

kernel_name = "hybrid_mla_rglru_convffn_step"

def rmsnorm(x, g):
    xf = x.astype(jnp.float32)
    y = xf * lax.rsqrt(jnp.mean(xf * xf, axis=-1, keepdims=True) + EPS)
    return (y * g.astype(jnp.float32)).astype(x.dtype)

def rope_cos_sin(pos):
    inv = ROPE_THETA ** (-jnp.arange(0, QK_ROPE, 2, dtype=jnp.float32) / QK_ROPE)
    ang = pos.astype(jnp.float32)[:, None] * inv[None, :]
    return jnp.cos(ang), jnp.sin(ang)

def apply_rope(x, cos, sin):
    half = x.shape[-1] // 2
    x1 = x[..., :half].astype(jnp.float32)
    x2 = x[..., half:].astype(jnp.float32)
    return jnp.concatenate([x1 * cos - x2 * sin, x1 * sin + x2 * cos], axis=-1).astype(x.dtype)

def causal_dwconv(x, buf, w, b):
    t = x.shape[1]
    width = w.shape[0]
    xp = jnp.concatenate([buf.astype(x.dtype), x], axis=1)
    y = xp[:, 0:t] * w[0] + b
    for k in range(1, width):
        y = y + xp[:, k:k + t] * w[k]
    return y, xp[:, t:]

def block_diag(x, w, b):
    xb = x.reshape(x.shape[:-1] + (N_LRU_BLOCKS, LRU_BLOCK))
    y = jnp.einsum('btnc,ncd->btnd', xb, w) + b
    return y.reshape(x.shape)

def rglru(x, h0, w_a, b_a, w_i, b_i, lam):
    r = jax.nn.sigmoid(block_diag(x, w_a, b_a).astype(jnp.float32))
    gi = jax.nn.sigmoid(block_diag(x, w_i, b_i).astype(jnp.float32))
    log_a = -LRU_C * r * jax.nn.softplus(-lam.astype(jnp.float32))
    a = jnp.exp(log_a)
    bx = jnp.sqrt(-jnp.expm1(2.0 * log_a)) * (gi * x.astype(jnp.float32))

    def step(h, inp):
        a_t, b_t = inp
        h = a_t * h + b_t
        return h, h

    h_last, hs = lax.scan(step, h0.astype(jnp.float32), (jnp.moveaxis(a, 1, 0), jnp.moveaxis(bx, 1, 0)))
    return jnp.moveaxis(hs, 0, 1).astype(x.dtype), h_last.astype(x.dtype)

def recurrent_mixer(xn, h0, conv_buf, w_in, conv_w, conv_b, w_a, b_a, w_i, b_i, lam, w_out):
    z = xn @ w_in
    xr, gate_in = z[..., :LRU_WIDTH], z[..., LRU_WIDTH:]
    gate = jax.nn.gelu(gate_in, approximate=True)
    xc, new_buf = causal_dwconv(xr, conv_buf, conv_w, conv_b)
    y, h_last = rglru(xc, h0, w_a, b_a, w_i, b_i, lam)
    return (y * gate) @ w_out, h_last, new_buf

def conv_ffn(xn, buf, w_up, conv_w, conv_b, w_down):
    gu = xn @ w_up
    g, u = gu[..., :D_FF], gu[..., D_FF:]
    gc, new_buf = causal_dwconv(g, buf, conv_w, conv_b)
    return (jax.nn.silu(gc) * u) @ w_down, new_buf

def mla_project(xn, pos, w_down, g_q_lora, w_uq, g_kv_lora, g_qn, g_qr, g_kr):
    b, t = xn.shape[:2]
    d = xn @ w_down
    cq = rmsnorm(d[..., :Q_LORA], g_q_lora)
    c_kv = rmsnorm(d[..., Q_LORA:Q_LORA + KV_LORA], g_kv_lora)
    kr = d[..., Q_LORA + KV_LORA:]
    q = (cq @ w_uq).reshape(b, t, N_HEADS, QK_NOPE + QK_ROPE)
    cos, sin = rope_cos_sin(pos)
    q_nope = rmsnorm(q[..., :QK_NOPE], g_qn)
    q_rope = apply_rope(rmsnorm(q[..., QK_NOPE:], g_qr), cos[:, None], sin[:, None])
    k_rope = apply_rope(rmsnorm(kr, g_kr), cos, sin)
    return q_nope, q_rope, c_kv, k_rope

def mla_prompt(q_nope, q_rope, c_kv, k_rope, w_uk, w_uv, g_kn):
    b, t = c_kv.shape[:2]
    k_nope = rmsnorm(jnp.einsum('btc,chd->bthd', c_kv, w_uk), g_kn)
    v = jnp.einsum('btc,chd->bthd', c_kv, w_uv)
    key_pos = jnp.arange(t)

    def attend_block(i):
        start = i * Q_BLOCK
        qn = lax.dynamic_slice_in_dim(q_nope, start, Q_BLOCK, axis=1)
        qr = lax.dynamic_slice_in_dim(q_rope, start, Q_BLOCK, axis=1)
        s = jnp.einsum('bqhd,bkhd->bhqk', qn, k_nope) + jnp.einsum('bqhr,bkr->bhqk', qr, k_rope)
        q_pos = start + jnp.arange(Q_BLOCK)
        mask = key_pos[None, :] <= q_pos[:, None]
        p = jax.nn.softmax(jnp.where(mask, s.astype(jnp.float32) * SOFTMAX_SCALE, -jnp.inf), axis=-1)
        return jnp.einsum('bhqk,bkhd->bqhd', p.astype(v.dtype), v)

    o = lax.map(attend_block, jnp.arange(t // Q_BLOCK))
    return jnp.moveaxis(o, 0, 1).reshape(b, t, N_HEADS * V_HEAD)

def mla_sample(q_nope, q_rope, c_kv, k_rope, page_table, cache_ckv, cache_krope, layer, w_uk, w_uv, g_kn):
    s_new = c_kv.shape[1]
    past = page_table.shape[1] * PAGE_SIZE
    key_pos = jnp.arange(past + s_new)
    q_pos = past + jnp.arange(s_new)
    mask = key_pos[None, :] <= q_pos[:, None]

    def attend_seq(args):
        pt, qn, qr, cn, krn = args
        c_all = jnp.concatenate([cache_ckv[layer, pt].reshape(past, KV_LORA).astype(cn.dtype), cn], axis=0)
        kr_all = jnp.concatenate([cache_krope[layer, pt].reshape(past, QK_ROPE).astype(krn.dtype), krn], axis=0)
        k_nope = rmsnorm(jnp.einsum('lc,chd->lhd', c_all, w_uk), g_kn)
        s = jnp.einsum('qhd,lhd->hql', qn, k_nope) + jnp.einsum('qhr,lr->hql', qr, kr_all)
        p = jax.nn.softmax(jnp.where(mask[None], s.astype(jnp.float32) * SOFTMAX_SCALE, -jnp.inf), axis=-1)
        ctx = jnp.einsum('hql,lc->qhc', p.astype(c_all.dtype), c_all)
        return jnp.einsum('qhc,chd->qhd', ctx, w_uv).reshape(s_new, N_HEADS * V_HEAD)

    return lax.map(attend_seq, (page_table, q_nope, q_rope, c_kv, k_rope))

def setup_inputs(seed: int = 0) -> dict:
    key = jax.random.key(seed)
    ks = iter(jax.random.split(key, 48))

    def nrm(shape, scale):
        return jax.random.normal(next(ks), shape, jnp.float32) * scale

    def gain(shape):
        return 1.0 + nrm(shape, 0.02)

    n_pages = PAST_LEN // PAGE_SIZE
    n_used = DEC_BATCH * n_pages
    n_pool = n_used + max(1, n_used // 4)
    page_table = jax.random.permutation(next(ks), n_pool)[:n_used].astype(jnp.int32).reshape(DEC_BATCH, n_pages)

    u = jax.random.uniform(next(ks), (N_REC_LAYERS, LRU_WIDTH), jnp.float32, 0.9, 0.999)
    s_lam = u ** (1.0 / LRU_C)
    rec_lambda = jnp.log(s_lam / (1.0 - s_lam))

    return {
        "x_prompt": nrm((BATCH, SEQ, D_MODEL), 1.0),
        "x_sample": nrm((DEC_BATCH, DEC_SEQ, D_MODEL), 1.0),
        "cache_ckv": nrm((N_ATTN_LAYERS, n_pool, PAGE_SIZE, KV_LORA), 1.0),
        "cache_krope": nrm((N_ATTN_LAYERS, n_pool, PAGE_SIZE, QK_ROPE), 1.0),
        "page_table": page_table,
        "state_lru_h": nrm((N_REC_LAYERS, DEC_BATCH, LRU_WIDTH), 0.5),
        "state_lru_conv": nrm((N_REC_LAYERS, DEC_BATCH, REC_CONV_W - 1, LRU_WIDTH), 1.0),
        "state_ffn_conv": nrm((DEPTH, DEC_BATCH, FFN_CONV_W - 1, D_FF), 1.0),
        "norm_mix": gain((DEPTH, D_MODEL)),
        "norm_ffn": gain((DEPTH, D_MODEL)),
        "attn_w_down": nrm((N_ATTN_LAYERS, D_MODEL, Q_LORA + KV_LORA + QK_ROPE), D_MODEL ** -0.5),
        "attn_g_q_lora": gain((N_ATTN_LAYERS, Q_LORA)),
        "attn_w_uq": nrm((N_ATTN_LAYERS, Q_LORA, N_HEADS * (QK_NOPE + QK_ROPE)), Q_LORA ** -0.5),
        "attn_g_kv_lora": gain((N_ATTN_LAYERS, KV_LORA)),
        "attn_g_qn": gain((N_ATTN_LAYERS, QK_NOPE)),
        "attn_g_qr": gain((N_ATTN_LAYERS, QK_ROPE)),
        "attn_g_kn": gain((N_ATTN_LAYERS, QK_NOPE)),
        "attn_g_kr": gain((N_ATTN_LAYERS, QK_ROPE)),
        "attn_w_uk": nrm((N_ATTN_LAYERS, KV_LORA, N_HEADS, QK_NOPE), KV_LORA ** -0.5),
        "attn_w_uv": nrm((N_ATTN_LAYERS, KV_LORA, N_HEADS, V_HEAD), KV_LORA ** -0.5),
        "attn_w_o": nrm((N_ATTN_LAYERS, N_HEADS * V_HEAD, D_MODEL), (N_HEADS * V_HEAD) ** -0.5),
        "rec_w_in": nrm((N_REC_LAYERS, D_MODEL, 2 * LRU_WIDTH), D_MODEL ** -0.5),
        "rec_conv_w": nrm((N_REC_LAYERS, REC_CONV_W, LRU_WIDTH), REC_CONV_W ** -0.5),
        "rec_conv_b": nrm((N_REC_LAYERS, LRU_WIDTH), 0.01),
        "rec_w_a": nrm((N_REC_LAYERS, N_LRU_BLOCKS, LRU_BLOCK, LRU_BLOCK), LRU_BLOCK ** -0.5),
        "rec_b_a": nrm((N_REC_LAYERS, N_LRU_BLOCKS, LRU_BLOCK), 0.01),
        "rec_w_i": nrm((N_REC_LAYERS, N_LRU_BLOCKS, LRU_BLOCK, LRU_BLOCK), LRU_BLOCK ** -0.5),
        "rec_b_i": nrm((N_REC_LAYERS, N_LRU_BLOCKS, LRU_BLOCK), 0.01),
        "rec_lambda": rec_lambda,
        "rec_w_out": nrm((N_REC_LAYERS, LRU_WIDTH, D_MODEL), LRU_WIDTH ** -0.5),
        "ffn_w_up": nrm((DEPTH, D_MODEL, 2 * D_FF), D_MODEL ** -0.5),
        "ffn_conv_w": nrm((DEPTH, FFN_CONV_W, D_FF), FFN_CONV_W ** -0.5),
        "ffn_conv_b": nrm((DEPTH, D_FF), 0.01),
        "ffn_w_down": nrm((DEPTH, D_FF, D_MODEL), D_FF ** -0.5),
    }

def reference(x_prompt, x_sample, cache_ckv, cache_krope, page_table, state_lru_h, state_lru_conv, state_ffn_conv,
              norm_mix, norm_ffn, attn_w_down, attn_g_q_lora, attn_w_uq, attn_g_kv_lora, attn_g_qn, attn_g_qr,
              attn_g_kn, attn_g_kr, attn_w_uk, attn_w_uv, attn_w_o, rec_w_in, rec_conv_w, rec_conv_b, rec_w_a,
              rec_b_a, rec_w_i, rec_b_i, rec_lambda, rec_w_out, ffn_w_up, ffn_conv_w, ffn_conv_b, ffn_w_down):
    bp, tp = x_prompt.shape[:2]
    bs, ts = x_sample.shape[:2]
    past = page_table.shape[1] * PAGE_SIZE
    pos_p = jnp.arange(tp)
    pos_s = past + jnp.arange(ts)
    xp, xs = x_prompt, x_sample
    ckv_p, kr_p, ckv_s, kr_s = [], [], [], []
    lh_p, lh_s, lc_p, lc_s = [], [], [], []
    fc_p, fc_s = [], []
    for i in range(DEPTH):
        j = i // N_MIXERS
        hp = rmsnorm(xp, norm_mix[i])
        hs = rmsnorm(xs, norm_mix[i])
        if i % N_MIXERS == 0:
            proj = (attn_w_down[j], attn_g_q_lora[j], attn_w_uq[j], attn_g_kv_lora[j], attn_g_qn[j], attn_g_qr[j], attn_g_kr[j])
            qn_p, qr_p, c_p, k_p = mla_project(hp, pos_p, *proj)
            qn_s, qr_s, c_s, k_s = mla_project(hs, pos_s, *proj)
            o_p = mla_prompt(qn_p, qr_p, c_p, k_p, attn_w_uk[j], attn_w_uv[j], attn_g_kn[j])
            o_s = mla_sample(qn_s, qr_s, c_s, k_s, page_table, cache_ckv, cache_krope, j,
                             attn_w_uk[j], attn_w_uv[j], attn_g_kn[j])
            xp = xp + o_p @ attn_w_o[j]
            xs = xs + o_s @ attn_w_o[j]
            ckv_p.append(c_p)
            kr_p.append(k_p)
            ckv_s.append(c_s)
            kr_s.append(k_s)
        else:
            rec = (rec_w_in[j], rec_conv_w[j], rec_conv_b[j], rec_w_a[j], rec_b_a[j], rec_w_i[j], rec_b_i[j],
                   rec_lambda[j], rec_w_out[j])
            h0_p = jnp.zeros((bp, LRU_WIDTH), xp.dtype)
            buf0_p = jnp.zeros((bp, REC_CONV_W - 1, LRU_WIDTH), xp.dtype)
            o_p, h_p, cv_p = recurrent_mixer(hp, h0_p, buf0_p, *rec)
            o_s, h_s, cv_s = recurrent_mixer(hs, state_lru_h[j], state_lru_conv[j], *rec)
            xp = xp + o_p
            xs = xs + o_s
            lh_p.append(h_p)
            lh_s.append(h_s)
            lc_p.append(cv_p)
            lc_s.append(cv_s)
        gp = rmsnorm(xp, norm_ffn[i])
        gs = rmsnorm(xs, norm_ffn[i])
        fbuf0_p = jnp.zeros((bp, FFN_CONV_W - 1, D_FF), xp.dtype)
        f_p, fb_p = conv_ffn(gp, fbuf0_p, ffn_w_up[i], ffn_conv_w[i], ffn_conv_b[i], ffn_w_down[i])
        f_s, fb_s = conv_ffn(gs, state_ffn_conv[i], ffn_w_up[i], ffn_conv_w[i], ffn_conv_b[i], ffn_w_down[i])
        xp = xp + f_p
        xs = xs + f_s
        fc_p.append(fb_p)
        fc_s.append(fb_s)
    return (xp, xs, jnp.stack(ckv_p), jnp.stack(kr_p), jnp.stack(ckv_s), jnp.stack(kr_s),
            jnp.stack(lh_p), jnp.stack(lh_s), jnp.stack(lc_p), jnp.stack(lc_s), jnp.stack(fc_p), jnp.stack(fc_s))


_drawn_inputs = setup_inputs


def setup_inputs(seed=0):
    import zlib

    import numpy as np

    out = dict(_drawn_inputs(seed))
    spreads = {}
    factors = {'attn_g_q_lora': 8.0,
     'attn_g_kv_lora': 2.899,
     'attn_g_qn': 8.0,
     'attn_g_qr': 23.903,
     'attn_g_kn': 8.0,
     'rec_b_a': 24.426,
     'rec_b_i': 8.0,
     'ffn_conv_b': 7.797}
    for name, (base, spread) in spreads.items():
        noise = np.random.default_rng([zlib.crc32(name.encode()), seed]).standard_normal(out[name].shape)
        drawn = base * np.exp(spread * noise) if base else spread * noise
        out[name] = __import__('jax').numpy.asarray(drawn.astype(out[name].dtype))
    for name, factor in factors.items():
        out[name] = (out[name] * factor).astype(out[name].dtype)
    return out
```

```python
from contextlib import ExitStack

import concourse.bass as bass
from concourse import mybir

F32 = mybir.dt.float32
F32R = mybir.dt.float32r
I32 = mybir.dt.int32
ALU = mybir.AluOpType
ACT = mybir.ActivationFunctionType
AX = mybir.AxisListType

P = 128
D = 1024
DC = D // P
TP, NB, TS = 512, 8, 8
TN = NB * TS
T = TP + TN
HT = T // 2
NH, DN, DR, DV = 16, 64, 32, 64
QL, KL = 512, 256
HQ = NH * TS
PAGES, PAGE = 16, 128
SEQ_BLOCKS = PAGES + 1
FF = 3 * D
FC = FF // P
THIRDS, TF = 3, FC // 3
RW, FW = 4, 3
EPS = 1e-6
SCALE = float((DN + DR) ** -0.5)
NEG = -1e30

C_ID, C_ONE, C_B64, C_B32, C_ROT, C_CM, C_NM, C_COS, C_SIN = 0, 128, 256, 384, 512, 640, 768, 832, 832 + T
C_ALL = C_SIN + T
R_CS, R_CW, R_CB, R_BA, R_BI, R_LAM, R_H, R_NM, R_NF = 0, 24, 28, 29, 30, 31, 32, 40, 42
R_ALL = 44
F_ST, F_CW, F_CB, F_ALL = 0, 16, 19, 20
G_Q, G_KV, G_QN, G_QR, G_KN, G_KR, G_QNS, G_QRS = 0, 4, 6, 7, 8, 9, 10, 11

DOWN0, UQ0, WO0 = 0, 7, 13
FFN0 = WO0 + 8
REC0 = FFN0 + THIRDS * 24
OUT0 = REC0 + 16
FFN1 = OUT0 + 8
TILES = FFN1 + THIRDS * 24
UQ_DMAS = 8

R0, R1, XN, AP_ = 0, 9216, 17280, 26496
ARENA = 33920
A_UK, A_CKV, A_OT, A_V, A_QC, A_P = 0, 5120, 8576, 13184, XN, AP_
UKC = 1280


def loaded(t):
    return sum(16 * (UQ_DMAS if UQ0 <= u < WO0 else 1) for u in range(t % 4, t + 1, 4))


def uk_col(h):
    return h * DN + (P if h * DN >= 768 else 0)


def build(nc, I, O):
    with ExitStack() as ctx:
        def sb(name, shape, dt=F32):
            return ctx.enter_context(nc.sbuf_tensor(name, shape, dt))

        def sem(name):
            return ctx.enter_context(nc.semaphore(name))

        xT = sb("xT", [P, DC, T])
        raw = sb("raw", [P, 4, 1024])
        whi = sb("whi", [P, 2, 1024], F32R)
        wlo = sb("wlo", [P, 2, 1024], F32R)
        cst = sb("cst", [P, C_ALL])
        arena_at = nc.sbuf_base
        arena = sb("arena", [P, ARENA])
        rpar = sb("rpar", [P, DC, R_ALL])
        smallg = sb("smallg", [P, 12])
        work = sb("work", [P, 5 * T])
        snew = sb("snew", [P, NB, HQ])
        cnat = sb("cnat", [TN, KL + 1])
        krw_rope = sb("krw_rope", [DR, T])
        pt = sb("pt", [1, NB * PAGES], I32)
        cols = sb("cols", [P, 32])
        ps = ctx.enter_context(nc.psum_tensor("ps", [P, 8, 512], F32))

        def area(off, *dims, dt=F32):
            n = 1
            for d in dims:
                n *= d
            if dt is F32:
                v = arena[:, off:off + n]
            else:
                v = nc.alloc_sbuf_tensor_at(f"split_{off}_{n}", [P, n], dt, offset=arena_at + 4 * off)[:]
            if len(dims) == 2:
                return v.rearrange("p (a b) -> p a b", a=dims[0])
            if len(dims) == 3:
                return v.rearrange("p (a b c) -> p a b c", a=dims[0], b=dims[1])
            if len(dims) == 4:
                return v.rearrange("p (a b c d) -> p a b c d", a=dims[0], b=dims[1], c=dims[2])
            return v

        def f32(v):
            return v.bitcast(F32)

        def pair(k, n=HT):
            return ps[:, 2 * k:2 * k + 2, 0:n]

        def two(v):
            return v.rearrange("p (a b) -> p a b", a=2)

        ident = cst[:, C_ID:C_ID + P]
        ones = cst[:, C_ONE:C_ONE + P]
        blk64 = cst[:, C_B64:C_B64 + P]
        blk32 = cst[:, C_B32:C_B32 + P]
        rotm = cst[:, C_ROT:C_ROT + P]
        cmask = cst[:, C_CM:C_CM + P]
        nmask = cst[0:TN, C_NM:C_NM + TN]
        cosT = cst[:, C_COS:C_COS + T]
        sinT = cst[:, C_SIN:C_SIN + T]
        sq = [work[:, i * T:(i + 1) * T] for i in range(2)]
        rs = [work[:, (2 + i) * T:(3 + i) * T] for i in range(3)]

        xin = area(R0, 5, D)
        xn_hi = area(XN, DC, T, dt=F32R)
        xn_lo = area(XN + DC * T, DC, T, dt=F32R)
        h_hi = area(R0, DC, T, dt=F32R)
        h_lo = area(R0 + DC * T, DC, T, dt=F32R)

        w_loaded = [sem(f"w_loaded{i}") for i in range(4)]
        w_hi, w_lo, w_used = sem("w_hi"), sem("w_lo"), sem("w_used")
        acc_free = [sem(f"acc_free{i}") for i in range(2)]

        block = ctx.enter_context(nc.Block())

        def load_tile(sp, t, src, it=0):
            if t >= 4:
                sp.wait_ge(w_lo, t - 3 + 4 * it)
            sp.dma_start(raw[:, t % 4, :].rearrange("p (k n) -> p k n", n=P), src).then_inc(w_loaded[t % 4], 16)

        def split_hi(act, t, it=0):
            act.wait_ge(w_loaded[t % 4], loaded(t) + 16 * it)
            if t >= 2:
                act.wait_ge(w_used, t - 1 + 4 * it)
            act.copy(whi[:, t % 2, :], raw[:, t % 4, :]).then_inc(w_hi, 1)

        def split_lo(pool, t, it=0):
            pool.wait_ge(w_hi, t + 1 + 4 * it)
            pool.tensor_tensor(wlo[:, t % 2, :], raw[:, t % 4, :], f32(whi[:, t % 2, :]),
                               ALU.subtract).then_inc(w_lo, 1)

        def product(pe, out, wh, wl, xh, xl, first, last):
            for o, a, b in zip(out, xh, xl):
                pe.matmul(o, wh, a, start=first, stop=False)
                pe.matmul(o, wh, b, start=False, stop=False)
            for o, a in zip(out, xh):
                mm = pe.matmul(o, wl, a, start=False, stop=last)
            return mm

        def halves(v):
            return [v[:, 0:HT], v[:, HT:T]]

        def acc(p):
            return [ps[:, 2 * p, 0:HT], ps[:, 2 * p + 1, 0:HT]]

        def tile_product(pe, t, a, xh, xl, it=0, at=0, kn=8, ready=None):
            pe.wait_ge(w_lo, t + 1 + 4 * it)
            if a >= 2:
                pe.wait_ge(acc_free[a % 2], a // 2 + 2 * it)
            wh = whi[:, t % 2, :].rearrange("p (k n) -> p k n", n=P)
            wl = wlo[:, t % 2, :].rearrange("p (k n) -> p k n", n=P)
            for k in range(kn):
                if ready:
                    ready(k)
                mm = product(pe, acc(a % 2), wh[:, at + k, :], wl[:, at + k, :],
                             halves(xh[:, k, :]), halves(xl[:, k, :]), k == 0, k == kn - 1)
            return mm

        def ones_product(pe, bank, m, src, first=True, last=True, n=P):
            for i in range(2):
                mm = pe.matmul(ps[0:n, bank + i, 0:HT], m, src[:, i * HT:(i + 1) * HT], start=first, stop=last)
            return mm

        class Chain:

            def __init__(self, eng, s, base=0):
                self.eng, self.s, self.n = eng, s, base

            def __call__(self, ins):
                ins.then_inc(self.s, 1)
                self.n = self.n + 1
                self.eng.wait_ge(self.s, self.n)

        n_sq = sem("n_sq")
        n_ss = sem("n_ss")
        n_ln = sem("n_ln")
        n_rs = sem("n_rs")
        n_f = sem("n_f")
        n_hi = sem("n_hi")
        n_lo = sem("n_lo")
        N_ROW = [R_NM, R_NF, R_NM + 1, R_NF + 1]

        def norm_square(act, i, c):
            if c >= 2:
                act.wait_ge(n_ss, DC * i + c - 1)
            act.activation(sq[c % 2], xT[:, c, :], ACT.Square).then_inc(n_sq, 1)

        def norm_sum(pe, i, c):
            pe.wait_ge(n_sq, DC * i + c + 1)
            ones_product(pe, 6, ones, sq[c % 2], c == 0, c == DC - 1).then_inc(n_ss, 1)

        def inverse_root(act, out, src, n, s_ln, s_out, k):
            act.activation(out, src, ACT.Ln, bias=EPS, scale=1.0 / n).then_inc(s_ln, 1)
            act.wait_ge(s_ln, k)
            act.activation(out, out, ACT.Exp, scale=-0.5).then_inc(s_out, 1)

        def norm_act(act, i):
            act.wait_ge(n_ss, DC * i + DC)
            inverse_root(act, two(rs[0]), pair(3), D, n_ln, n_rs, i + 1)
            for c in range(DC):
                act.wait_ge(n_f, DC * i + c + 1)
                act.copy(xn_hi[:, c, :], sq[c % 2]).then_inc(n_hi, 1)

        def norm_dve(dve, i):
            dve.wait_ge(n_rs, i + 1)

            def low(c):
                dve.wait_ge(n_hi, DC * i + c + 1)
                dve.tensor_tensor(xn_lo[:, c, :], sq[c % 2], f32(xn_hi[:, c, :]), ALU.subtract).then_inc(n_lo, 1)

            for c in range(DC):
                if c >= 2:
                    low(c - 2)
                    dve.wait_ge(n_lo, DC * i + c - 1)
                dve.scalar_tensor_tensor(out=sq[c % 2], in0=xT[:, c, :], scalar=rpar[:, c, N_ROW[i]:N_ROW[i] + 1],
                                         in1=rs[0], op0=ALU.mult, op1=ALU.mult).then_inc(n_f, 1)
            low(DC - 2)
            low(DC - 1)

        def norm_ready(pe, i):
            return lambda k: pe.wait_ge(n_lo, DC * i + k + 1)

        s_cst, s_nat, s_small, s_pt = sem("s_cst"), sem("s_nat"), sem("s_small"), sem("s_pt")
        s_x = [sem(f"s_x{i}") for i in range(5)]
        xt_ps, xt_ev, rp_ps, rp_ev, s_gs = sem("xt_ps"), sem("xt_ev"), sem("rp_ps"), sem("rp_ev"), sem("s_gs")
        rnat = area(A_P, D)

        def load_inputs(sp):
            sp.dma_start(cst[:], I["consts"]).then_inc(s_cst, 16)
            for i in range(4):
                sp.dma_start(xin[:, i, :], I["x_prompt"][0, i * P:(i + 1) * P, :]).then_inc(s_x[i], 16)
            sp.dma_start(xin[0:TN, 4, :], I["x_sample"].rearrange("b t d -> (b t) d")).then_inc(s_x[4], 16)
            for row, src in ((R_CS, I["state_lru_conv"][0].rearrange("b w d -> (b w) d")),
                             (R_CW, I["rec_conv_w"][0]), (R_CB, I["rec_conv_b"]),
                             (R_BA, I["rec_b_a"].rearrange("a n d -> a (n d)")),
                             (R_BI, I["rec_b_i"].rearrange("a n d -> a (n d)")),
                             (R_LAM, I["rec_lambda"]), (R_H, I["state_lru_h"][0]),
                             (R_NM, I["norm_mix"]), (R_NF, I["norm_ffn"])):
                sp.dma_start(rnat[row:row + src.shape[0], :], src).then_inc(s_nat, 16)

        NAT_DMAS = 9

        def load_gains(sp):
            with nc.allow_non_contiguous_dma(reason="a few hundred words"):
                def col(at, n, c, name, m=1):
                    sp.dma_start(smallg[at:at + n, c:c + m],
                                 I[name].rearrange("a (c p) -> p (a c)", p=n)).then_inc(s_small, 16)
                col(0, P, G_Q, "attn_g_q_lora", 4)
                col(0, P, G_KV, "attn_g_kv_lora", 2)
                for k in range(2):
                    col(64 * k, DN, G_QN, "attn_g_qn")
                    col(64 * k, DN, G_KN, "attn_g_kn")
                for k in range(4):
                    col(32 * k, DR, G_QR, "attn_g_qr")
                col(0, DR, G_KR, "attn_g_kr")
            sp.dma_start(pt[:], I["page_table"].rearrange("b n -> (b n)").rearrange("(a n) -> a n", a=1))\
              .then_inc(s_pt, 16)

        SMALL_DMAS = 11

        def transpose_inputs(pe):
            pe.wait_ge(s_cst, 16)
            for i in range(5):
                pe.wait_ge(s_x[i], 16)
            for c in range(DC):
                if c >= 2:
                    pe.wait_ge(xt_ev, c - 1)
                b = 2 * (c % 2)
                for i in range(5):
                    n = P if i < 4 else TN
                    mm = pe.transpose(ps[:, b + i // 4, (i % 4) * P:(i % 4) * P + n],
                                      xin[0:n, i, c * P:(c + 1) * P], ident[0:n, 0:n])
                mm.then_inc(xt_ps, 1)
            pe.wait_ge(s_nat, 16 * NAT_DMAS)
            for c in range(DC):
                mm = pe.transpose(ps[:, 4, c * R_ALL:(c + 1) * R_ALL], rnat[0:R_ALL, c * P:(c + 1) * P],
                                  ident[0:R_ALL, 0:R_ALL])
            mm.then_inc(rp_ps, 1)

        def keep_inputs(dve):
            for c in range(DC):
                dve.wait_ge(xt_ps, c + 1)
                b = 2 * (c % 2)
                dve.tensor_copy(xT[:, c, 0:TP], ps[:, b, :])
                dve.tensor_copy(xT[:, c, TP:T], ps[:, b + 1, 0:TN]).then_inc(xt_ev, 1)
            dve.wait_ge(rp_ps, 1)
            dve.tensor_copy(rpar[:].rearrange("p a b -> p (a b)"), ps[:, 4, 0:DC * R_ALL]).then_inc(rp_ev, 1)
            dve.wait_ge(s_small, 16 * SMALL_DMAS)
            dve.tensor_scalar(smallg[:, G_QNS:G_QRS + 1], smallg[:, G_QN:G_QR + 1], SCALE, None,
                              ALU.mult).then_inc(s_gs, 1)
            dve.memset(cnat[:, KL:KL + 1], 1.0)
            dve.wait_ge(rp_ev, 1)

        dq = area(A_P + 4608, 4, T)
        cq_hi = area(A_P, 4, T, dt=F32R)
        cq_lo = area(A_P + 2304, 4, T, dt=F32R)
        ckv = area(A_CKV, 2, T)
        ckv_hi = area(A_CKV + 1152, 2, T, dt=F32R)
        ckv_lo = area(A_CKV + 2304, 2, T, dt=F32R)
        krw = area(A_OT, 4, T)
        onat = area(A_OT + 2304, 5, KL + DR)
        d_sq, d_ss, d_ln, d_rs = sem("d_sq"), sem("d_ss"), sem("d_ln"), sem("d_rs")
        d_f, d_hi, d_lo, d_ch = sem("d_f"), sem("d_hi"), sem("d_lo"), sem("d_ch")
        kr_n, kr_rot, kr_ok = sem("kr_n"), sem("kr_rot"), sem("kr_ok")
        on_ps, on_ev, s_onat = sem("on_ps"), sem("on_ev"), sem("s_onat")
        SS_BANK = [6, 6, 6, 6, 4, 4, 6]

        def down_src(t):
            n0 = min(t * P, QL + KL + DR - P)
            return I["attn_w_down"][0].rearrange("(k p) n -> p k n", p=P)[:, :, n0:n0 + P]

        def down_dst(c):
            return dq[:, c, :] if c < 4 else ckv[:, c - 4, :] if c < 6 else krw[0:DR, 0, :]

        def down_sum(pe, c):
            pe.wait_ge(d_sq, c + 1)
            if c == 6:
                pe.wait_ge(d_ln, 1)
            n = P if c < 6 else DR
            ones_product(pe, SS_BANK[c], ones[0:n, 0:n], sq[c % 2][0:n, :], c in (0, 4, 6), c in (3, 5, 6), n)\
                .then_inc(d_ss, 1)

        def down_pe(pe):
            pe.wait_ge(rp_ev, 1)
            for t in range(7):
                if t < 2:
                    pe.wait_ge(xt_ev, DC)
                tile_product(pe, t, t, xn_hi, xn_lo, ready=norm_ready(pe, 0) if t == 0 else None).then_inc(w_used, 1)
                if t:
                    down_sum(pe, t - 1)
            down_sum(pe, 6)
            pe.wait_ge(kr_n, 1)
            pe.wait_ge(d_ln, 2)
            ones_product(pe, 4, rotm[0:DR, 0:DR], krw[0:DR, 1, :], n=DR).then_inc(kr_rot, 1)
            pe.wait_ge(d_f, 6)
            pe.wait_ge(kr_ok, 1)
            for i in range(5):
                n = P if i < 4 else TN
                if i >= 2:
                    pe.wait_ge(on_ev, i - 1)
                for c in range(2):
                    pe.transpose(ps[0:n, i % 2, c * P:(c + 1) * P], ckv[:, c, i * P:i * P + n], ident)
                pe.transpose(ps[0:n, i % 2, KL:KL + DR], krw_rope[:, i * P:i * P + n],
                             ident[0:DR, 0:DR]).then_inc(on_ps, 1)

        def down_act(act):
            for t in range(7):
                split_hi(act, t + 1)
                act.wait_ge(acc_free[t % 2], t // 2 + 1)
                if t >= 2:
                    act.wait_ge(d_ss, t - 1)
                n = P if t < 6 else DR
                act.activation(sq[t % 2][0:n, :], down_dst(t), ACT.Square).then_inc(d_sq, 1)
                if t == 5:
                    act.wait_ge(d_ss, 4)
                    inverse_root(act, two(rs[0]), pair(3), QL, d_ln, d_rs, 1)
            act.wait_ge(d_ss, 6)
            inverse_root(act, two(rs[1]), pair(2), KL, d_ln, d_rs, 2)
            act.wait_ge(d_ss, 7)
            inverse_root(act, two(rs[2])[0:DR], pair(3)[0:DR], DR, d_ln, d_rs, 3)
            for c in range(6):
                act.wait_ge(d_f, c + 1)
                act.copy(cq_hi[:, c, :] if c < 4 else ckv_hi[:, c - 4, :], down_dst(c)).then_inc(d_hi, 1)

        def down_dve(dve, ch):
            for t in range(7):
                dve.wait_ge(w_used, t + 1)
                if t < 6:
                    dve.tensor_copy(two(down_dst(t)), pair(t % 2)).then_inc(acc_free[t % 2], 1)
                else:
                    dve.tensor_copy(two(krw[0:DR, 0, :]), pair(0)[P - DR:P]).then_inc(acc_free[0], 1)
            dve.wait_ge(s_gs, 1)
            dve.wait_ge(acc_free[0], 4)
            dve.wait_ge(acc_free[1], 3)
            for c in range(6):
                if c == 0:
                    dve.wait_ge(d_rs, 1)
                    dve.wait_ge(d_sq, 7)
                if c == 4:
                    dve.wait_ge(d_rs, 2)
                g = smallg[:, (G_Q + c if c < 4 else G_KV + c - 4):(G_Q + c if c < 4 else G_KV + c - 4) + 1]
                dve.scalar_tensor_tensor(out=down_dst(c), in0=down_dst(c), scalar=g, in1=rs[0 if c < 4 else 1],
                                         op0=ALU.mult, op1=ALU.mult).then_inc(d_f, 1)
            for c in range(6):
                dve.wait_ge(d_hi, c + 1)
                hi, lo = (cq_hi[:, c, :], cq_lo[:, c, :]) if c < 4 else (ckv_hi[:, c - 4, :], ckv_lo[:, c - 4, :])
                dve.tensor_tensor(lo, down_dst(c), f32(hi), ALU.subtract).then_inc(d_lo, 1)
            dve.wait_ge(d_rs, 3)
            dve.scalar_tensor_tensor(out=krw[0:DR, 1, :], in0=krw[0:DR, 0, :], scalar=smallg[0:DR, G_KR:G_KR + 1],
                                     in1=rs[2][0:DR, :], op0=ALU.mult, op1=ALU.mult).then_inc(kr_n, 1)
            dve.wait_ge(kr_n, 1)
            ch(dve.tensor_tensor(krw[0:DR, 2, :], krw[0:DR, 1, :], cosT[0:DR, :], ALU.mult))
            dve.wait_ge(kr_rot, 1)
            ch(dve.tensor_tensor(two(krw[0:DR, 3, :]), pair(2)[0:DR], two(sinT[0:DR, :]), ALU.mult))
            dve.tensor_tensor(krw_rope[:, :], krw[0:DR, 2, :], krw[0:DR, 3, :], ALU.add).then_inc(kr_ok, 1)
            for i in range(5):
                n = P if i < 4 else TN
                dve.wait_ge(on_ps, i + 1)
                dve.tensor_copy(onat[0:n, i, :], ps[0:n, i % 2, 0:KL + DR]).then_inc(on_ev, 1)
            dve.wait_ge(on_ev, 5)
            dve.tensor_copy(cnat[:, 0:KL], onat[0:TN, 4, 0:KL]).then_inc(on_ev, 1)

        def down_store(sp):
            sp.wait_ge(on_ev, 5)
            sp.dma_start(O["ckv_prompt"][0, 0].rearrange("(i p) c -> p i c", p=P), onat[:, 0:4, 0:KL]).then_inc(s_onat, 16)
            sp.dma_start(O["krope_prompt"][0, 0].rearrange("(i p) c -> p i c", p=P), onat[:, 0:4, KL:KL + DR])\
              .then_inc(s_onat, 16)
            sp.dma_start(O["ckv_sample"][0].rearrange("b t c -> (b t) c"), onat[0:TN, 4, 0:KL]).then_inc(s_onat, 16)
            sp.dma_start(O["krope_sample"][0].rearrange("b t c -> (b t) c"), onat[0:TN, 4, KL:KL + DR])\
              .then_inc(s_onat, 16)

        qc = area(A_QC, NH, T)
        qraw = area(A_V, 2, T)
        qrn = area(A_V + 2 * T, 2, T)
        qt = area(A_V + 4 * T, 2, T)
        u_half, u_sq, u_ss = sem("u_half"), sem("u_sq"), sem("u_ss")
        u_ln, u_rs, u_n, u_rot, u_ch, u_q = (sem("u_ln"), sem("u_rs"), sem("u_n"), sem("u_rot"), sem("u_ch"),
                                             sem("u_q"))
        uk_raw = area(A_OT, 2, D)
        uk = area(A_UK, 2, 2, UKC, dt=F32R)
        s_uk = sem("s_uk")
        res_h, res_l = sem("res_h"), sem("res_l")

        def load_uq(sp, t):
            sp.wait_ge(w_lo, t - 3)
            w = I["attn_w_uq"][0].rearrange("(k p) (h e) -> p k h e", p=P, e=DN + DR)
            for j in range(2):
                c = 2 * (t - UQ0) + j
                for k in range(4):
                    dst = raw[:, t % 4, (4 * j + k) * P:(4 * j + k + 1) * P]
                    if c < 8:
                        src, e = w[:, k, 2 * c:2 * c + 2, 0:DN], DN
                    else:
                        src, e = w[:, k, 4 * (c - 8):4 * (c - 8) + 4, DN:DN + DR], DR
                    sp.dma_start(dst.rearrange("p (h e) -> p h e", e=e), src).then_inc(w_loaded[t % 4], 16)

        def uq_sum(pe, c):
            pe.wait_ge(u_sq, c + 1)
            if c >= 2:
                pe.wait_ge(u_ln, c - 1)
            if c >= 10:
                pe.wait_ge(u_q, c - 9)
            ones_product(pe, 4 + 2 * (c % 2), blk64 if c < 8 else blk32, sq[c % 2]).then_inc(u_ss, 1)

        def uq_rotate(pe, c):
            pe.wait_ge(u_n, c - 7)
            pe.wait_ge(u_ln, c + 1)
            ones_product(pe, 4 + 2 * (c % 2), rotm, qrn[:, c % 2, :]).then_inc(u_rot, 1)

        def uq_pe(pe):
            pe.wait_ge(d_ln, 3)
            pe.wait_ge(on_ev, 5)
            for c in range(12):
                t = UQ0 + c // 2
                mm = tile_product(pe, t, 7 + c, cq_hi, cq_lo, at=4 * (c % 2), kn=4,
                                  ready=(lambda k: pe.wait_ge(d_lo, k + 1)) if c == 0 else None)
                mm.then_inc(w_used if c % 2 else u_half, 1)
                if c >= 1:
                    uq_sum(pe, c - 1)
                if c >= 10:
                    uq_rotate(pe, c - 2)
            uq_sum(pe, 11)
            uq_rotate(pe, 10)
            uq_rotate(pe, 11)

        def uq_act(act):
            for c in range(12):
                if c % 2 == 0 and c < 10:
                    split_hi(act, UQ0 + c // 2 + 1)
                act.wait_ge(acc_free[(7 + c) % 2], (7 + c) // 2 + 1)
                if c >= 2:
                    act.wait_ge(u_ss, c - 1)
                act.activation(sq[c % 2], qraw[:, c % 2, :], ACT.Square).then_inc(u_sq, 1)
                act.wait_ge(u_ss, c + 1)
                if c >= 2:
                    act.wait_ge(*((u_n, c - 9) if c >= 10 else (u_ch, 2 * (c - 1))))
                inverse_root(act, two(rs[c % 2]), pair(2 + c % 2), DN if c < 8 else DR, u_ln, u_rs, c + 1)
            act.wait_ge(s_uk, 16)
            for k in range(2):
                act.copy(uk[:, 0, k, 0:768], uk_raw[:, k, 0:768])
                act.copy(uk[:, 0, k, 896:1152], uk_raw[:, k, 768:1024]).then_inc(res_h, 1)

        def uq_dve(dve):
            ch = Chain(dve, u_ch)

            def evacuate(c):
                if c % 2:
                    dve.wait_ge(w_used, UQ0 + c // 2 + 1)
                else:
                    dve.wait_ge(u_half, c // 2 + 1)
                if c >= 2:
                    dve.wait_ge(u_sq, c - 1)
                if c >= 10:
                    dve.wait_ge(u_n, c - 9)
                dve.tensor_copy(two(qraw[:, c % 2, :]), pair((7 + c) % 2)).then_inc(acc_free[(7 + c) % 2], 1)

            def finish(c):
                dve.wait_ge(u_rs, c + 1)
                dve.wait_ge(acc_free[(7 + c) % 2], (7 + c) // 2 + 1)
                if c < 8:
                    for k in range(2):
                        r = slice(DN * k, DN * k + DN)
                        ch(dve.scalar_tensor_tensor(out=qc[0:DN, 2 * c + k, :], in0=qraw[r, c % 2, :],
                                                    scalar=smallg[r, G_QNS:G_QNS + 1], in1=rs[c % 2][r, :],
                                                    op0=ALU.mult, op1=ALU.mult))
                    return
                if c >= 10:
                    dve.wait_ge(u_rot, c - 9)
                dve.scalar_tensor_tensor(out=qrn[:, c % 2, :], in0=qraw[:, c % 2, :],
                                         scalar=smallg[:, G_QRS:G_QRS + 1], in1=rs[c % 2],
                                         op0=ALU.mult, op1=ALU.mult).then_inc(u_n, 1)

            def rotate(c):
                dve.wait_ge(u_n, c - 7)
                if c >= 9:
                    dve.wait_ge(u_q, c - 8)
                ch(dve.tensor_tensor(qt[:, 0, :], qrn[:, c % 2, :], cosT, ALU.mult))
                dve.wait_ge(u_rot, c - 7)
                ch(dve.tensor_tensor(two(qt[:, 1, :]), pair(2 + c % 2), two(sinT), ALU.mult))
                for k in range(4):
                    r = slice(DR * k, DR * k + DR)
                    ins = dve.tensor_tensor(qc[DN:DN + DR, 4 * (c - 8) + k, :], qt[r, 0, :], qt[r, 1, :], ALU.add)
                ins.then_inc(u_q, 1)

            for c in range(12):
                evacuate(c)
                if c >= 1:
                    finish(c - 1)
                if c >= 10:
                    rotate(c - 2)
            finish(11)
            rotate(10)
            rotate(11)

        def uk_pool(pool):
            for k in range(2):
                pool.wait_ge(res_h, k + 1)
                pool.tensor_tensor(uk[:, 1, k, 0:768], uk_raw[:, k, 0:768], f32(uk[:, 0, k, 0:768]), ALU.subtract)
                pool.tensor_tensor(uk[:, 1, k, 896:1152], uk_raw[:, k, 768:1024], f32(uk[:, 0, k, 896:1152]),
                                   ALU.subtract).then_inc(res_l, 1)

        wukT = area(A_P, NH, KL)
        qs = area(A_V, NH, TN)
        qabs = [w[:].rearrange("p a n -> p (a n)").rearrange("p (k b q) -> p k b q", k=2, b=NB)
                for w in (whi, wlo)]
        wt_ps, wt_ev, qs_ok, qa_ps, qa_hi, qa_lo = (sem("wt_ps"), sem("wt_ev"), sem("qs_ok"), sem("qa_ps"),
                                                    sem("qa_hi"), sem("qa_lo"))
        uv_raw = area(A_P + 4608, 2, D)
        uv = area(A_P, 2, 2, D, dt=F32R)
        vals = area(A_V, 4, D)
        s_uv = sem("s_uv")

        def values_pe(pe):
            pe.wait_ge(s_uk, 16)
            pe.wait_ge(u_q, 4)
            pe.wait_ge(acc_free[0], 10)
            pe.wait_ge(acc_free[1], 9)
            for h in range(NH):
                b = (h // 2) % 4
                if h % 2 == 0 and h >= 8:
                    pe.wait_ge(wt_ev, h // 2 - 3)
                for k in range(2):
                    mm = pe.transpose(ps[0:DN, b, (h % 2) * KL + k * P:(h % 2) * KL + (k + 1) * P],
                                      uk_raw[:, k, h * DN:(h + 1) * DN], ident)
                if h % 2:
                    mm.then_inc(wt_ps, 1)
            pe.wait_ge(qs_ok, 1)
            pe.wait_ge(wt_ev, 8)
            for k in range(2):
                for h in range(NH):
                    mm = pe.matmul(ps[:, 4 + 2 * k + h // 8, (h % 8) * TN:(h % 8 + 1) * TN],
                                   wukT[0:DN, h, k * P:(k + 1) * P], qs[0:DN, h, :], start=True, stop=True)
                    if h % 8 == 7:
                        mm.then_inc(qa_ps, 1)
            pe.wait_ge(res_l, 4)
            pe.wait_ge(d_lo, 6)
            for i in range(8):
                blk, half = i // 2, i % 2
                if i >= 4:
                    pe.wait_ge(wt_ev, 8 + i - 3)
                tok = slice(blk * P, (blk + 1) * P)
                col = slice(half * 512, half * 512 + 512)
                for k in range(2):
                    pe.matmul(ps[:, i % 4, :], ckv_hi[:, k, tok], uv[:, 0, k, col], start=(k == 0), stop=False)
                    pe.matmul(ps[:, i % 4, :], ckv_hi[:, k, tok], uv[:, 1, k, col], start=False, stop=False)
                    mm = pe.matmul(ps[:, i % 4, :], ckv_lo[:, k, tok], uv[:, 0, k, col], start=False, stop=(k == 1))
                mm.then_inc(wt_ps, 1)

        def values_dve(dve):
            dve.wait_ge(u_q, 4)
            dve.tensor_copy(snew[DN:DN + DR, :, :].rearrange("p b (h t) -> p b h t", h=NH),
                            qc[DN:DN + DR, :, TP:T].rearrange("p h (b t) -> p b h t", b=NB))
            dve.tensor_scalar(qs[0:DN, :, :], qc[0:DN, :, TP:T], smallg[0:DN, G_KN:G_KN + 1], None,
                              ALU.mult).then_inc(qs_ok, 1)
            for j in range(8):
                dve.wait_ge(wt_ps, j + 1)
                dve.tensor_copy(wukT[0:DN, 2 * j:2 * j + 2, :].rearrange("p a b -> p (a b)"), ps[0:DN, j % 4, :])\
                   .then_inc(wt_ev, 1)
            for j in range(4):
                k, g = j // 2, j % 2
                dve.wait_ge(qa_hi, j + 1)
                for b in range(NB):
                    ins = dve.tensor_tensor(
                        qabs[1][:, k, b, g * 64:(g + 1) * 64].rearrange("p (h t) -> p h t", h=8),
                        ps[:, 4 + j, :].rearrange("p (h b t) -> p b h t", h=8, b=NB)[:, b],
                        f32(qabs[0][:, k, b, g * 64:(g + 1) * 64]).rearrange("p (h t) -> p h t", h=8), ALU.subtract)
                ins.then_inc(qa_lo, 1)
            for i in range(1, 8, 2):
                dve.wait_ge(wt_ps, 8 + i)
                if i == 1:
                    dve.wait_ge(qa_ps, 4)
                    dve.wait_ge(qs_ok, 1)
                dve.tensor_copy(vals[:, i // 2, 0:512], ps[:, i - 1 - 4 * ((i - 1) // 4), :])
                dve.wait_ge(wt_ps, 9 + i)
                dve.tensor_copy(vals[:, i // 2, 512:1024], ps[:, i - 4 * (i // 4), :]).then_inc(wt_ev, 2)

        def values_act(act):
            act.wait_ge(w_used, WO0)
            for j in range(4):
                k, g = j // 2, j % 2
                act.wait_ge(qa_ps, j + 1)
                for b in range(NB):
                    ins = act.copy(qabs[0][:, k, b, g * 64:(g + 1) * 64].rearrange("p (h t) -> p h t", h=8),
                                   ps[:, 4 + j, :].rearrange("p (h b t) -> p b h t", h=8, b=NB)[:, b])
                ins.then_inc(qa_hi, 1)
            act.wait_ge(s_uv, 16)
            for k in range(2):
                act.copy(uv[:, 0, k, :], uv_raw[:, k, :]).then_inc(res_h, 1)

        def uv_pool(pool):
            for k in range(2):
                pool.wait_ge(res_h, k + 3)
                pool.tensor_tensor(uv[:, 1, k, :], uv_raw[:, k, :], f32(uv[:, 0, k, :]), ALU.subtract).then_inc(res_l, 1)

        pT = area(A_P, 2, 4, TP)
        kcat = area(A_P + 4096, 4, T)
        pr = area(A_P + 4096 + 2304, 2, 512)
        oT = area(A_OT, DC, T)
        k_mm, k_ev, k_sq, k_ss, k_ln, k_rs, k_cat, k_rope = (sem("k_mm"), sem("k_ev"), sem("k_sq"), sem("k_ss"),
                                                             sem("k_ln"), sem("k_rs"), sem("k_cat"), sem("k_rope"))
        p_s, p_max, p_exp, p_inv, p_ok, p_t, p_tev, p_o, p_oev, p_n, p_nev = (
            sem("p_s"), sem("p_max"), sem("p_exp"), sem("p_inv"), sem("p_ok"), sem("p_t"), sem("p_tev"),
            sem("p_o"), sem("p_oev"), sem("p_n"), sem("p_nev"))
        kflat = rs[2]
        UNITS = 4 * NH

        def key_pair(pe, j):
            if j >= 1:
                pe.wait_ge(k_ln, j)
            c0 = uk_col(2 * j)
            out = [ps[:, 4, 0:HT], ps[:, 5, 0:HT]]
            for k in range(2):
                mm = product(pe, out, uk[:, 0, k, c0:c0 + P], uk[:, 1, k, c0:c0 + P],
                             halves(ckv_hi[:, k, :]), halves(ckv_lo[:, k, :]), k == 0, k == 1)
            mm.then_inc(k_mm, 1)

        def key_sum(pe, j):
            pe.wait_ge(k_sq, j + 1)
            ones_product(pe, 4, blk64, sq[0]).then_inc(k_ss, 1)

        def key_evacuate(dve, j):
            dve.wait_ge(k_mm, j + 1)
            dve.tensor_copy(two(kflat), pair(2)).then_inc(k_ev, 1)

        def key_square(act, j):
            act.wait_ge(k_ev, j + 1)
            act.activation(sq[0], kflat, ACT.Square).then_inc(k_sq, 1)

        def key_root(act, j):
            act.wait_ge(k_ss, j + 1)
            inverse_root(act, two(rs[0]), pair(2), DN, k_ln, k_rs, j + 1)

        def key_norm(dve, j):
            dve.wait_ge(k_rs, j + 1)
            if j >= 2:
                dve.wait_ge(p_n, 2 * (j - 1))
            for k in range(2):
                r = slice(DN * k, DN * k + DN)
                ins = dve.scalar_tensor_tensor(out=kcat[0:DN, (2 * j + k) % 4, :], in0=kflat[r, :],
                                               scalar=smallg[r, G_KN:G_KN + 1], in1=rs[0][r, :],
                                               op0=ALU.mult, op1=ALU.mult)
            ins.then_inc(k_cat, 1)

        def scores(pe, u):
            h, qb = divmod(u, 4)
            n = (qb + 1) * P
            if u >= 2:
                pe.wait_ge(p_exp, u - 1)
            if qb == 0:
                pe.wait_ge(k_cat, h // 2 + 1)
            pe.matmul(ps[:, u % 2, 0:n], qc[0:96, h, qb * P:(qb + 1) * P], kcat[0:96, h % 4, 0:n],
                      start=True, stop=False)
            pe.matmul(ps[:, u % 2, qb * P:n], ident, cmask, start=False, stop=True).then_inc(p_s, 1)

        def new_scores(pe, h):
            if h == 8:
                pe.wait_ge(p_nev, 1)
            pe.matmul(ps[0:TN, 7, (h % 8) * TN:(h % 8 + 1) * TN], kcat[0:96, h % 4, TP:T], qc[0:96, h, TP:T],
                      start=True, stop=True).then_inc(p_n, 1)

        def probs_turn(pe, u):
            qb = u % 4
            pe.wait_ge(p_ok, u + 1)
            if u >= 2:
                pe.wait_ge(p_tev, u - 1)
            for kb in range(qb + 1):
                mm = pe.transpose(ps[:, 2 + u % 2, kb * P:(kb + 1) * P], pr[:, u % 2, kb * P:(kb + 1) * P], ident)
            mm.then_inc(p_t, 1)

        def attend(pe, h):
            if h >= 2 and h % 2 == 0:
                pe.wait_ge(p_oev, h // 2)
            pe.wait_ge(p_tev, 4 * h + 4)
            r = slice(DV * (h % 2), DV * (h % 2) + DV)
            for kb in range(4):
                mm = pe.matmul(ps[r, 6, kb * P:TP], vals[:, kb, h * DV:(h + 1) * DV], pT[:, h % 2, kb, kb * P:TP],
                               start=(kb == 0), stop=(kb == 3))
            mm.then_inc(p_o, 1)

        LAG = 2

        def prompt_pe(pe):
            pe.wait_ge(res_l, 2)
            pe.wait_ge(k_rope, 1)
            pe.wait_ge(qa_lo, 4)
            pe.wait_ge(wt_ev, 16)
            key_pair(pe, 0)
            key_sum(pe, 0)
            for u in range(UNITS + LAG):
                if u < UNITS:
                    h, qb = divmod(u, 4)
                    scores(pe, u)
                    if qb == 3:
                        new_scores(pe, h)
                    if u % 8 == 1 and h // 2 < 7:
                        key_pair(pe, h // 2 + 1)
                    if u % 8 == 4 and h // 2 < 7:
                        key_sum(pe, h // 2 + 1)
                if u >= LAG:
                    probs_turn(pe, u - LAG)
                    if (u - LAG) % 4 == 3 and u - LAG >= 7:
                        attend(pe, (u - LAG) // 4 - 1)
            attend(pe, NH - 1)

        def prompt_act(act):
            key_square(act, 0)
            key_root(act, 0)
            for u in range(UNITS + LAG):
                if u < UNITS:
                    h, qb = divmod(u, 4)
                    n = (qb + 1) * P
                    act.wait_ge(p_max, u + 1)
                    if u >= 2:
                        act.wait_ge(p_t, u - 1)
                    act.activation(pr[:, u % 2, 0:n], ps[:, u % 2, 0:n], ACT.Exp, bias=cols[:, u % 4:u % 4 + 1],
                                   accum_out=cols[:, 4 + u % 4:5 + u % 4]).then_inc(p_exp, 1)
                    if u % 8 == 3 and h // 2 < 7:
                        key_square(act, h // 2 + 1)
                    if u % 8 == 5 and h // 2 < 7:
                        key_root(act, h // 2 + 1)
                if u >= LAG:
                    v = u - LAG
                    h, qb = divmod(v, 4)
                    act.wait_ge(p_t, v + 1)
                    if qb == 0 and h >= 2:
                        act.wait_ge(p_o, h - 1)
                    act.copy(pT[:, h % 2, 0:qb + 1, qb * P:(qb + 1) * P],
                             ps[:, 2 + v % 2, 0:(qb + 1) * P].rearrange("p (k q) -> p k q", q=P)).then_inc(p_tev, 1)

        def prompt_dve(dve):
            dve.wait_ge(res_l, 4)
            dve.wait_ge(wt_ps, 16)
            dve.wait_ge(s_onat, 64)
            for k in range(4):
                ins = dve.tensor_copy(kcat[DN:DN + DR, k, :], krw_rope[:, :])
            ins.then_inc(k_rope, 1)
            key_evacuate(dve, 0)
            key_norm(dve, 0)
            for u in range(UNITS + 1):
                if u < UNITS:
                    h, qb = divmod(u, 4)
                    n = (qb + 1) * P
                    dve.wait_ge(p_s, u + 1)
                    if u >= 4:
                        dve.wait_ge(p_exp, u - 3)
                    dve.tensor_reduce(cols[:, u % 4:u % 4 + 1], ps[:, u % 2, 0:n], AX.X, ALU.max, negate=True)\
                       .then_inc(p_max, 1)
                if u >= 1:
                    v = u - 1
                    m = (v % 4 + 1) * P
                    dve.wait_ge(p_exp, v + 1)
                    dve.reciprocal(cols[:, 8 + v % 4:9 + v % 4], cols[:, 4 + v % 4:5 + v % 4]).then_inc(p_inv, 1)
                    dve.wait_ge(p_inv, v + 1)
                    dve.tensor_scalar(pr[:, v % 2, 0:m], pr[:, v % 2, 0:m], cols[:, 8 + v % 4:9 + v % 4], None,
                                      ALU.mult).then_inc(p_ok, 1)
                if u < UNITS:
                    if u % 8 == 2 and h // 2 < 7:
                        key_evacuate(dve, h // 2 + 1)
                    if u % 8 == 6 and h // 2 < 7:
                        key_norm(dve, h // 2 + 1)
                    if u % 8 == 7 and u >= 15:
                        outputs(dve, u // 8 - 1)
                    if u in (32, UNITS - 1):
                        new_block(dve, 0 if u == 32 else 1)
            outputs(dve, 7)

        def outputs(dve, j):
            dve.wait_ge(p_o, 2 * j + 2)
            dve.tensor_copy(oT[:, j, 0:TP], ps[:, 6, :]).then_inc(p_oev, 1)

        def new_block(dve, g):
            dve.wait_ge(p_n, 8 * g + 8)
            for b in range(NB):
                ins = dve.tensor_tensor(snew[0:TN, b, g * 64:(g + 1) * 64].rearrange("p (h t) -> p h t", h=8),
                                        ps[0:TN, 7, :].rearrange("p (h b t) -> p b h t", h=8, b=NB)[:, b],
                                        nmask[:, b * TS:(b + 1) * TS].unsqueeze(1).to_broadcast([TN, 8, TS]), ALU.add)
            ins.then_inc(p_nev, 1)

        cpg = area(A_QC, 2 * PAGES, 260)
        s_all = [area(A_P + i * SEQ_BLOCKS * HQ, SEQ_BLOCKS, HQ) for i in range(2)]
        a_sb = [area(A_P + 2 * SEQ_BLOCKS * HQ + i * 512, 4, HQ) for i in range(2)]
        sqk = area(A_P + 2 * SEQ_BLOCKS * HQ + 1024, 2, 1024)
        ctxT = area(A_CKV, 2, NH, TN)
        ct_hi = area(A_CKV + 2048, 2, 2, P, dt=F32R)
        ct_lo = area(A_CKV + 2560, 2, 2, P, dt=F32R)
        krp = sb("krp", [P, 4, DR])
        krT = sb("krT", [P, 2, P])
        qr_s = sb("qr_s", [P, 2, HQ])
        ssq = sb("ssq", [P, 2, 4 * NH])
        cx = area(A_V, KL)
        mx = area(A_V + 256, P)
        dg = area(A_V + 384, P)
        pg_in = [sem(f"pg_in{i}") for i in range(4)]
        t_ps, t_hi, t_lo, kb_mm, kb_sq, a_ev, b_mm, sq_ok, g_red = (
            sem("t_ps"), sem("t_hi"), sem("t_lo"), sem("kb_mm"), sem("kb_sq"), sem("a_ev"), sem("b_mm"),
            sem("sq_ok"), sem("g_red"))
        g_ln, g_rs, g_s1, g_s = sem("g_ln"), sem("g_rs"), sem("g_s1"), sem("g_s")
        q_hi, q_lo, q_r, n_ok = sem("q_hi"), sem("q_lo"), sem("q_r"), sem("n_ok")
        x_max, x_mt, x_m, x_dg, x_mb, x_sub, x_exp, x_ctx, x_inv, x_cx, x_ct, x_cev = (
            sem("x_max"), sem("x_mt"), sem("x_m"), sem("x_dg"), sem("x_mb"), sem("x_sub"), sem("x_exp"),
            sem("x_ctx"), sem("x_inv"), sem("x_cx"), sem("x_ct"), sem("x_cev"))
        s_init = sem("s_init")

        def page_load(sp, b, par, i, free):
            page = sp.value_load(pt[0:1, bass.ds(b * PAGES + i, 1)], min_val=0, max_val=I["cache_ckv"].shape[1] - 1)
            src = I["cache_ckv"][0][bass.ds(page, 1), :, :].rearrange("a p c -> p (a c)")
            if free and i < 3:
                sp.wait_ge(x_ctx, b - 1)
            elif free or i >= 4 or par:
                sp.wait_ge(t_ps, b * PAGES + i - 3)
            sp.dma_start(cpg[:, par * PAGES + i, 0:KL], src).then_inc(pg_in[i % 4], 16)
            src = I["cache_krope"][0][bass.ds(page, 1), :, :].rearrange("a p c -> p (a c)")
            sp.dma_start(krp[:, i % 4, :], src).then_inc(pg_in[i % 4], 16)

        def turn(pe, b, par, i):
            pe.wait_ge(pg_in[i % 4], 32 * (b * 4 + i // 4 + 1))
            if i >= 2 or par or not isinstance(b, int):
                pe.wait_ge(t_lo, b * PAGES + i - 1)
            bank = 3 + i % 2
            for k in range(2):
                pe.transpose(ps[:, bank, k * P:(k + 1) * P], cpg[:, par * PAGES + i, k * P:(k + 1) * P], ident)
            pe.transpose(ps[0:DR, bank, 2 * P:3 * P], krp[:, i % 4, :], ident).then_inc(t_ps, 1)

        def page_products(pe, b, par, i):
            pe.wait_ge(t_lo, b * PAGES + i + 1)
            later = i >= 1 or par or not isinstance(b, int)
            if i == 0:
                pe.wait_ge(q_lo, b + 1)
            c0 = [0, 384, 768 if par else 896]
            for j in range(3):
                if later:
                    pe.wait_ge(kb_sq, 3 * (b * PAGES + i) - 2 + j)
                    if j == 2:
                        pe.wait_ge(a_ev, b * PAGES + i)
                col = slice(c0[j], c0[j] + 384)
                for k in range(2):
                    pe.matmul(ps[:, j, 0:384], ct_hi[:, i % 2, k, :], uk[:, 0, k, col], start=(k == 0), stop=False)
                    pe.matmul(ps[:, j, 0:384], ct_hi[:, i % 2, k, :], uk[:, 1, k, col], start=False, stop=False)
                    mm = pe.matmul(ps[:, j, 0:384], ct_lo[:, i % 2, k, :], uk[:, 0, k, col], start=False,
                                   stop=(k == 1))
                mm.then_inc(kb_mm, 1)
            g = i // 4
            if i % 4 == 0 and (g >= 2 or par or not isinstance(b, int)):
                pe.wait_ge(g_s, b * 4 + g - 1)
            pe.matmul(ps[:, 5 + g % 2, (i % 4) * HQ:(i % 4 + 1) * HQ], krT[DN:DN + DR, i % 2, :],
                      qr_s[DN:DN + DR, par, :], start=True, stop=True).then_inc(b_mm, 1)

        def tail_pe(pe, b, par, i):
            if i == 3:
                pe.wait_ge(x_max, b + 1)
                pe.wait_ge(x_cev, b + 1)
                pe.transpose(ps[:, 7, 0:P], mx, ident).then_inc(x_mt, 1)
            if i == 5:
                pe.wait_ge(x_dg, b + 1)
                pe.matmul(ps[:, 7, P:2 * P], ones, dg, start=True, stop=True).then_inc(x_mb, 1)
            if 8 <= i <= 13:
                if i == 8:
                    pe.wait_ge(x_exp, b + 1)
                for k in range(3 * (i - 8), min(3 * (i - 8) + 3, SEQ_BLOCKS)):
                    n = P if k < PAGES else TN
                    rhs = cpg[:, par * PAGES + k, 0:KL + 1] if k < PAGES else cnat[:, :]
                    mm = pe.matmul(ps[:, 7, 0:KL + 1], s_all[par][0:n, k, :], rhs, start=(k == 0),
                                   stop=(k == SEQ_BLOCKS - 1))
                if i == 13:
                    mm.then_inc(x_ctx, 1)
            if i == 14:
                pe.wait_ge(x_cx, b + 1)
                for k in range(2):
                    mm = pe.transpose(ps[:, 7, k * P:(k + 1) * P], cx[:, k * P:(k + 1) * P], ident)
                mm.then_inc(x_ct, 1)

        def seq_pe(pe, b, par, tail, last):
            for i in range(PAGES):
                if i < PAGES - 1:
                    turn(pe, b, par, i + 1)
                elif not last:
                    turn(pe, b + 1, 1 - par, 0)
                page_products(pe, b, par, i)
                if tail:
                    tail_pe(pe, b - 1, 1 - par, i)

        def hi_act(act, b, par, i):
            act.wait_ge(t_ps, b * PAGES + i + 1)
            if i >= 2 or par or not isinstance(b, int):
                act.wait_ge(kb_mm, 3 * (b * PAGES + i - 1))
            act.copy(ct_hi[:, i % 2, :, :].rearrange("p a b -> p (a b)"), ps[:, 3 + i % 2, 0:KL]).then_inc(t_hi, 1)

        def group_act(act, b, g):
            act.wait_ge(sq_ok, b * PAGES + 4 * g + 4)
            v = ssq[:, g % 2, :]
            act.activation(v, v, ACT.Ln, bias=EPS, scale=1.0 / DN).then_inc(g_ln, 1)
            act.wait_ge(g_ln, b * 4 + g + 1)
            act.activation(v, v, ACT.Exp, scale=-0.5).then_inc(g_rs, 1)

        def query_act(act, b, par, first):
            if not first:
                act.wait_ge(kb_mm, 3 * PAGES * (b - 1))
            c0 = 768 if par else 1152
            act.copy(uk[:, 0, :, c0:c0 + P], f32(qabs[0][:, :, bass.ds(b, 1), :]).rearrange("p k a q -> p k (a q)"))\
               .then_inc(q_hi, 1)

        def query_dve(dve, b, par, first):
            if not first:
                dve.wait_ge(kb_mm, 3 * PAGES * (b - 1))
                dve.wait_ge(b_mm, PAGES * (b - 1))
                dve.wait_ge(x_ctx, b - 1)
            c0 = 768 if par else 1152
            dve.tensor_copy(uk[:, 1, :, c0:c0 + P], f32(qabs[1][:, :, bass.ds(b, 1), :]).rearrange("p k a q -> p k (a q)"))
            dve.tensor_copy(qr_s[DN:DN + DR, par, :], snew[DN:DN + DR, bass.ds(b, 1), :].rearrange("p a q -> p (a q)"))
            dve.tensor_copy(s_all[par][0:TN, PAGES, :], snew[0:TN, bass.ds(b, 1), :].rearrange("p a q -> p (a q)"))\
               .then_inc(q_lo, 1)

        def seq_act(act, b, par, tail, last):
            for i in range(PAGES):
                if i == 8 and not last:
                    query_act(act, b + 1, 1 - par, isinstance(b, int) and b == 0)
                if i < PAGES - 1:
                    hi_act(act, b, par, i + 1)
                elif not last:
                    hi_act(act, b + 1, 1 - par, 0)
                for j in range(3):
                    act.wait_ge(kb_mm, 3 * (b * PAGES + i) + j + 1)
                    if j == 0 and (i >= 2 or par or not isinstance(b, int)):
                        act.wait_ge(sq_ok, b * PAGES + i - 1)
                    if j < 2:
                        dst, src = sqk[:, i % 2, j * 384:(j + 1) * 384], ps[:, j, 0:384]
                    else:
                        dst, src = sqk[:, i % 2, 768:1024], ps[:, 2, P * par:P * par + 256]
                    act.activation(dst, src, ACT.Square).then_inc(kb_sq, 1)
                if i % 4 == 0 and (i or par or not isinstance(b, int)):
                    group_act(act, b if i else b - 1, i // 4 - 1 if i else 3)
                if tail and i == 7:
                    act.wait_ge(x_sub, b)
                    act.activation(s_all[1 - par].rearrange("p a b -> p (a b)"),
                                   s_all[1 - par].rearrange("p a b -> p (a b)"), ACT.Exp).then_inc(x_exp, 1)

        def lo_dve(dve, b, par, i):
            dve.wait_ge(t_hi, b * PAGES + i + 1)
            if i >= 2 or par or not isinstance(b, int):
                dve.wait_ge(b_mm, b * PAGES + i - 1)
            dve.tensor_copy(krT[DN:DN + DR, i % 2, :], ps[0:DR, 3 + i % 2, 2 * P:3 * P])
            dve.tensor_tensor(ct_lo[:, i % 2, :, :].rearrange("p a b -> p (a b)"), ps[:, 3 + i % 2, 0:KL],
                              f32(ct_hi[:, i % 2, :, :]).rearrange("p a b -> p (a b)"), ALU.subtract).then_inc(t_lo, 1)

        def group_dve(dve, b, par, g):
            n = b * 4 + g
            dve.wait_ge(g_rs, n + 1)
            dve.wait_ge(a_ev, b * PAGES + 4 * g + 4)
            dst = s_all[par][:, 4 * g:4 * g + 4, :].rearrange("p a (h t) -> p (a h) t", t=TS)
            dve.tensor_tensor(dst, a_sb[g % 2].rearrange("p a (h t) -> p (a h) t", t=TS),
                              ssq[:, g % 2, :].unsqueeze(2).to_broadcast([P, 4 * NH, TS]), ALU.mult).then_inc(g_s1, 1)
            dve.wait_ge(g_s1, n + 1)
            dve.wait_ge(b_mm, b * PAGES + 4 * g + 4)
            flat = s_all[par][:, 4 * g:4 * g + 4, :].rearrange("p a q -> p (a q)")
            dve.tensor_tensor(flat, flat, ps[:, 5 + g % 2, :], ALU.add).then_inc(g_s, 1)

        def tail_dve(dve, b, par, i):
            if i == 2:
                dve.wait_ge(g_s, 4 * b + 4)
                dve.wait_ge(q_lo, b + 1)
                dve.tensor_reduce(mx, s_all[par].rearrange("p k q -> p q k"), AX.X, ALU.max).then_inc(x_max, 1)
            if i == 4:
                dve.wait_ge(x_mt, b + 1)
                dve.tensor_reduce(cols[:, 12:13], ps[:, 7, 0:P], AX.X, ALU.max).then_inc(x_m, 1)
                dve.wait_ge(x_m, b + 1)
                dve.tensor_scalar(dg, ident, cols[:, 12:13], None, ALU.mult).then_inc(x_dg, 1)
            if i == 6:
                dve.wait_ge(x_mb, b + 1)
                dve.tensor_tensor(s_all[par], s_all[par],
                                  ps[:, 7, P:2 * P].unsqueeze(1).to_broadcast([P, SEQ_BLOCKS, HQ]), ALU.subtract)\
                   .then_inc(x_sub, 1)
            if i == 14:
                dve.wait_ge(x_ctx, b + 1)
                dve.reciprocal(cols[:, 13:14], ps[:, 7, KL:KL + 1]).then_inc(x_inv, 1)
                dve.wait_ge(x_inv, b + 1)
                dve.tensor_scalar(cx, ps[:, 7, 0:KL], cols[:, 13:14], None, ALU.mult).then_inc(x_cx, 1)
            if i == 15:
                dve.wait_ge(x_ct, b + 1)
                for k in range(2):
                    ins = dve.tensor_copy(ctxT[:, k, :, bass.ds(b * TS, TS)],
                                          ps[:, 7, k * P:(k + 1) * P].rearrange("p (h t) -> p h t", t=TS))
                ins.then_inc(x_cev, 1)

        def seq_dve(dve, b, par, tail, last):
            for i in range(PAGES):
                if i < PAGES - 1:
                    lo_dve(dve, b, par, i + 1)
                elif not last:
                    lo_dve(dve, b + 1, 1 - par, 0)
                n = b * PAGES + i
                q0 = 0 if par else 256
                dve.wait_ge(kb_sq, 3 * n + 3)
                dve.tensor_copy(a_sb[(i // 4) % 2][:, i % 4, :], ps[:, 2, q0:q0 + HQ]).then_inc(a_ev, 1)
                dve.tensor_reduce(ssq[:, (i // 4) % 2, (i % 4) * NH:(i % 4 + 1) * NH],
                                  sqk[:, i % 2, :].rearrange("p (h e) -> p h e", e=DN), AX.X, ALU.add)\
                   .then_inc(sq_ok, 1)
                if i % 4 == 1 and (i > 1 or par or not isinstance(b, int)):
                    if i == 1:
                        group_dve(dve, b - 1, 1 - par, 3)
                    else:
                        group_dve(dve, b, par, i // 4 - 1)
                if tail:
                    tail_dve(dve, b - 1, 1 - par, i)
                if i == 14 and not last:
                    query_dve(dve, b + 1, 1 - par, isinstance(b, int) and b == 0)

        LAST = NB - 1

        def sample_pe(pe):
            pe.wait_ge(p_oev, 8)
            pe.wait_ge(p_nev, 2)
            pe.wait_ge(s_init, 1)
            turn(pe, 0, 0, 0)
            seq_pe(pe, 0, 0, False, False)
            with pe.Fori(0, 3) as r:
                seq_pe(pe, r * 2 + 1, 1, True, False)
                seq_pe(pe, r * 2 + 2, 0, True, False)
            seq_pe(pe, LAST, 1, True, True)
            for i in range(PAGES):
                tail_pe(pe, LAST, 1, i)
            pe.wait_ge(s_uv, 32)
            pe.wait_ge(x_cev, NB + 1)
            for h in range(NH):
                r = slice(DV * (h % 2), DV * (h % 2) + DV)
                for k in range(2):
                    mm = pe.matmul(ps[r, 0, (h // 2) * TN:(h // 2 + 1) * TN], uv2[:, k, h * DV:(h + 1) * DV],
                                   ctxT[:, k, h, :], start=(k == 0), stop=(k == 1))
            mm.then_inc(o_mm, 1)

        uv2 = area(A_UK, 2, D)
        o_hi = area(A_QC, DC, T, dt=F32R)
        o_lo = area(A_QC + DC * T, DC, T, dt=F32R)
        o_mm, o_ev = sem("o_mm"), sem("o_ev")

        def sample_act(act):
            act.wait_ge(qa_lo, 4)
            query_act(act, 0, 0, True)
            hi_act(act, 0, 0, 0)
            seq_act(act, 0, 0, False, False)
            with act.Fori(0, 3) as r:
                seq_act(act, r * 2 + 1, 1, True, False)
                seq_act(act, r * 2 + 2, 0, True, False)
            seq_act(act, LAST, 1, True, True)
            group_act(act, LAST, 3)
            act.wait_ge(x_sub, NB)
            act.activation(s_all[1].rearrange("p a b -> p (a b)"), s_all[1].rearrange("p a b -> p (a b)"),
                           ACT.Exp).then_inc(x_exp, 1)
            split_hi(act, WO0)
            act.wait_ge(x_cev, NB + 1)
            for c in range(DC):
                if c == 0:
                    act.wait_ge(o_ev, 1)
                act.copy(o_hi[:, c, :], oT[:, c, :]).then_inc(d_hi, 1)

        def sample_dve(dve):
            dve.wait_ge(p_tev, UNITS)
            dve.wait_ge(p_o, NH)
            dve.memset(s_all[0][TN:P, PAGES, :], NEG).then_inc(x_cev, 1)
            dve.memset(s_all[1][TN:P, PAGES, :], NEG)
            dve.memset(cpg[:, :, KL:KL + 1], 1.0).then_inc(s_init, 1)
            query_dve(dve, 0, 0, True)
            lo_dve(dve, 0, 0, 0)
            seq_dve(dve, 0, 0, False, False)
            with dve.Fori(0, 3) as r:
                seq_dve(dve, r * 2 + 1, 1, True, False)
                seq_dve(dve, r * 2 + 2, 0, True, False)
            seq_dve(dve, LAST, 1, True, True)
            group_dve(dve, LAST, 1, 3)
            for i in range(PAGES):
                tail_dve(dve, LAST, 1, i)
            dve.wait_ge(o_mm, 1)
            dve.tensor_copy(oT[:, :, TP:T], ps[:, 0, :].rearrange("p (c t) -> p c t", c=DC)).then_inc(o_ev, 1)
            for c in range(DC):
                dve.wait_ge(d_hi, c + 7)
                dve.tensor_tensor(o_lo[:, c, :], oT[:, c, :], f32(o_hi[:, c, :]), ALU.subtract).then_inc(d_lo, 1)

        def sample_sp(sp):
            sp.wait_ge(s_pt, 16)
            sp.wait_ge(s_init, 1)
            for b in range(2):
                for i in range(PAGES):
                    page_load(sp, b, b % 2, i, False)
            with sp.Fori(0, 3) as r:
                for par in range(2):
                    for i in range(PAGES):
                        page_load(sp, r * 2 + 2 + par, par, i, True)
            sp.wait_ge(kb_mm, 3 * PAGES * NB)
            sp.dma_start(uv2, I["attn_w_uv"][0].rearrange("(k p) h d -> p k (h d)", p=P)).then_inc(s_uv, 16)

        def proj_src(name):
            w = I[name][0].rearrange("(k p) n -> p k n", p=P)
            return lambda d: w[:, :, d * P:(d + 1) * P]

        def proj_pe(pe, t0, i, xh, xl, ready):
            for d in range(DC):
                tile_product(pe, t0 + d, t0 + d + 6, xh, xl, ready=ready if d == 0 else None).then_inc(w_used, 1)
                if d:
                    norm_sum(pe, i, d - 1)
            norm_sum(pe, i, DC - 1)

        def x_added(act, t):
            act.wait_ge(acc_free[t % 2], (t + 6) // 2 + 1)

        def proj_act(act, t0, i):
            for d in range(DC):
                split_hi(act, t0 + d + 1)
                x_added(act, t0 + d)
                norm_square(act, i, d)

        def add_x(dve, t, d, it=0):
            dve.wait_ge(w_used, t + 1 + 4 * it)
            v = xT[:, bass.ds(d, 1), :].rearrange("p a (b c) -> p (a b) c", b=2)
            dve.tensor_tensor(v, v, pair(t % 2), ALU.add).then_inc(acc_free[t % 2], 1)

        fnat = area(AP_, FF)
        frow = area(AP_, FF)
        FT = (FW - 1) * (1 + NB)
        ftail = snew[:].rearrange("p a b -> p (a b)")[:, 0:2 * FC * FT].rearrange("p (f t) -> p f t", f=FC)
        GB = TP + FW - 1
        gb = area(R1, 2, GB + NB * (FW - 1 + TS))
        CBN = GB + NB * (FW - 1 + TS) - (FW - 1)
        cb = area(R1 + 2 * 594, 2, CBN + FW - 1)
        hf = area(R1 + 4 * 594, 2, T)
        fpar = sb("fpar", [P, FC, F_ALL])
        SG = FW - 1 + TS
        S = {k: sem(f"f_{k}") for k in ("nat", "par", "parev", "conv", "silu", "h", "ch", "tail", "tailev", "store")}

        def gate_out(act, pr_, j, buf, pad, w):
            act.copy(buf[:, pad:pad + HT], ps[:, 2 * pr_, 0:HT])
            act.copy(buf[:, pad + HT:pad + TP], ps[:, 2 * pr_ + 1, 0:TP - HT])
            dst = buf[:, TP + pad:TP + pad + NB * w].rearrange("p (b t) -> p b t", t=w)[:, :, pad:pad + TS]
            return act.copy(dst, ps[:, 2 * pr_ + 1, TP - HT:HT].rearrange("p (b t) -> p b t", t=TS))

        def ffn_load(sp, l, t0):
            for row, src in ((F_ST, I["state_ffn_conv"][l].rearrange("b w d -> (b w) d")),
                             (F_CW, I["ffn_conv_w"][l]), (F_CB, I["ffn_conv_b"][l:l + 1, :])):
                sp.dma_start(fnat[row:row + src.shape[0], :], src).then_inc(S["nat"], 16)
            up = I["ffn_w_up"][l].rearrange("(k p) n -> p k n", p=P)
            dn = I["ffn_w_down"][l].rearrange("(s k p) n -> s p k n", p=P, k=TF)
            with sp.Fori(0, THIRDS) as s:
                with sp.Fori(0, 4) as r:
                    for j in range(4):
                        col = (s * TF + r * 2 + j // 2) * P + (j % 2) * FF
                        load_tile(sp, t0 + j, up[:, :, bass.ds(col, P)], s * 6 + r)
                with sp.Fori(0, 2) as r:
                    for j in range(4):
                        src = dn[bass.ds(s, 1), :, :, bass.ds(r * 512 + j * P, P)]
                        load_tile(sp, t0 + 16 + j, src.rearrange("a p k n -> p (a k) n"), s * 6 + r)

        def ffn_pe(pe, l, t0, i, nxt):
            pe.wait_ge(S["nat"], 48 * l + 48)
            for c in range(FC):
                mm = pe.transpose(ps[:, 4, c * F_ALL:(c + 1) * F_ALL], fnat[0:F_ALL, c * P:(c + 1) * P],
                                  ident[0:F_ALL, 0:F_ALL])
            mm.then_inc(S["par"], 1)
            pe.wait_ge(S["parev"], l + 1)
            def up(s, r, wait):
                for j in range(2):
                    t = t0 + 2 * j
                    it = s * 6 + r
                    tile_product(pe, t, t + 6, xn_hi, xn_lo, it,
                                 ready=norm_ready(pe, i) if wait and j == 0 else None).then_inc(w_used, 1)
                    tile_product(pe, t + 1, t + 7, xn_hi, xn_lo, it).then_inc(w_used, 1)

            def down(s, r, j):
                t = t0 + 16 + j
                first = isinstance(r, int) and r == 0 and j == 0
                tile_product(pe, t, t + 6, h_hi, h_lo, s * 6 + r,
                             ready=(lambda k: pe.wait_ge(S["h"], l * FC + s * TF + k + 1)) if first else None)\
                    .then_inc(w_used, 1)

            def third(s, first, last):
                if first:
                    up(s, 0, True)
                with pe.Fori(1 if first else 0, 4) as r:
                    up(s, r, False)
                if last:
                    for d in range(DC):
                        down(s, d // 4, d % 4)
                        if nxt is None and d in (1, 4):
                            tails_pe(pe, d == 4)
                        if d:
                            norm_sum(pe, nxt, d - 1) if nxt is not None else None
                    if nxt is not None:
                        norm_sum(pe, nxt, DC - 1)
                else:
                    pe.wait_ge(S["h"], l * FC + s * TF + TF)
                    with pe.Fori(0, 2) as r:
                        for j in range(4):
                            down(s, r, j)

            third(0, True, False)
            third(1, False, False)
            third(2, False, True)

        def ffn_act(act, l, t0, nxt):

            def up(s, r):
                for j in range(2):
                    t, it = t0 + 2 * j, s * 6 + r
                    f = l * FC + s * TF + r * 2 + j
                    split_hi(act, t + 1, it)
                    act.wait_ge(w_used, t + 1 + 4 * it)
                    act.wait_ge(S["conv"], f + 1)
                    gate_out(act, t % 2, j, gb[:, j, :], FW - 1, SG).then_inc(acc_free[t % 2], 1)
                    split_hi(act, t + 2, it)
                    act.wait_ge(S["conv"], f + 3)
                    act.activation(cb[:, j, 0:CBN], cb[:, j, 0:CBN], ACT.Silu).then_inc(S["silu"], 1)

            def down(s, r, j, sq_i=None):
                t, it = t0 + 16 + j, s * 6 + r
                if t + 1 + 4 * (it if isinstance(it, int) else 0) < TILES:
                    split_hi(act, t + 1, it)
                if sq_i is not None:
                    act.wait_ge(acc_free[t % 2], (t + 6) // 2 + 1 + 2 * it)
                    norm_square(act, sq_i, 4 * r + j)

            with act.Fori(0, THIRDS - 1) as s:
                with act.Fori(0, 4) as r:
                    up(s, r)
                with act.Fori(0, 2) as r:
                    for j in range(4):
                        down(s, r, j)
            with act.Fori(0, 4) as r:
                up(THIRDS - 1, r)
            for d in range(DC):
                down(THIRDS - 1, d // 4, d % 4, nxt)
                if nxt is None and d in (2, 5):
                    tails_act(act, d == 5)

        def ffn_pool(pool, t0, last):
            n = THIRDS * 6
            with pool.Fori(0, n - 1) as r:
                for j in range(4):
                    split_lo(pool, t0 + 1 + j, r)
            for j in range(3 if last else 4):
                split_lo(pool, t0 + 1 + j, n - 1)

        def ffn_dve(dve, l, t0):
            pad = dve.memset(gb[:, :, 0:FW - 1], 0.0)
            if l == 0:
                pad.then_inc(S["conv"], 2)
            dve.wait_ge(S["par"], l + 1)
            dve.tensor_copy(fpar[:].rearrange("p a b -> p (a b)"), ps[:, 4, 0:FC * F_ALL]).then_inc(S["parev"], 1)
            dve.wait_ge(S["parev"], l + 1)

            def up(s, r):
                for j in range(2):
                    t, it = t0 + 2 * j, s * 6 + r
                    f = s * TF + r * 2 + j
                    F = l * FC + f
                    ch = Chain(dve, S["ch"], F * 4)
                    par = fpar[:, bass.ds(f, 1), :].rearrange("p a b -> p (a b)")
                    ch(dve.tensor_copy(gb_pad(j), par[:, F_ST:F_ST + 16].rearrange("p (b w) -> p b w", b=NB)))
                    dve.wait_ge(acc_free[t % 2], (t + 6) // 2 + 1 + 2 * it)
                    last = ftail[:, bass.ds(f, 1), l * FT:(l + 1) * FT].rearrange("p a b -> p (a b)")
                    dve.tensor_copy(last[:, 0:FW - 1], gb[:, j, TP:GB])
                    dve.tensor_copy(last[:, FW - 1:FT].rearrange("p (w b) -> p b w", b=NB),
                                    gb[:, j, GB:GB + NB * SG].rearrange("p (b t) -> p b t", t=SG)[:, :, TS:SG])
                    ch(dve.tensor_scalar(cb[:, j, 0:CBN], gb[:, j, 0:CBN], par[:, F_CW:F_CW + 1], par[:, F_CB:F_CB + 1],
                                         ALU.mult, ALU.add))
                    ch(dve.scalar_tensor_tensor(out=cb[:, j, 0:CBN], in0=gb[:, j, 1:1 + CBN],
                                                scalar=par[:, F_CW + 1:F_CW + 2], in1=cb[:, j, 0:CBN],
                                                op0=ALU.mult, op1=ALU.add))
                    dve.scalar_tensor_tensor(out=cb[:, j, 0:CBN], in0=gb[:, j, 2:2 + CBN],
                                             scalar=par[:, F_CW + 2:F_CW + 3], in1=cb[:, j, 0:CBN],
                                             op0=ALU.mult, op1=ALU.add).then_inc(S["conv"], 1)
                    dve.wait_ge(S["silu"], F + 1)
                    dve.wait_ge(w_used, t + 2 + 4 * it)
                    q = (t + 1) % 2
                    dve.tensor_tensor(hf[:, j, 0:HT], cb[:, j, 0:HT], ps[:, 2 * q, 0:HT], ALU.mult)
                    dve.tensor_tensor(hf[:, j, HT:TP], cb[:, j, HT:TP], ps[:, 2 * q + 1, 0:TP - HT], ALU.mult)
                    dve.tensor_tensor(hf[:, j, TP:T].rearrange("p (b t) -> p b t", t=TS),
                                      cb_new(j), ps[:, 2 * q + 1, TP - HT:HT].rearrange("p (b t) -> p b t", t=TS),
                                      ALU.mult).then_inc(acc_free[q], 1)
                    dve.wait_ge(acc_free[q], (t + 7) // 2 + 1 + 2 * it)
                    hh = h_hi[:, bass.ds(r * 2 + j, 1), :].rearrange("p a b -> p (a b)")
                    hl = h_lo[:, bass.ds(r * 2 + j, 1), :].rearrange("p a b -> p (a b)")
                    ch(dve.tensor_copy(hh, hf[:, j, :]))
                    dve.tensor_tensor(hl, hf[:, j, :], f32(hh), ALU.subtract).then_inc(S["h"], 1)

            with dve.Fori(0, THIRDS) as s:
                with dve.Fori(0, 4) as r:
                    up(s, r)
                with dve.Fori(0, 2) as r:
                    for j in range(4):
                        add_x(dve, t0 + 16 + j, r * 4 + j, s * 6 + r)

        def gb_pad(j):
            return gb[:, j, TP + FW - 1:TP + FW - 1 + NB * SG].rearrange("p (b t) -> p b t", t=SG)[:, :, 0:FW - 1]

        def cb_new(j):
            return cb[:, j, GB:GB + NB * SG].rearrange("p (b t) -> p b t", t=SG)[:, :, 0:TS]

        def tails_pe(pe, second):
            if second:
                pe.wait_ge(S["tailev"], 4)
            else:
                pe.wait_ge(S["conv"], 2 + 2 * FC)
            for c in range(16, FC) if second else range(16):
                mm = pe.transpose(ps[0:2 * FT, 4 + c % 16 // 4, c % 4 * P:(c % 4 + 1) * P], ftail[:, c, :], ident)
                if c % 4 == 3:
                    mm.then_inc(S["tail"], 1)

        def tails_act(act, second):
            for c in range(4, FC // 4) if second else range(4):
                act.wait_ge(S["tail"], c + 1)
                act.copy(frow[0:2 * FT, c * 512:(c + 1) * 512], ps[0:2 * FT, 4 + c % 4, :]).then_inc(S["tailev"], 1)

        def ffn_store(sp):
            sp.wait_ge(S["tailev"], FC // 4)
            for l in range(2):
                r = l * FT
                sp.dma_start(O["ffn_conv_prompt"][l, 0], frow[r:r + FW - 1, :]).then_inc(S["store"], 16)
                for w in range(FW - 1):
                    q = r + FW - 1 + w * NB
                    sp.dma_start(O["ffn_conv_sample"][l, :, w, :], frow[q:q + NB, :]).then_inc(S["store"], 16)

        XP = RW - 1
        XW = TP + XP
        XS = XP + TS
        XB = XW + NB * XS
        XC = XB - XP
        xrb = area(R1, 2, XB)
        xcv = area(R1 + 2 * XB, 2, XB)
        o_ = R1 + (4 * XB + 7) // 8 * 8
        xch = area(o_, 2, T, dt=F32R)
        xcl = area(o_ + 2 * T, 2, T, dt=F32R)
        ri = area(o_ + 4 * T, T)
        gl = area(o_ + 5 * T, 2, T)
        ra, th, aa, mm_ = sq[0], sq[1], rs[1], rs[2]
        HL = (1 + NB) * (1 + XP)
        hl = area(A_P, DC, HL)
        gw = area(A_P + 1024, 2, 2, NB, P, dt=F32R)
        gw_raw = area(A_P + 5120, 2, D)
        hn = area(A_P + 5120, D)
        yh = area(A_P + 6144, T)
        spc = sb("spc", [P, 8, DC])
        c_abs, c_exp, c_ok = sem("c_abs"), sem("c_exp"), sem("c_ok")
        s_gw = sem("s_gw")
        r_conv, r_hi, r_lo, r_ga, r_gi, r_ta, r_ti, r_a, r_m, r_y, r_yh, r_yl = (
            sem("r_conv"), sem("r_hi"), sem("r_lo"), sem("r_ga"), sem("r_gi"), sem("r_ta"), sem("r_ti"),
            sem("r_a"), sem("r_m"), sem("r_y"), sem("r_yh"),
            sem("r_yl"))

        def lam(row):
            return rpar[:, :, row:row + 1].rearrange("p c a -> p (c a)")

        def decay_act(act):
            act.wait_ge(rp_ev, 1)
            act.activation(spc[:, 0, :], lam(R_LAM), ACT.Abs).then_inc(c_abs, 1)
            act.wait_ge(c_abs, 1)
            act.activation(spc[:, 1, :], spc[:, 0, :], ACT.Exp, scale=-1.0).then_inc(c_exp, 1)

        def decay_dve(dve, ch):
            e, z, z2, q = spc[:, 1, :], spc[:, 2, :], spc[:, 3, :], spc[:, 4, :]
            dve.wait_ge(c_exp, 1)
            ch(dve.tensor_scalar(z2, e, 2.0, None, ALU.add))
            ch(dve.reciprocal(q, z2))
            ch(dve.tensor_tensor(z, e, q, ALU.mult))
            ch(dve.tensor_tensor(z2, z, z, ALU.mult))
            ch(dve.tensor_scalar(q, z2, 1.0 / 19, None, ALU.mult))
            for k in range(17, 1, -2):
                ch(dve.scalar_tensor_tensor(out=q, in0=q, scalar=1.0 / k, in1=z2, op0=ALU.add, op1=ALU.mult))
            ch(dve.tensor_scalar(q, q, 1.0, 2.0, ALU.add, ALU.mult))
            ch(dve.tensor_tensor(q, q, z, ALU.mult))
            ch(dve.tensor_scalar(z, lam(R_LAM), -1.0, 0.0, ALU.mult, ALU.max))
            ch(dve.tensor_tensor(z, z, q, ALU.add))
            ch(dve.tensor_scalar(spc[:, 5, :], z, -4.0, None, ALU.mult))
            ch(dve.tensor_scalar(spc[:, 6, :], lam(R_BA), 0.5, None, ALU.mult))
            dve.tensor_scalar(spc[:, 7, :], lam(R_BI), 0.5, None, ALU.mult).then_inc(c_ok, 1)

        def xr_t(n):
            return REC0 + 2 * n

        def prompt_new(v, off):
            return v[:, 0:TP], v[:, XW:XB].rearrange("p (b t) -> p b t", t=XS)[:, :, off:off + TS]

        def rec_load(sp):
            w = I["rec_w_in"][0].rearrange("(k p) n -> p k n", p=P)
            for n in range(DC):
                for g in range(2):
                    load_tile(sp, xr_t(n) + g, w[:, :, g * D + n * P:g * D + (n + 1) * P])
                if n == 1:
                    for g, name in enumerate(("rec_w_a", "rec_w_i")):
                        sp.dma_start(gw_raw[:, g, :].rearrange("p (n d) -> p n d", n=NB),
                                     I[name][0].rearrange("n c d -> c n d")).then_inc(s_gw, 16)

        def rec_gates(pe, n):
            pe.wait_ge(r_lo, n + 1)
            if n == 0:
                pe.wait_ge(res_l, 6)
            for g, (bank, free) in enumerate(((4, r_ta), (6, r_ti))):
                if n >= 1:
                    pe.wait_ge(free, n)
                out = [ps[:, bank, 0:HT], ps[:, bank + 1, 0:HT]]
                product(pe, out, gw[:, g, 0, n, :], gw[:, g, 1, n, :], halves(xch[:, n % 2, :]),
                        halves(xcl[:, n % 2, :]), True, True).then_inc((r_ga, r_gi)[g], 1)

        def rec_pe(pe):
            for n in range(DC):
                t = xr_t(n)
                tile_product(pe, t, t + 6, xn_hi, xn_lo, ready=norm_ready(pe, 2) if n == 0 else None)\
                    .then_inc(w_used, 1)
                if n:
                    rec_gates(pe, n - 1)
                tile_product(pe, t + 1, t + 7, xn_hi, xn_lo).then_inc(w_used, 1)
            rec_gates(pe, DC - 1)

        def rec_finish_act(act, n):
            act.wait_ge(r_ga, n + 1)
            if n:
                act.wait_ge(r_y, n)
            act.activation(two(ra), pair(2), ACT.Tanh, bias=spc[:, 6, n:n + 1], scale=0.5).then_inc(r_ta, 1)
            act.wait_ge(r_gi, n + 1)
            act.activation(two(ri), pair(3), ACT.Tanh, bias=spc[:, 7, n:n + 1], scale=0.5).then_inc(r_ti, 1)
            act.wait_ge(r_ta, n + 1)
            act.activation(aa, ra, ACT.Exp, bias=spc[:, 5, n:n + 1], scale=spc[:, 5, n:n + 1]).then_inc(r_a, 1)
            act.activation(th, ra, ACT.Tanh, bias=spc[:, 5, n:n + 1], scale=spc[:, 5, n:n + 1])
            act.wait_ge(r_a, 3 * n + 1)
            act.activation(mm_, aa, ACT.Square).then_inc(r_a, 1)
            act.wait_ge(r_m, n + 1)
            act.activation(mm_, mm_, ACT.Sqrt, scale=-1.0).then_inc(r_a, 1)

        def rec_act(act):
            act.wait_ge(s_gw, 32)
            for g in range(2):
                act.copy(gw[:, g, 0, :, :].rearrange("p a b -> p (a b)"), gw_raw[:, g, :]).then_inc(res_h, 1)
            for n in range(DC):
                t = xr_t(n)
                split_hi(act, t + 1)
                act.wait_ge(w_used, t + 1)
                if n >= 2:
                    act.wait_ge(r_conv, n - 1)
                gate_out(act, t % 2, 0, xrb[:, n % 2, :], XP, XS).then_inc(acc_free[t % 2], 1)
                act.wait_ge(r_conv, n + 1)
                src, dst = prompt_new(xcv[:, n % 2, :], 0), xch[:, n % 2, :]
                act.copy(dst[:, 0:TP], src[0])
                act.copy(dst[:, TP:T].rearrange("p (b t) -> p b t", t=TS), src[1]).then_inc(r_hi, 1)
                split_hi(act, t + 2)
                if n:
                    rec_finish_act(act, n - 1)
                act.wait_ge(w_used, t + 2)
                act.activation(two(gl[:, n % 2, :]), pair((t + 1) % 2), ACT.Gelu_apprx_tanh)\
                   .then_inc(acc_free[(t + 1) % 2], 1)
                if n:
                    act.wait_ge(r_y, n)
                    act.copy(h_hi[:, n - 1, :], yh).then_inc(r_yh, 1)
            rec_finish_act(act, DC - 1)
            act.wait_ge(r_y, DC)
            act.copy(h_hi[:, DC - 1, :], yh).then_inc(r_yh, 1)

        def rec_finish_dve(dve, n, ch):
            t = xr_t(n)
            dve.wait_ge(r_ti, n + 1)
            xp_, xs_ = prompt_new(xcv[:, n % 2, :], 0)
            new = lambda v: v[:, TP:T].rearrange("p (b t) -> p b t", t=TS)
            dve.scalar_tensor_tensor(out=ri[:, 0:TP], in0=ri[:, 0:TP], scalar=1.0, in1=xp_, op0=ALU.add, op1=ALU.mult)
            ch(dve.scalar_tensor_tensor(out=new(ri), in0=new(ri), scalar=1.0, in1=xs_, op0=ALU.add, op1=ALU.mult))
            dve.wait_ge(r_a, 3 * n + 2)
            dve.scalar_tensor_tensor(out=mm_, in0=mm_, scalar=1.0, in1=th, op0=ALU.add, op1=ALU.mult).then_inc(r_m, 1)
            dve.wait_ge(r_a, 3 * n + 3)
            ch(dve.scalar_tensor_tensor(out=ri, in0=ri, scalar=0.5, in1=mm_, op0=ALU.mult, op1=ALU.mult))
            a0, b0 = new(aa)[:, :, 0:1], new(ri)[:, :, 0:1]
            h0 = rpar[:, n, R_H:R_H + NB].unsqueeze(2)
            ch(dve.tensor_tensor(cols[:, 16:24].unsqueeze(2), a0, h0, ALU.mult))
            ch(dve.tensor_tensor(b0, b0, cols[:, 16:24].unsqueeze(2), ALU.add))
            ch(dve.memset(a0, 0.0))
            ch(dve.tensor_tensor_scan(mm_, aa, ri, 0.0, ALU.mult, ALU.add))
            dve.tensor_copy(hl[:, n, 0:1], mm_[:, TP - 1:TP])
            dve.tensor_copy(hl[:, n, 1:1 + NB].unsqueeze(2), new(mm_)[:, :, TS - 1:TS])
            dve.wait_ge(acc_free[(t + 1) % 2], (t + 7) // 2 + 1)
            if n:
                dve.wait_ge(r_yh, n)
            ch(dve.tensor_tensor(yh, mm_, gl[:, n % 2, :], ALU.mult))
            dve.memset(cols[:, 15:16], 0.0).then_inc(r_y, 1)
            dve.wait_ge(r_yh, n + 1)
            dve.tensor_tensor(h_lo[:, n, :], yh, f32(h_hi[:, n, :]), ALU.subtract).then_inc(r_yl, 1)

        def rec_dve(dve, ch):
            dve.memset(xrb[:, :, 0:XP], 0.0)
            for n in range(DC):
                t = xr_t(n)
                buf, out = xrb[:, n % 2, :], xcv[:, n % 2, 0:XC]
                ch(dve.tensor_copy(buf[:, XW:XB].rearrange("p (b t) -> p b t", t=XS)[:, :, 0:XP],
                                   rpar[:, n, R_CS:R_CS + NB * XP].rearrange("p (b w) -> p b w", b=NB)))
                dve.wait_ge(acc_free[t % 2], (t + 6) // 2 + 1)
                dve.tensor_copy(hl[:, n, 1 + NB:1 + NB + XP], buf[:, TP:XW])
                dve.tensor_copy(hl[:, n, 1 + NB + XP:HL].rearrange("p (w b) -> p b w", b=NB),
                                buf[:, XW:XB].rearrange("p (b t) -> p b t", t=XS)[:, :, TS:XS])
                ch(dve.tensor_scalar(out, buf[:, 0:XC], rpar[:, n, R_CW:R_CW + 1], rpar[:, n, R_CB:R_CB + 1],
                                     ALU.mult, ALU.add))
                for k in range(1, RW):
                    ins = dve.scalar_tensor_tensor(out=out, in0=buf[:, k:k + XC],
                                                   scalar=rpar[:, n, R_CW + k:R_CW + k + 1], in1=out,
                                                   op0=ALU.mult, op1=ALU.add)
                    if k < RW - 1:
                        ch(ins)
                ins.then_inc(r_conv, 1)
                dve.wait_ge(r_hi, n + 1)
                src, hi, lo = prompt_new(xcv[:, n % 2, :], 0), f32(xch[:, n % 2, :]), xcl[:, n % 2, :]
                dve.tensor_tensor(lo[:, 0:TP], src[0], hi[:, 0:TP], ALU.subtract)
                new = lambda v: v[:, TP:T].rearrange("p (b t) -> p b t", t=TS)
                dve.tensor_tensor(new(lo), src[1], new(hi), ALU.subtract).then_inc(r_lo, 1)
                if n:
                    rec_finish_dve(dve, n - 1, ch)
            rec_finish_dve(dve, DC - 1, ch)

        def gw_pool(pool):
            for g in range(2):
                pool.wait_ge(res_h, g + 5)
                pool.tensor_tensor(gw[:, g, 1, :, :].rearrange("p a b -> p (a b)"), gw_raw[:, g, :],
                                   f32(gw[:, g, 0, :, :]).rearrange("p a b -> p (a b)"), ALU.subtract)\
                    .then_inc(res_l, 1)

        def states_pe(pe):
            pe.wait_ge(r_yl, DC)
            for c in range(DC):
                mm = pe.transpose(ps[0:HL, 4 + c // 4, (c % 4) * P:(c % 4 + 1) * P], hl[:, c, :], ident)
            mm.then_inc(rp_ps, 1)

        def states_dve(dve):
            dve.wait_ge(rp_ps, 2)
            dve.tensor_copy(hn[0:HL, :].rearrange("p (a b) -> p a b", a=2), ps[0:HL, 4:6, :]).then_inc(rp_ev, 1)

        def rec_store(sp):
            sp.wait_ge(rp_ev, 2)
            sp.dma_start(O["lru_h_prompt"][0], hn[0:1, :]).then_inc(s_onat, 16)
            sp.dma_start(O["lru_h_sample"][0], hn[1:1 + NB, :]).then_inc(s_onat, 16)
            sp.dma_start(O["lru_conv_prompt"][0, 0], hn[1 + NB:1 + NB + XP, :]).then_inc(s_onat, 16)
            for w in range(XP):
                row = 1 + NB + XP + w * NB
                sp.dma_start(O["lru_conv_sample"][0, :, w, :], hn[row:row + NB, :]).then_inc(s_onat, 16)

        yn = area(R1, 2, D)
        s_y = [sem("s_y0"), sem("s_y1")]

        def out_pe(pe):
            last = TILES + 5
            pe.wait_ge(acc_free[last % 2], last // 2 + 1)
            pe.wait_ge(acc_free[1 - last % 2], (last - 1) // 2 + 1)
            for i in range(5):
                n = P if i < 4 else TN
                b = 2 * (i % 2)
                if i >= 2:
                    pe.wait_ge(xt_ev, DC + i - 1)
                for c in range(DC):
                    mm = pe.transpose(ps[0:n, b + c // 4, (c % 4) * P:(c % 4 + 1) * P], xT[:, c, i * P:i * P + n], ident)
                mm.then_inc(xt_ps, 1)

        def out_dve(dve):
            for i in range(5):
                n = P if i < 4 else TN
                b = 2 * (i % 2)
                dve.wait_ge(xt_ps, DC + i + 1)
                if i >= 2:
                    dve.wait_ge(s_y[i % 2], 16 * (i // 2))
                dve.tensor_copy(yn[0:n, i % 2, :].rearrange("p (a b) -> p a b", a=2), ps[0:n, b:b + 2, :])\
                   .then_inc(xt_ev, 1)

        def out_store(sp):
            for i in range(5):
                n = P if i < 4 else TN
                sp.wait_ge(xt_ev, DC + i + 1)
                dst = O["y_prompt"][0, i * P:(i + 1) * P, :] if i < 4 else O["y_sample"].rearrange("b t d -> (b t) d")
                sp.dma_start(dst, yn[0:n, i % 2, :]).then_inc(s_y[i % 2], 16)

        @block.sync
        def _(sp):
            load_inputs(sp)
            for t in range(4):
                load_tile(sp, t, down_src(t))
            load_gains(sp)
            for t in range(4, UQ0):
                load_tile(sp, t, down_src(t))
            for t in range(UQ0, UQ0 + 3):
                load_uq(sp, t)
            sp.wait_ge(kr_ok, 1)
            sp.dma_start(uk_raw, I["attn_w_uk"][0].rearrange("(k p) h d -> p k (h d)", p=P)).then_inc(s_uk, 16)
            sp.wait_ge(d_lo, 6)
            sp.dma_start(uv_raw, I["attn_w_uv"][0].rearrange("(k p) h d -> p k (h d)", p=P)).then_inc(s_uv, 16)
            for t in range(UQ0 + 3, WO0):
                load_uq(sp, t)
            down_store(sp)
            wo = proj_src("attn_w_o")
            for d in range(4):
                load_tile(sp, WO0 + d, wo(d))
            sample_sp(sp)
            for d in range(4, DC):
                load_tile(sp, WO0 + d, wo(d))
            sp.wait_ge(x_ctx, NB)
            ffn_load(sp, 0, FFN0)
            rec_load(sp)
            out = proj_src("rec_w_out")
            for d in range(DC):
                load_tile(sp, OUT0 + d, out(d))
                if d == 3:
                    rec_store(sp)
            sp.wait_ge(s_onat, 160)
            ffn_load(sp, 1, FFN1)
            ffn_store(sp)
            out_store(sp)
            sp.wait_ge(S["store"], 96)
            sp.wait_ge(s_y[0], 48)
            sp.wait_ge(s_y[1], 32)

        @block.gpsimd
        def _(pool):
            for t in range(WO0):
                split_lo(pool, t)
            uk_pool(pool)
            uv_pool(pool)
            for t in range(WO0, FFN0 + 1):
                split_lo(pool, t)
            ffn_pool(pool, FFN0, False)
            gw_pool(pool)
            for t in range(REC0 + 1, FFN1 + 1):
                split_lo(pool, t)
            ffn_pool(pool, FFN1, True)

        @block.scalar
        def _(act):
            act.preload_act_table_set("natural_log_exp_and_others")
            split_hi(act, 0)
            for c in range(DC):
                if c == 0:
                    act.wait_ge(xt_ev, DC)
                norm_square(act, 0, c)
            norm_act(act, 0)
            decay_act(act)
            down_act(act)
            uq_act(act)
            values_act(act)
            prompt_act(act)
            sample_act(act)
            proj_act(act, WO0, 1)
            norm_act(act, 1)
            ffn_act(act, 0, FFN0, 2)
            norm_act(act, 2)
            rec_act(act)
            proj_act(act, OUT0, 3)
            norm_act(act, 3)
            ffn_act(act, 1, FFN1, None)

        @block.vector
        def _(dve):
            ch = Chain(dve, d_ch)
            keep_inputs(dve)
            norm_dve(dve, 0)
            down_dve(dve, ch)
            uq_dve(dve)
            values_dve(dve)
            prompt_dve(dve)
            sample_dve(dve)
            for d in range(DC):
                add_x(dve, WO0 + d, d)
            norm_dve(dve, 1)
            ffn_dve(dve, 0, FFN0)
            decay_dve(dve, ch)
            norm_dve(dve, 2)
            rec_dve(dve, ch)
            states_dve(dve)
            for d in range(DC):
                add_x(dve, OUT0 + d, d)
            norm_dve(dve, 3)
            ffn_dve(dve, 1, FFN1)
            out_dve(dve)

        @block.tensor
        def _(pe):
            transpose_inputs(pe)
            for c in range(DC):
                norm_sum(pe, 0, c)
            down_pe(pe)
            uq_pe(pe)
            values_pe(pe)
            prompt_pe(pe)
            sample_pe(pe)
            proj_pe(pe, WO0, 1, o_hi, o_lo, lambda k: pe.wait_ge(d_lo, k + 7))
            ffn_pe(pe, 0, FFN0, 1, 2)
            rec_pe(pe)
            states_pe(pe)
            proj_pe(pe, OUT0, 3, h_hi, h_lo, None)
            ffn_pe(pe, 1, FFN1, 3, None)
            out_pe(pe)


_INS = ["x_prompt", "x_sample", "cache_ckv", "cache_krope", "page_table", "state_lru_h", "state_lru_conv",
        "state_ffn_conv", "norm_mix", "norm_ffn", "attn_w_down", "attn_g_q_lora", "attn_w_uq", "attn_g_kv_lora",
        "attn_g_qn", "attn_g_qr", "attn_g_kn", "attn_g_kr", "attn_w_uk", "attn_w_uv", "attn_w_o", "rec_w_in",
        "rec_conv_w", "rec_conv_b", "rec_w_a", "rec_b_a", "rec_w_i", "rec_b_i", "rec_lambda", "rec_w_out",
        "ffn_w_up", "ffn_conv_w", "ffn_conv_b", "ffn_w_down"]
_OUTS = [("y_prompt", (1, TP, D)), ("y_sample", (NB, TS, D)), ("ckv_prompt", (1, 1, TP, KL)),
         ("krope_prompt", (1, 1, TP, DR)), ("ckv_sample", (1, NB, TS, KL)), ("krope_sample", (1, NB, TS, DR)),
         ("lru_h_prompt", (1, 1, D)), ("lru_h_sample", (1, NB, D)), ("lru_conv_prompt", (1, 1, RW - 1, D)),
         ("lru_conv_sample", (1, NB, RW - 1, D)), ("ffn_conv_prompt", (2, 1, FW - 1, FF)),
         ("ffn_conv_sample", (2, NB, FW - 1, FF))]


def constants():
    import numpy as np

    c = np.zeros((P, C_ALL), np.float32)
    i = np.arange(P)
    c[:, C_ID:C_ID + P] = np.eye(P)
    c[:, C_ONE:C_ONE + P] = 1.0
    c[:, C_B64:C_B64 + P] = i[:, None] // 64 == i[None, :] // 64
    c[:, C_B32:C_B32 + P] = i[:, None] // 32 == i[None, :] // 32
    same = i[:, None] // DR == i[None, :] // DR
    k, m = i[:, None] % DR, i[None, :] % DR
    half = DR // 2
    c[:, C_ROT:C_ROT + P] = same * ((k == m - half) * 1.0 - (k == m + half) * 1.0)
    c[:, C_CM:C_CM + P] = np.where(i[None, :] <= i[:, None], 0.0, NEG)
    j = np.arange(TN)
    ok = (j[:, None] // TS == j[None, :] // TS) & (j[:, None] <= j[None, :])
    c[:TN, C_NM:C_NM + TN] = np.where(ok, 0.0, NEG)
    pos = np.concatenate([np.arange(TP), PAGES * PAGE + np.arange(TN) % TS]).astype(np.float32)
    inv = (np.float32(10000.0) ** (-np.arange(0, DR, 2, dtype=np.float32) / np.float32(DR))).astype(np.float32)
    ang = (pos[None, :] * inv[(i % half)][:, None]).astype(np.float32).astype(np.float64)
    c[:, C_COS:C_COS + T] = np.cos(ang)
    c[:, C_SIN:C_SIN + T] = np.sin(ang)
    return c


def kernel(**inputs):
    import numpy as _np
    import concourse.bacc as _bacc
    from concourse import mybir as _mybir
    from concourse.bass_utils import run_bass_kernel_spmd as _run

    nc = _bacc.Bacc("TRN2", target_bir_lowering=False, num_devices=1, dynamic_dma_scratch_size=1024)
    arrays, I, O = {}, {}, {}
    for name in _INS + ["consts"]:
        a = constants() if name == "consts" else _np.ascontiguousarray(inputs[name])
        arrays[f"in_{name}"] = a
        I[name] = nc.dram_tensor(f"in_{name}", a.shape, _mybir.dt.from_np(a.dtype), kind="ExternalInput").ap()
    for name, shape in _OUTS:
        O[name] = nc.dram_tensor(f"out_{name}", shape, F32, kind="ExternalOutput").ap()
    build(nc, I, O)
    r = _run(nc, [arrays], core_ids=[0])
    return tuple(r.results[0][f"out_{name}"] for name, _ in _OUTS)
```

```python
from contextlib import ExitStack

import concourse.bass as bass
from concourse import mybir

F32 = mybir.dt.float32
F32R = mybir.dt.float32r
I32 = mybir.dt.int32
ALU = mybir.AluOpType
ACT = mybir.ActivationFunctionType
AX = mybir.AxisListType

P = 128
D = 1024
DC = D // P
TP, NB, TS = 512, 8, 8
TN = NB * TS
T = TP + TN
HT = T // 2
NH, DN, DR, DV = 16, 64, 32, 64
QL, KL = 512, 256
HQ = NH * TS
PAGES, PAGE = 16, 128
SEQ_BLOCKS = PAGES + 1
FF = 3 * D
FC = FF // P
THIRDS, TF = 3, FC // 3
RW, FW = 4, 3
EPS = 1e-6
SCALE = float((DN + DR) ** -0.5)
NEG = -1e30

C_ID, C_ONE, C_B64, C_B32, C_ROT, C_CM, C_NM, C_COS, C_SIN = 0, 128, 256, 384, 512, 640, 768, 832, 832 + T
C_ALL = C_SIN + T
R_CS, R_CW, R_CB, R_BA, R_BI, R_LAM, R_H, R_NM, R_NF = 0, 24, 28, 29, 30, 31, 32, 40, 42
R_ALL = 44
F_ST, F_CW, F_CB, F_ALL = 0, 16, 19, 20
G_Q, G_KV, G_QN, G_QR, G_KN, G_KR, G_QNS, G_QRS = 0, 4, 6, 7, 8, 9, 10, 11

DOWN0, UQ0, WO0 = 0, 7, 13
FFN0 = WO0 + 8
REC0 = FFN0 + THIRDS * 24
OUT0 = REC0 + 16
FFN1 = OUT0 + 8
TILES = FFN1 + THIRDS * 24
UQ_DMAS = 8

R0, R1, XN, AP_ = 0, 9216, 17280, 26496
ARENA = 33920
A_UK, A_CKV, A_OT, A_V, A_QC, A_P = 0, 5120, 8576, 13184, XN, AP_
UKC = 1280


def loaded(t):
    return sum(16 * (UQ_DMAS if UQ0 <= u < WO0 else 1) for u in range(t % 4, t + 1, 4))


def uk_col(h):
    return h * DN + (P if h * DN >= 768 else 0)


def build(nc, I, O):
    with ExitStack() as ctx:
        def sb(name, shape, dt=F32):
            return ctx.enter_context(nc.sbuf_tensor(name, shape, dt))

        def sem(name):
            return ctx.enter_context(nc.semaphore(name))

        xT = sb("xT", [P, DC, T])
        raw = sb("raw", [P, 4, 1024])
        whi = sb("whi", [P, 2, 1024], F32R)
        wlo = sb("wlo", [P, 2, 1024], F32R)
        cst = sb("cst", [P, C_ALL])
        arena_at = nc.sbuf_base
        arena = sb("arena", [P, ARENA])
        rpar = sb("rpar", [P, DC, R_ALL])
        smallg = sb("smallg", [P, 12])
        work = sb("work", [P, 5 * T])
        snew = sb("snew", [P, NB, HQ])
        cnat = sb("cnat", [TN, KL + 1])
        krw_rope = sb("krw_rope", [DR, T])
        pt = sb("pt", [1, NB * PAGES], I32)
        cols = sb("cols", [P, 32])
        ps = ctx.enter_context(nc.psum_tensor("ps", [P, 8, 512], F32))

        def area(off, *dims, dt=F32):
            n = 1
            for d in dims:
                n *= d
            if dt is F32:
                v = arena[:, off:off + n]
            else:
                v = nc.alloc_sbuf_tensor_at(f"split_{off}_{n}", [P, n], dt, offset=arena_at + 4 * off)[:]
            if len(dims) == 2:
                return v.rearrange("p (a b) -> p a b", a=dims[0])
            if len(dims) == 3:
                return v.rearrange("p (a b c) -> p a b c", a=dims[0], b=dims[1])
            if len(dims) == 4:
                return v.rearrange("p (a b c d) -> p a b c d", a=dims[0], b=dims[1], c=dims[2])
            return v

        def f32(v):
            return v.bitcast(F32)

        def pair(k, n=HT):
            return ps[:, 2 * k:2 * k + 2, 0:n]

        def two(v):
            return v.rearrange("p (a b) -> p a b", a=2)

        ident = cst[:, C_ID:C_ID + P]
        ones = cst[:, C_ONE:C_ONE + P]
        blk64 = cst[:, C_B64:C_B64 + P]
        blk32 = cst[:, C_B32:C_B32 + P]
        rotm = cst[:, C_ROT:C_ROT + P]
        cmask = cst[:, C_CM:C_CM + P]
        nmask = cst[0:TN, C_NM:C_NM + TN]
        cosT = cst[:, C_COS:C_COS + T]
        sinT = cst[:, C_SIN:C_SIN + T]
        sq = [work[:, i * T:(i + 1) * T] for i in range(2)]
        rs = [work[:, (2 + i) * T:(3 + i) * T] for i in range(3)]

        xin = area(R0, 5, D)
        xn_hi = area(XN, DC, T, dt=F32R)
        xn_lo = area(XN + DC * T, DC, T, dt=F32R)
        h_hi = area(R0, DC, T, dt=F32R)
        h_lo = area(R0 + DC * T, DC, T, dt=F32R)

        w_loaded = [sem(f"w_loaded{i}") for i in range(4)]
        w_hi, w_lo, w_used = sem("w_hi"), sem("w_lo"), sem("w_used")
        acc_free = [sem(f"acc_free{i}") for i in range(2)]

        block = ctx.enter_context(nc.Block())

        def load_tile(sp, t, src, it=0):
            if t >= 4:
                sp.wait_ge(w_lo, t - 3 + 4 * it)
            sp.dma_start(raw[:, t % 4, :].rearrange("p (k n) -> p k n", n=P), src).then_inc(w_loaded[t % 4], 16)

        def split_hi(act, t, it=0):
            act.wait_ge(w_loaded[t % 4], loaded(t) + 16 * it)
            if t >= 2:
                act.wait_ge(w_used, t - 1 + 4 * it)
            act.copy(whi[:, t % 2, :], raw[:, t % 4, :]).then_inc(w_hi, 1)

        def split_lo(pool, t, it=0):
            pool.wait_ge(w_hi, t + 1 + 4 * it)
            pool.tensor_tensor(wlo[:, t % 2, :], raw[:, t % 4, :], f32(whi[:, t % 2, :]),
                               ALU.subtract).then_inc(w_lo, 1)

        def product(pe, out, wh, wl, xh, xl, first, last):
            for o, a, b in zip(out, xh, xl):
                pe.matmul(o, wh, a, start=first, stop=False)
                pe.matmul(o, wh, b, start=False, stop=False)
            for o, a in zip(out, xh):
                mm = pe.matmul(o, wl, a, start=False, stop=last)
            return mm

        def halves(v):
            return [v[:, 0:HT], v[:, HT:T]]

        def acc(p):
            return [ps[:, 2 * p, 0:HT], ps[:, 2 * p + 1, 0:HT]]

        def tile_product(pe, t, a, xh, xl, it=0, at=0, kn=8, ready=None, part=None):
            pe.wait_ge(w_lo, t + 1 + 4 * it)
            if a >= 2:
                pe.wait_ge(acc_free[a % 2], a // 2 + 2 * it)
            wh = whi[:, t % 2, :].rearrange("p (k n) -> p k n", n=P)
            wl = wlo[:, t % 2, :].rearrange("p (k n) -> p k n", n=P)
            for k in part or range(kn):
                if ready:
                    ready(k)
                mm = product(pe, acc(a % 2), wh[:, at + k, :], wl[:, at + k, :],
                             halves(xh[:, k, :]), halves(xl[:, k, :]), k == 0, k == kn - 1)
            return mm

        def ones_product(pe, bank, m, src, first=True, last=True, n=P):
            for i in range(2):
                mm = pe.matmul(ps[0:n, bank + i, 0:HT], m, src[:, i * HT:(i + 1) * HT], start=first, stop=last)
            return mm

        class Chain:

            def __init__(self, eng, s, base=0):
                self.eng, self.s, self.n = eng, s, base

            def __call__(self, ins):
                ins.then_inc(self.s, 1)
                self.n = self.n + 1
                self.eng.wait_ge(self.s, self.n)

        n_sq = sem("n_sq")
        n_ac = sem("n_ac")
        n_ss = sem("n_ss")
        n_ln = sem("n_ln")
        n_rs = sem("n_rs")
        n_hi = sem("n_hi")
        n_lo = sem("n_lo")
        N_ROW = [R_NM, R_NF, R_NM + 1, R_NF + 1]

        def gain(i, c):
            return rpar[:, c, N_ROW[i]:N_ROW[i] + 1]

        def norm_chunk_act(act, i, c):
            act.activation(xn_hi[:, c, :], xT[:, c, :], ACT.Copy, scale=gain(i, c)).then_inc(n_hi, 1)
            if c >= 3:
                act.wait_ge(n_ac, (DC - 1) * i + c - 2)
            act.activation(sq[c % 2] if c else rs[1], xT[:, c, :], ACT.Square).then_inc(n_sq, 1)

        def norm_chunk_dve(dve, i, c):
            dve.wait_ge(n_hi, DC * i + c + 1)
            dve.scalar_tensor_tensor(out=xn_lo[:, c, :], in0=xT[:, c, :], scalar=gain(i, c),
                                     in1=f32(xn_hi[:, c, :]), op0=ALU.mult, op1=ALU.subtract).then_inc(n_lo, 1)

        def norm_add(pool, i, c):
            if c == 0:
                return
            pool.wait_ge(n_sq, DC * i + c + 1)
            if c >= 2:
                pool.wait_ge(n_ac, (DC - 1) * i + c - 1)
            pool.tensor_tensor(rs[1], rs[1], sq[c % 2], ALU.add).then_inc(n_ac, 1)

        def norm_sum(pe, i):
            pe.wait_ge(n_ac, (DC - 1) * (i + 1))
            ones_product(pe, 6, ones, rs[1]).then_inc(n_ss, 1)

        def inverse_root(act, out, src, n, s_ln, s_out, k):
            act.activation(out, src, ACT.Ln, bias=EPS, scale=1.0 / n).then_inc(s_ln, 1)
            act.wait_ge(s_ln, k)
            act.activation(out, out, ACT.Exp, scale=-0.5).then_inc(s_out, 1)

        def norm_root(act, i):
            act.wait_ge(n_ss, i + 1)
            inverse_root(act, two(rs[0]), pair(3), D, n_ln, n_rs, i + 1)

        def norm_ready(pe, i):
            return lambda k: pe.wait_ge(n_lo, DC * i + k + 1)

        def add_x(dve, t, d, it=0):
            dve.wait_ge(w_used, t + 1 + 4 * it)
            v = xT[:, bass.ds(d, 1), :].rearrange("p a (b c) -> p (a b) c", b=2)
            dve.tensor_tensor(v, v, pair(t % 2), ALU.add).then_inc(acc_free[t % 2], 1)

        def x_added(eng, t, it=0):
            eng.wait_ge(acc_free[t % 2], (t + 6) // 2 + 1 + 2 * it)

        s_cst, s_nat, s_small, s_pt = sem("s_cst"), sem("s_nat"), sem("s_small"), sem("s_pt")
        s_x = [sem(f"s_x{i}") for i in range(5)]
        xt_ps, xt_ev, rp_ps, rp_ev, s_gs = sem("xt_ps"), sem("xt_ev"), sem("rp_ps"), sem("rp_ev"), sem("s_gs")
        rnat = area(A_P, D)

        def load_inputs(sp):
            sp.dma_start(cst[:], I["consts"]).then_inc(s_cst, 16)
            for i in range(4):
                sp.dma_start(xin[:, i, :], I["x_prompt"][0, i * P:(i + 1) * P, :]).then_inc(s_x[i], 16)
            sp.dma_start(xin[0:TN, 4, :], I["x_sample"].rearrange("b t d -> (b t) d")).then_inc(s_x[4], 16)
            for row, src in ((R_CS, I["state_lru_conv"][0].rearrange("b w d -> (b w) d")),
                             (R_CW, I["rec_conv_w"][0]), (R_CB, I["rec_conv_b"]),
                             (R_BA, I["rec_b_a"].rearrange("a n d -> a (n d)")),
                             (R_BI, I["rec_b_i"].rearrange("a n d -> a (n d)")),
                             (R_LAM, I["rec_lambda"]), (R_H, I["state_lru_h"][0]),
                             (R_NM, I["norm_mix"]), (R_NF, I["norm_ffn"])):
                sp.dma_start(rnat[row:row + src.shape[0], :], src).then_inc(s_nat, 16)

        NAT_DMAS = 9

        def load_gains(sp):
            with nc.allow_non_contiguous_dma(reason="a few hundred words"):
                def col(at, n, c, name, m=1):
                    sp.dma_start(smallg[at:at + n, c:c + m],
                                 I[name].rearrange("a (c p) -> p (a c)", p=n)).then_inc(s_small, 16)
                col(0, P, G_Q, "attn_g_q_lora", 4)
                col(0, P, G_KV, "attn_g_kv_lora", 2)
                for k in range(2):
                    col(64 * k, DN, G_QN, "attn_g_qn")
                    col(64 * k, DN, G_KN, "attn_g_kn")
                for k in range(4):
                    col(32 * k, DR, G_QR, "attn_g_qr")
                col(0, DR, G_KR, "attn_g_kr")
            sp.dma_start(pt[:], I["page_table"].rearrange("b n -> (b n)").rearrange("(a n) -> a n", a=1))\
              .then_inc(s_pt, 16)

        SMALL_DMAS = 11

        def transpose_inputs(pe):
            pe.wait_ge(s_cst, 16)
            for i in range(5):
                pe.wait_ge(s_x[i], 16)
            pe.wait_ge(s_nat, 16 * NAT_DMAS)
            for c in range(DC):
                mm = pe.transpose(ps[:, 4, c * R_ALL:(c + 1) * R_ALL], rnat[0:R_ALL, c * P:(c + 1) * P],
                                  ident[0:R_ALL, 0:R_ALL])
            mm.then_inc(rp_ps, 1)
            for c in range(DC):
                if c >= 2:
                    pe.wait_ge(xt_ev, c - 1)
                b = 2 * (c % 2)
                for i in range(5):
                    n = P if i < 4 else TN
                    mm = pe.transpose(ps[:, b + i // 4, (i % 4) * P:(i % 4) * P + n],
                                      xin[0:n, i, c * P:(c + 1) * P], ident[0:n, 0:n])
                mm.then_inc(xt_ps, 1)

        def keep_inputs(dve):
            dve.wait_ge(rp_ps, 1)
            dve.tensor_copy(rpar[:].rearrange("p a b -> p (a b)"), ps[:, 4, 0:DC * R_ALL]).then_inc(rp_ev, 1)
            dve.wait_ge(rp_ev, 1)
            for c in range(DC):
                dve.wait_ge(xt_ps, c + 1)
                b = 2 * (c % 2)
                dve.tensor_copy(xT[:, c, 0:TP], ps[:, b, :])
                dve.tensor_copy(xT[:, c, TP:T], ps[:, b + 1, 0:TN]).then_inc(xt_ev, 1)
                if c:
                    norm_chunk_dve(dve, 0, c - 1)
            norm_chunk_dve(dve, 0, DC - 1)
            dve.wait_ge(s_small, 16 * SMALL_DMAS)
            dve.tensor_scalar(smallg[:, G_QNS:G_QRS + 1], smallg[:, G_QN:G_QR + 1], SCALE, None,
                              ALU.mult).then_inc(s_gs, 1)
            dve.memset(cnat[:, KL:KL + 1], 1.0)

        dq = area(A_P + 4608, 4, T)
        cq_hi = area(A_P, 4, T, dt=F32R)
        cq_lo = area(A_P + 2304, 4, T, dt=F32R)
        ckv = area(A_CKV, 2, T)
        ckv_hi = area(A_CKV + 1152, 2, T, dt=F32R)
        ckv_lo = area(A_CKV + 2304, 2, T, dt=F32R)
        krw = area(A_OT, 4, T)
        onat = area(A_OT + 2304, 5, KL + DR)
        d_sq, d_ss, d_ln, d_rs = sem("d_sq"), sem("d_ss"), sem("d_ln"), sem("d_rs")
        d_f, d_hi, d_lo, d_ch = sem("d_f"), sem("d_hi"), sem("d_lo"), sem("d_ch")
        kr_n, kr_rot, kr_ok = sem("kr_n"), sem("kr_rot"), sem("kr_ok")
        on_ps, on_ev, s_onat = sem("on_ps"), sem("on_ev"), sem("s_onat")
        SS_BANK = [6, 6, 6, 6, 4, 4, 6]

        def down_src(t):
            n0 = min(t * P, QL + KL + DR - P)
            return I["attn_w_down"][0].rearrange("(k p) n -> p k n", p=P)[:, :, n0:n0 + P]

        def down_dst(c):
            return dq[:, c, :] if c < 4 else ckv[:, c - 4, :] if c < 6 else krw[0:DR, 0, :]

        def down_sum(pe, c):
            pe.wait_ge(d_sq, c + 1)
            if c == 6:
                pe.wait_ge(d_ln, 1)
            n = P if c < 6 else DR
            ones_product(pe, SS_BANK[c], ones[0:n, 0:n], sq[c % 2][0:n, :], c in (0, 4, 6), c in (3, 5, 6), n)\
                .then_inc(d_ss, 1)

        def down_pe(pe):
            pe.wait_ge(rp_ev, 1)
            for t in range(7):
                if t < 2:
                    pe.wait_ge(xt_ev, DC)
                tile_product(pe, t, t, xn_hi, xn_lo, ready=norm_ready(pe, 0) if t == 0 else None).then_inc(w_used, 1)
                if t == 0:
                    norm_sum(pe, 0)
                if t == 1:
                    pe.wait_ge(n_ln, 1)
                if t:
                    down_sum(pe, t - 1)
            down_sum(pe, 6)
            pe.wait_ge(kr_n, 1)
            pe.wait_ge(d_ln, 2)
            ones_product(pe, 4, rotm[0:DR, 0:DR], krw[0:DR, 1, :], n=DR).then_inc(kr_rot, 1)
            pe.wait_ge(d_f, 6)
            pe.wait_ge(kr_ok, 1)
            for i in range(5):
                n = P if i < 4 else TN
                if i >= 2:
                    pe.wait_ge(on_ev, i - 1)
                for c in range(2):
                    pe.transpose(ps[0:n, i % 2, c * P:(c + 1) * P], ckv[:, c, i * P:i * P + n], ident)
                pe.transpose(ps[0:n, i % 2, KL:KL + DR], krw_rope[:, i * P:i * P + n],
                             ident[0:DR, 0:DR]).then_inc(on_ps, 1)

        def down_act(act):
            for t in range(7):
                split_hi(act, t + 1)
                if t == 0:
                    norm_root(act, 0)
                act.wait_ge(acc_free[t % 2], t // 2 + 1)
                if t >= 2:
                    act.wait_ge(d_ss, t - 1)
                n = P if t < 6 else DR
                act.activation(sq[t % 2][0:n, :], down_dst(t), ACT.Square).then_inc(d_sq, 1)
                if t == 5:
                    act.wait_ge(d_ss, 4)
                    inverse_root(act, two(rs[1]), pair(3), QL, d_ln, d_rs, 1)
            act.wait_ge(d_ss, 6)
            inverse_root(act, two(rs[2]), pair(2), KL, d_ln, d_rs, 2)
            act.wait_ge(d_ss, 7)
            inverse_root(act, two(rs[0])[0:DR], pair(3)[0:DR], DR, d_ln, d_rs, 3)
            for c in range(6):
                act.wait_ge(d_f, c + 1)
                act.copy(cq_hi[:, c, :] if c < 4 else ckv_hi[:, c - 4, :], down_dst(c)).then_inc(d_hi, 1)

        def down_dve(dve, ch):
            for t in range(7):
                dve.wait_ge(w_used, t + 1)
                if t == 0:
                    dve.wait_ge(n_rs, 1)
                if t < 6:
                    dve.tensor_tensor(two(down_dst(t)), pair(t % 2), two(rs[0]), ALU.mult).then_inc(acc_free[t % 2], 1)
                else:
                    dve.tensor_tensor(two(krw[0:DR, 0, :]), pair(0)[P - DR:P], two(rs[0])[P - DR:P], ALU.mult)\
                       .then_inc(acc_free[0], 1)
            dve.wait_ge(s_gs, 1)
            dve.wait_ge(acc_free[0], 4)
            dve.wait_ge(acc_free[1], 3)
            for c in range(6):
                if c == 0:
                    dve.wait_ge(d_rs, 1)
                    dve.wait_ge(d_sq, 7)
                if c == 4:
                    dve.wait_ge(d_rs, 2)
                g = smallg[:, (G_Q + c if c < 4 else G_KV + c - 4):(G_Q + c if c < 4 else G_KV + c - 4) + 1]
                dve.scalar_tensor_tensor(out=down_dst(c), in0=down_dst(c), scalar=g, in1=rs[1 if c < 4 else 2],
                                         op0=ALU.mult, op1=ALU.mult).then_inc(d_f, 1)
            for c in range(6):
                dve.wait_ge(d_hi, c + 1)
                hi, lo = (cq_hi[:, c, :], cq_lo[:, c, :]) if c < 4 else (ckv_hi[:, c - 4, :], ckv_lo[:, c - 4, :])
                dve.tensor_tensor(lo, down_dst(c), f32(hi), ALU.subtract).then_inc(d_lo, 1)
            dve.wait_ge(d_rs, 3)
            dve.scalar_tensor_tensor(out=krw[0:DR, 1, :], in0=krw[0:DR, 0, :], scalar=smallg[0:DR, G_KR:G_KR + 1],
                                     in1=rs[0][0:DR, :], op0=ALU.mult, op1=ALU.mult).then_inc(kr_n, 1)
            dve.wait_ge(kr_n, 1)
            ch(dve.tensor_tensor(krw[0:DR, 2, :], krw[0:DR, 1, :], cosT[0:DR, :], ALU.mult))
            dve.wait_ge(kr_rot, 1)
            ch(dve.tensor_tensor(two(krw[0:DR, 3, :]), pair(2)[0:DR], two(sinT[0:DR, :]), ALU.mult))
            dve.tensor_tensor(krw_rope[:, :], krw[0:DR, 2, :], krw[0:DR, 3, :], ALU.add).then_inc(kr_ok, 1)
            for i in range(5):
                n = P if i < 4 else TN
                dve.wait_ge(on_ps, i + 1)
                dve.tensor_copy(onat[0:n, i, :], ps[0:n, i % 2, 0:KL + DR]).then_inc(on_ev, 1)
            dve.wait_ge(on_ev, 5)
            dve.tensor_copy(cnat[:, 0:KL], onat[0:TN, 4, 0:KL]).then_inc(on_ev, 1)

        def down_store(sp):
            sp.wait_ge(on_ev, 5)
            sp.dma_start(O["ckv_prompt"][0, 0].rearrange("(i p) c -> p i c", p=P), onat[:, 0:4, 0:KL]).then_inc(s_onat, 16)
            sp.dma_start(O["krope_prompt"][0, 0].rearrange("(i p) c -> p i c", p=P), onat[:, 0:4, KL:KL + DR])\
              .then_inc(s_onat, 16)
            sp.dma_start(O["ckv_sample"][0].rearrange("b t c -> (b t) c"), onat[0:TN, 4, 0:KL]).then_inc(s_onat, 16)
            sp.dma_start(O["krope_sample"][0].rearrange("b t c -> (b t) c"), onat[0:TN, 4, KL:KL + DR])\
              .then_inc(s_onat, 16)

        qc = area(A_QC, NH, T)
        qraw = area(A_V, 2, T)
        qrn = area(A_V + 2 * T, 2, T)
        qt = area(A_V + 4 * T, 2, T)
        u_half, u_sq, u_ss = sem("u_half"), sem("u_sq"), sem("u_ss")
        u_ln, u_rs, u_n, u_rot, u_ch, u_q = (sem("u_ln"), sem("u_rs"), sem("u_n"), sem("u_rot"), sem("u_ch"),
                                             sem("u_q"))
        uk_raw = area(A_OT, 2, D)
        uk = area(A_UK, 2, 2, UKC, dt=F32R)
        s_uk = sem("s_uk")
        res_h, res_l = sem("res_h"), sem("res_l")

        def load_uq(sp, t):
            sp.wait_ge(w_lo, t - 3)
            w = I["attn_w_uq"][0].rearrange("(k p) (h e) -> p k h e", p=P, e=DN + DR)
            for j in range(2):
                c = 2 * (t - UQ0) + j
                for k in range(4):
                    dst = raw[:, t % 4, (4 * j + k) * P:(4 * j + k + 1) * P]
                    if c < 8:
                        src, e = w[:, k, 2 * c:2 * c + 2, 0:DN], DN
                    else:
                        src, e = w[:, k, 4 * (c - 8):4 * (c - 8) + 4, DN:DN + DR], DR
                    sp.dma_start(dst.rearrange("p (h e) -> p h e", e=e), src).then_inc(w_loaded[t % 4], 16)

        def uq_sum(pe, c):
            pe.wait_ge(u_sq, c + 1)
            if c >= 2:
                pe.wait_ge(u_ln, c - 1)
            if c >= 10:
                pe.wait_ge(u_q, c - 9)
            ones_product(pe, 4 + 2 * (c % 2), blk64 if c < 8 else blk32, sq[c % 2]).then_inc(u_ss, 1)

        def uq_rotate(pe, c):
            pe.wait_ge(u_n, c - 7)
            pe.wait_ge(u_ln, c + 1)
            ones_product(pe, 4 + 2 * (c % 2), rotm, qrn[:, c % 2, :]).then_inc(u_rot, 1)

        def uq_pe(pe):
            pe.wait_ge(d_ln, 3)
            pe.wait_ge(on_ev, 5)
            for c in range(12):
                t = UQ0 + c // 2
                mm = tile_product(pe, t, 7 + c, cq_hi, cq_lo, at=4 * (c % 2), kn=4,
                                  ready=(lambda k: pe.wait_ge(d_lo, k + 1)) if c == 0 else None)
                mm.then_inc(w_used if c % 2 else u_half, 1)
                if c >= 1:
                    uq_sum(pe, c - 1)
                if c >= 10:
                    uq_rotate(pe, c - 2)
            uq_sum(pe, 11)
            uq_rotate(pe, 10)
            uq_rotate(pe, 11)

        def uq_act(act):
            for c in range(12):
                if c % 2 == 0 and c < 10:
                    split_hi(act, UQ0 + c // 2 + 1)
                act.wait_ge(acc_free[(7 + c) % 2], (7 + c) // 2 + 1)
                if c >= 2:
                    act.wait_ge(u_ss, c - 1)
                act.activation(sq[c % 2], qraw[:, c % 2, :], ACT.Square).then_inc(u_sq, 1)
                act.wait_ge(u_ss, c + 1)
                if c >= 2:
                    act.wait_ge(*((u_n, c - 9) if c >= 10 else (u_ch, 2 * (c - 1))))
                inverse_root(act, two(rs[c % 2]), pair(2 + c % 2), DN if c < 8 else DR, u_ln, u_rs, c + 1)
            act.wait_ge(s_uk, 16)
            for k in range(2):
                act.copy(uk[:, 0, k, 0:768], uk_raw[:, k, 0:768])
                act.copy(uk[:, 0, k, 896:1152], uk_raw[:, k, 768:1024]).then_inc(res_h, 1)

        def uq_dve(dve):
            ch = Chain(dve, u_ch)

            def evacuate(c):
                if c % 2:
                    dve.wait_ge(w_used, UQ0 + c // 2 + 1)
                else:
                    dve.wait_ge(u_half, c // 2 + 1)
                if c >= 2:
                    dve.wait_ge(u_sq, c - 1)
                if c >= 10:
                    dve.wait_ge(u_n, c - 9)
                dve.tensor_copy(two(qraw[:, c % 2, :]), pair((7 + c) % 2)).then_inc(acc_free[(7 + c) % 2], 1)

            def finish(c):
                dve.wait_ge(u_rs, c + 1)
                dve.wait_ge(acc_free[(7 + c) % 2], (7 + c) // 2 + 1)
                if c < 8:
                    for k in range(2):
                        r = slice(DN * k, DN * k + DN)
                        ch(dve.scalar_tensor_tensor(out=qc[0:DN, 2 * c + k, :], in0=qraw[r, c % 2, :],
                                                    scalar=smallg[r, G_QNS:G_QNS + 1], in1=rs[c % 2][r, :],
                                                    op0=ALU.mult, op1=ALU.mult))
                    return
                if c >= 10:
                    dve.wait_ge(u_rot, c - 9)
                dve.scalar_tensor_tensor(out=qrn[:, c % 2, :], in0=qraw[:, c % 2, :],
                                         scalar=smallg[:, G_QRS:G_QRS + 1], in1=rs[c % 2],
                                         op0=ALU.mult, op1=ALU.mult).then_inc(u_n, 1)

            def rotate(c):
                dve.wait_ge(u_n, c - 7)
                if c >= 9:
                    dve.wait_ge(u_q, c - 8)
                ch(dve.tensor_tensor(qt[:, 0, :], qrn[:, c % 2, :], cosT, ALU.mult))
                dve.wait_ge(u_rot, c - 7)
                ch(dve.tensor_tensor(two(qt[:, 1, :]), pair(2 + c % 2), two(sinT), ALU.mult))
                for k in range(4):
                    r = slice(DR * k, DR * k + DR)
                    ins = dve.tensor_tensor(qc[DN:DN + DR, 4 * (c - 8) + k, :], qt[r, 0, :], qt[r, 1, :], ALU.add)
                ins.then_inc(u_q, 1)

            for c in range(12):
                evacuate(c)
                if c >= 1:
                    finish(c - 1)
                if c >= 10:
                    rotate(c - 2)
            finish(11)
            rotate(10)
            rotate(11)

        def uk_pool(pool):
            for k in range(2):
                pool.wait_ge(res_h, k + 1)
                pool.tensor_tensor(uk[:, 1, k, 0:768], uk_raw[:, k, 0:768], f32(uk[:, 0, k, 0:768]), ALU.subtract)
                pool.tensor_tensor(uk[:, 1, k, 896:1152], uk_raw[:, k, 768:1024], f32(uk[:, 0, k, 896:1152]),
                                   ALU.subtract).then_inc(res_l, 1)

        wukT = area(A_P, NH, KL)
        qs = area(A_V, NH, TN)
        qabs = [w[:].rearrange("p a n -> p (a n)").rearrange("p (k b q) -> p k b q", k=2, b=NB)
                for w in (whi, wlo)]
        wt_ps, wt_ev, qs_ok, qa_ps, qa_hi, qa_lo = (sem("wt_ps"), sem("wt_ev"), sem("qs_ok"), sem("qa_ps"),
                                                    sem("qa_hi"), sem("qa_lo"))
        uv_raw = area(A_P + 4608, 2, D)
        uv = area(A_P, 2, 2, D, dt=F32R)
        vals = area(A_V, 4, D)
        s_uv = sem("s_uv")

        def values_pe(pe):
            pe.wait_ge(s_uk, 16)
            pe.wait_ge(u_q, 4)
            pe.wait_ge(acc_free[0], 10)
            pe.wait_ge(acc_free[1], 9)
            for h in range(NH):
                b = (h // 2) % 4
                if h % 2 == 0 and h >= 8:
                    pe.wait_ge(wt_ev, h // 2 - 3)
                for k in range(2):
                    mm = pe.transpose(ps[0:DN, b, (h % 2) * KL + k * P:(h % 2) * KL + (k + 1) * P],
                                      uk_raw[:, k, h * DN:(h + 1) * DN], ident)
                if h % 2:
                    mm.then_inc(wt_ps, 1)
            pe.wait_ge(qs_ok, 1)
            pe.wait_ge(wt_ev, 8)
            for k in range(2):
                for h in range(NH):
                    mm = pe.matmul(ps[:, 4 + 2 * k + h // 8, (h % 8) * TN:(h % 8 + 1) * TN],
                                   wukT[0:DN, h, k * P:(k + 1) * P], qs[0:DN, h, :], start=True, stop=True)
                    if h % 8 == 7:
                        mm.then_inc(qa_ps, 1)
            pe.wait_ge(res_l, 4)
            pe.wait_ge(d_lo, 6)
            for i in range(8):
                blk, half = i // 2, i % 2
                if i >= 4:
                    pe.wait_ge(wt_ev, 8 + i - 3)
                tok = slice(blk * P, (blk + 1) * P)
                col = slice(half * 512, half * 512 + 512)
                for k in range(2):
                    pe.matmul(ps[:, i % 4, :], ckv_hi[:, k, tok], uv[:, 0, k, col], start=(k == 0), stop=False)
                    pe.matmul(ps[:, i % 4, :], ckv_hi[:, k, tok], uv[:, 1, k, col], start=False, stop=False)
                    mm = pe.matmul(ps[:, i % 4, :], ckv_lo[:, k, tok], uv[:, 0, k, col], start=False, stop=(k == 1))
                mm.then_inc(wt_ps, 1)

        def values_dve(dve):
            dve.wait_ge(u_q, 4)
            dve.tensor_copy(snew[DN:DN + DR, :, :].rearrange("p b (h t) -> p b h t", h=NH),
                            qc[DN:DN + DR, :, TP:T].rearrange("p h (b t) -> p b h t", b=NB))
            dve.tensor_scalar(qs[0:DN, :, :], qc[0:DN, :, TP:T], smallg[0:DN, G_KN:G_KN + 1], None,
                              ALU.mult).then_inc(qs_ok, 1)
            for j in range(8):
                dve.wait_ge(wt_ps, j + 1)
                dve.tensor_copy(wukT[0:DN, 2 * j:2 * j + 2, :].rearrange("p a b -> p (a b)"), ps[0:DN, j % 4, :])\
                   .then_inc(wt_ev, 1)
            for j in range(4):
                k, g = j // 2, j % 2
                dve.wait_ge(qa_hi, j + 1)
                for b in range(NB):
                    ins = dve.tensor_tensor(
                        qabs[1][:, k, b, g * 64:(g + 1) * 64].rearrange("p (h t) -> p h t", h=8),
                        ps[:, 4 + j, :].rearrange("p (h b t) -> p b h t", h=8, b=NB)[:, b],
                        f32(qabs[0][:, k, b, g * 64:(g + 1) * 64]).rearrange("p (h t) -> p h t", h=8), ALU.subtract)
                ins.then_inc(qa_lo, 1)
            for i in range(1, 8, 2):
                dve.wait_ge(wt_ps, 8 + i)
                if i == 1:
                    dve.wait_ge(qa_ps, 4)
                    dve.wait_ge(qs_ok, 1)
                dve.tensor_copy(vals[:, i // 2, 0:512], ps[:, i - 1 - 4 * ((i - 1) // 4), :])
                dve.wait_ge(wt_ps, 9 + i)
                dve.tensor_copy(vals[:, i // 2, 512:1024], ps[:, i - 4 * (i // 4), :]).then_inc(wt_ev, 2)

        def values_act(act):
            act.wait_ge(w_used, WO0)
            for j in range(4):
                k, g = j // 2, j % 2
                act.wait_ge(qa_ps, j + 1)
                for b in range(NB):
                    ins = act.copy(qabs[0][:, k, b, g * 64:(g + 1) * 64].rearrange("p (h t) -> p h t", h=8),
                                   ps[:, 4 + j, :].rearrange("p (h b t) -> p b h t", h=8, b=NB)[:, b])
                ins.then_inc(qa_hi, 1)
            act.wait_ge(s_uv, 16)
            for k in range(2):
                act.copy(uv[:, 0, k, :], uv_raw[:, k, :]).then_inc(res_h, 1)

        def uv_pool(pool):
            for k in range(2):
                pool.wait_ge(res_h, k + 3)
                pool.tensor_tensor(uv[:, 1, k, :], uv_raw[:, k, :], f32(uv[:, 0, k, :]), ALU.subtract).then_inc(res_l, 1)

        pT = area(A_P, 2, 4, TP)
        kcat = area(A_P + 4096, 4, T)
        pr = [area(A_P + 4096 + 2304, 512), area(A_P + 4096 + 2304 + 512, 512), sq[1], rs[1]]
        oT = area(A_OT, DC, T)
        k_mm, k_ev, k_sq, k_ss, k_ln, k_rs, k_cat, k_rope = (sem("k_mm"), sem("k_ev"), sem("k_sq"), sem("k_ss"),
                                                             sem("k_ln"), sem("k_rs"), sem("k_cat"), sem("k_rope"))
        p_s, p_max, p_exp, p_inv, p_ok, p_t, p_tev, p_o, p_oev, p_n, p_nev = (
            sem("p_s"), sem("p_max"), sem("p_exp"), sem("p_inv"), sem("p_ok"), sem("p_t"), sem("p_tev"),
            sem("p_o"), sem("p_oev"), sem("p_n"), sem("p_nev"))
        kflat = rs[2]
        UNITS = 4 * NH

        def key_pair(pe, j):
            if j >= 1:
                pe.wait_ge(k_ln, j)
            c0 = uk_col(2 * j)
            out = [ps[:, 4, 0:HT], ps[:, 5, 0:HT]]
            for k in range(2):
                mm = product(pe, out, uk[:, 0, k, c0:c0 + P], uk[:, 1, k, c0:c0 + P],
                             halves(ckv_hi[:, k, :]), halves(ckv_lo[:, k, :]), k == 0, k == 1)
            mm.then_inc(k_mm, 1)

        def key_sum(pe, j):
            pe.wait_ge(k_sq, j + 1)
            ones_product(pe, 4, blk64, sq[0]).then_inc(k_ss, 1)

        def key_evacuate(dve, j):
            dve.wait_ge(k_mm, j + 1)
            dve.tensor_copy(two(kflat), pair(2)).then_inc(k_ev, 1)

        def key_square(act, j):
            act.wait_ge(k_ev, j + 1)
            act.activation(sq[0], kflat, ACT.Square).then_inc(k_sq, 1)

        def key_root(act, j):
            act.wait_ge(k_ss, j + 1)
            inverse_root(act, two(rs[0]), pair(2), DN, k_ln, k_rs, j + 1)

        def key_norm(dve, j):
            dve.wait_ge(k_rs, j + 1)
            if j >= 2:
                dve.wait_ge(p_n, 2 * (j - 1))
            for k in range(2):
                r = slice(DN * k, DN * k + DN)
                ins = dve.scalar_tensor_tensor(out=kcat[0:DN, (2 * j + k) % 4, :], in0=kflat[r, :],
                                               scalar=smallg[r, G_KN:G_KN + 1], in1=rs[0][r, :],
                                               op0=ALU.mult, op1=ALU.mult)
            ins.then_inc(k_cat, 1)

        def scores(pe, u):
            h, qb = divmod(u, 4)
            n = (qb + 1) * P
            if u >= 2:
                pe.wait_ge(p_exp, u - 1)
            if qb == 0:
                pe.wait_ge(k_cat, h // 2 + 1)
            pe.matmul(ps[:, u % 2, 0:n], qc[0:96, h, qb * P:(qb + 1) * P], kcat[0:96, h % 4, 0:n],
                      start=True, stop=False)
            pe.matmul(ps[:, u % 2, qb * P:n], ident, cmask, start=False, stop=True).then_inc(p_s, 1)

        def new_scores(pe, h):
            if h == 8:
                pe.wait_ge(p_nev, 1)
            pe.matmul(ps[0:TN, 7, (h % 8) * TN:(h % 8 + 1) * TN], kcat[0:96, h % 4, TP:T], qc[0:96, h, TP:T],
                      start=True, stop=True).then_inc(p_n, 1)

        def probs_turn(pe, u):
            qb = u % 4
            pe.wait_ge(p_ok, u + 1)
            if u >= 2:
                pe.wait_ge(p_tev, u - 1)
            for kb in range(qb + 1):
                mm = pe.transpose(ps[:, 2 + u % 2, kb * P:(kb + 1) * P], pr[u % 4][:, kb * P:(kb + 1) * P], ident)
            mm.then_inc(p_t, 1)

        def attend(pe, h):
            if h >= 2 and h % 2 == 0:
                pe.wait_ge(p_oev, h // 2)
            pe.wait_ge(p_tev, 4 * h + 4)
            r = slice(DV * (h % 2), DV * (h % 2) + DV)
            for kb in range(4):
                mm = pe.matmul(ps[r, 6, kb * P:TP], vals[:, kb, h * DV:(h + 1) * DV], pT[:, h % 2, kb, kb * P:TP],
                               start=(kb == 0), stop=(kb == 3))
            mm.then_inc(p_o, 1)

        LAG = 3

        def prompt_pe(pe):
            pe.wait_ge(res_l, 2)
            pe.wait_ge(k_rope, 1)
            pe.wait_ge(qa_lo, 4)
            pe.wait_ge(wt_ev, 16)
            key_pair(pe, 0)
            key_sum(pe, 0)
            for u in range(UNITS + LAG):
                if u < UNITS:
                    h, qb = divmod(u, 4)
                    scores(pe, u)
                    if qb == 3:
                        new_scores(pe, h)
                    if u % 8 == 0 and h // 2 < 7:
                        key_pair(pe, h // 2 + 1)
                    if u % 8 == 4 and h // 2 < 7:
                        key_sum(pe, h // 2 + 1)
                if u >= LAG:
                    probs_turn(pe, u - LAG)
                    if (u - LAG) % 4 == 3 and u - LAG >= 7:
                        attend(pe, (u - LAG) // 4 - 1)
            attend(pe, NH - 1)

        def prompt_act(act):
            key_square(act, 0)
            key_root(act, 0)
            for u in range(UNITS + LAG):
                if u < UNITS:
                    h, qb = divmod(u, 4)
                    n = (qb + 1) * P
                    act.wait_ge(p_max, u + 1)
                    if u >= 4:
                        act.wait_ge(p_t, u - 3)
                    act.activation(pr[u % 4][:, 0:n], ps[:, u % 2, 0:n], ACT.Exp, bias=cols[:, u % 4:u % 4 + 1],
                                   accum_out=cols[:, 4 + u % 4:5 + u % 4]).then_inc(p_exp, 1)
                    if u % 8 == 2 and h // 2 < 7:
                        key_square(act, h // 2 + 1)
                    if u % 8 == 5 and h // 2 < 7:
                        key_root(act, h // 2 + 1)
                if u >= LAG:
                    v = u - LAG
                    h, qb = divmod(v, 4)
                    act.wait_ge(p_t, v + 1)
                    if qb == 0 and h >= 2:
                        act.wait_ge(p_o, h - 1)
                    act.copy(pT[:, h % 2, 0:qb + 1, qb * P:(qb + 1) * P],
                             ps[:, 2 + v % 2, 0:(qb + 1) * P].rearrange("p (k q) -> p k q", q=P)).then_inc(p_tev, 1)

        def prompt_dve(dve):
            dve.wait_ge(res_l, 4)
            dve.wait_ge(wt_ps, 16)
            dve.wait_ge(s_onat, 64)
            for k in range(4):
                ins = dve.tensor_copy(kcat[DN:DN + DR, k, :], krw_rope[:, :])
            ins.then_inc(k_rope, 1)
            key_evacuate(dve, 0)
            key_norm(dve, 0)
            for u in range(UNITS + 1):
                if u < UNITS:
                    h, qb = divmod(u, 4)
                    n = (qb + 1) * P
                    dve.wait_ge(p_s, u + 1)
                    if u >= 4:
                        dve.wait_ge(p_exp, u - 3)
                    dve.tensor_reduce(cols[:, u % 4:u % 4 + 1], ps[:, u % 2, 0:n], AX.X, ALU.max, negate=True)\
                       .then_inc(p_max, 1)
                if u >= 1:
                    v = u - 1
                    m = (v % 4 + 1) * P
                    dve.wait_ge(p_exp, v + 1)
                    dve.reciprocal(cols[:, 8 + v % 4:9 + v % 4], cols[:, 4 + v % 4:5 + v % 4]).then_inc(p_inv, 1)
                    dve.wait_ge(p_inv, v + 1)
                    dve.tensor_scalar(pr[v % 4][:, 0:m], pr[v % 4][:, 0:m], cols[:, 8 + v % 4:9 + v % 4], None,
                                      ALU.mult).then_inc(p_ok, 1)
                if u < UNITS:
                    if u % 8 == 1 and h // 2 < 7:
                        key_evacuate(dve, h // 2 + 1)
                    if u % 8 == 6 and h // 2 < 7:
                        key_norm(dve, h // 2 + 1)
                    if u % 8 == 7 and u >= 15:
                        outputs(dve, u // 8 - 1)
                    if u in (32, UNITS - 1):
                        new_block(dve, 0 if u == 32 else 1)
            outputs(dve, 7)

        def outputs(dve, j):
            dve.wait_ge(p_o, 2 * j + 2)
            dve.tensor_copy(oT[:, j, 0:TP], ps[:, 6, :]).then_inc(p_oev, 1)

        def new_block(dve, g):
            dve.wait_ge(p_n, 8 * g + 8)
            for b in range(NB):
                ins = dve.tensor_tensor(snew[0:TN, b, g * 64:(g + 1) * 64].rearrange("p (h t) -> p h t", h=8),
                                        ps[0:TN, 7, :].rearrange("p (h b t) -> p b h t", h=8, b=NB)[:, b],
                                        nmask[:, b * TS:(b + 1) * TS].unsqueeze(1).to_broadcast([TN, 8, TS]), ALU.add)
            ins.then_inc(p_nev, 1)

        cpg = area(A_QC, 2 * PAGES, 260)
        s_all = [area(A_P + i * SEQ_BLOCKS * HQ, SEQ_BLOCKS, HQ) for i in range(2)]
        a_sb = [area(A_P + 2 * SEQ_BLOCKS * HQ + i * 512, 4, HQ) for i in range(2)]
        sqk = area(A_P + 2 * SEQ_BLOCKS * HQ + 1024, 2, 1024)
        ctxT = area(A_CKV, 2, NH, TN)
        ct_hi = area(A_CKV + 2048, 2, 2, P, dt=F32R)
        ct_lo = area(A_CKV + 2560, 2, 2, P, dt=F32R)
        krp = sb("krp", [P, 4, DR])
        krT = sb("krT", [P, 2, P])
        qr_s = sb("qr_s", [P, 2, HQ])
        ssq = sb("ssq", [P, 2, 4 * NH])
        cx = area(A_V, KL)
        mx = area(A_V + 256, P)
        dg = area(A_V + 384, P)
        pg_in = [sem(f"pg_in{i}") for i in range(4)]
        t_ps, t_hi, t_lo, kb_mm, kb_sq, a_ev, b_mm, sq_ok, g_red = (
            sem("t_ps"), sem("t_hi"), sem("t_lo"), sem("kb_mm"), sem("kb_sq"), sem("a_ev"), sem("b_mm"),
            sem("sq_ok"), sem("g_red"))
        g_ln, g_rs, g_s1, g_s = sem("g_ln"), sem("g_rs"), sem("g_s1"), sem("g_s")
        q_hi, q_lo, q_r, n_ok = sem("q_hi"), sem("q_lo"), sem("q_r"), sem("n_ok")
        x_max, x_mt, x_m, x_dg, x_mb, x_sub, x_exp, x_ctx, x_inv, x_cx, x_ct, x_cev = (
            sem("x_max"), sem("x_mt"), sem("x_m"), sem("x_dg"), sem("x_mb"), sem("x_sub"), sem("x_exp"),
            sem("x_ctx"), sem("x_inv"), sem("x_cx"), sem("x_ct"), sem("x_cev"))
        s_init = sem("s_init")

        def page_load(sp, b, par, i, free):
            page = sp.value_load(pt[0:1, bass.ds(b * PAGES + i, 1)], min_val=0, max_val=I["cache_ckv"].shape[1] - 1)
            src = I["cache_ckv"][0][bass.ds(page, 1), :, :].rearrange("a p c -> p (a c)")
            if free and i < 3:
                sp.wait_ge(x_ctx, b - 1)
            elif free or i >= 4 or par:
                sp.wait_ge(t_ps, b * PAGES + i - 3)
            sp.dma_start(cpg[:, par * PAGES + i, 0:KL], src).then_inc(pg_in[i % 4], 16)
            src = I["cache_krope"][0][bass.ds(page, 1), :, :].rearrange("a p c -> p (a c)")
            sp.dma_start(krp[:, i % 4, :], src).then_inc(pg_in[i % 4], 16)

        def turn(pe, b, par, i):
            pe.wait_ge(pg_in[i % 4], 32 * (b * 4 + i // 4 + 1))
            if i >= 2 or par or not isinstance(b, int):
                pe.wait_ge(t_lo, b * PAGES + i - 1)
            bank = 3 + i % 2
            for k in range(2):
                pe.transpose(ps[:, bank, k * P:(k + 1) * P], cpg[:, par * PAGES + i, k * P:(k + 1) * P], ident)
            pe.transpose(ps[0:DR, bank, 2 * P:3 * P], krp[:, i % 4, :], ident).then_inc(t_ps, 1)

        def page_products(pe, b, par, i):
            pe.wait_ge(t_lo, b * PAGES + i + 1)
            later = i >= 1 or par or not isinstance(b, int)
            if i == 0:
                pe.wait_ge(q_lo, b + 1)
            c0 = [0, 384, 768 if par else 896]
            for j in range(3):
                if later:
                    pe.wait_ge(kb_sq, 3 * (b * PAGES + i) - 2 + j)
                    if j == 2:
                        pe.wait_ge(a_ev, b * PAGES + i)
                col = slice(c0[j], c0[j] + 384)
                for k in range(2):
                    pe.matmul(ps[:, j, 0:384], ct_hi[:, i % 2, k, :], uk[:, 0, k, col], start=(k == 0), stop=False)
                    pe.matmul(ps[:, j, 0:384], ct_hi[:, i % 2, k, :], uk[:, 1, k, col], start=False, stop=False)
                    mm = pe.matmul(ps[:, j, 0:384], ct_lo[:, i % 2, k, :], uk[:, 0, k, col], start=False,
                                   stop=(k == 1))
                mm.then_inc(kb_mm, 1)
            g = i // 4
            if i % 4 == 0 and (g >= 2 or par or not isinstance(b, int)):
                pe.wait_ge(g_s, b * 4 + g - 1)
            pe.matmul(ps[:, 5 + g % 2, (i % 4) * HQ:(i % 4 + 1) * HQ], krT[DN:DN + DR, i % 2, :],
                      qr_s[DN:DN + DR, par, :], start=True, stop=True).then_inc(b_mm, 1)

        def tail_pe(pe, b, par, i):
            if i == 3:
                pe.wait_ge(x_max, b + 1)
                pe.wait_ge(x_cev, b + 1)
                pe.transpose(ps[:, 7, 0:P], mx, ident).then_inc(x_mt, 1)
            if i == 5:
                pe.wait_ge(x_dg, b + 1)
                pe.matmul(ps[:, 7, P:2 * P], ones, dg, start=True, stop=True).then_inc(x_mb, 1)
            if 9 <= i <= 13:
                if i == 9:
                    pe.wait_ge(x_exp, b + 1)
                for k in range(4 * (i - 9), min(4 * (i - 9) + 4, SEQ_BLOCKS)):
                    n = P if k < PAGES else TN
                    rhs = cpg[:, par * PAGES + k, 0:KL + 1] if k < PAGES else cnat[:, :]
                    mm = pe.matmul(ps[:, 7, 0:KL + 1], s_all[par][0:n, k, :], rhs, start=(k == 0),
                                   stop=(k == SEQ_BLOCKS - 1))
                if i == 13:
                    mm.then_inc(x_ctx, 1)
            if i == 15:
                pe.wait_ge(x_cx, b + 1)
                for k in range(2):
                    mm = pe.transpose(ps[:, 7, k * P:(k + 1) * P], cx[:, k * P:(k + 1) * P], ident)
                mm.then_inc(x_ct, 1)

        def seq_pe(pe, b, par, tail, last):
            for i in range(PAGES):
                if i < PAGES - 1:
                    turn(pe, b, par, i + 1)
                elif not last:
                    turn(pe, b + 1, 1 - par, 0)
                page_products(pe, b, par, i)
                if tail:
                    tail_pe(pe, b - 1, 1 - par, i)

        def hi_act(act, b, par, i):
            act.wait_ge(t_ps, b * PAGES + i + 1)
            if i >= 2 or par or not isinstance(b, int):
                act.wait_ge(kb_mm, 3 * (b * PAGES + i - 1))
            act.copy(ct_hi[:, i % 2, :, :].rearrange("p a b -> p (a b)"), ps[:, 3 + i % 2, 0:KL]).then_inc(t_hi, 1)

        def group_act(act, b, g):
            act.wait_ge(sq_ok, b * PAGES + 4 * g + 4)
            v = ssq[:, g % 2, :]
            act.activation(v, v, ACT.Ln, bias=EPS, scale=1.0 / DN).then_inc(g_ln, 1)
            act.wait_ge(g_ln, b * 4 + g + 1)
            act.activation(v, v, ACT.Exp, scale=-0.5).then_inc(g_rs, 1)

        def query_act(act, b, par, first):
            if not first:
                act.wait_ge(kb_mm, 3 * PAGES * (b - 1))
            c0 = 768 if par else 1152
            act.copy(uk[:, 0, :, c0:c0 + P], f32(qabs[0][:, :, bass.ds(b, 1), :]).rearrange("p k a q -> p k (a q)"))\
               .then_inc(q_hi, 1)

        def query_dve(dve, b, par, first):
            if not first:
                dve.wait_ge(kb_mm, 3 * PAGES * (b - 1))
                dve.wait_ge(b_mm, PAGES * (b - 1))
                dve.wait_ge(x_ctx, b - 1)
            c0 = 768 if par else 1152
            dve.tensor_copy(uk[:, 1, :, c0:c0 + P], f32(qabs[1][:, :, bass.ds(b, 1), :]).rearrange("p k a q -> p k (a q)"))
            dve.tensor_copy(qr_s[DN:DN + DR, par, :], snew[DN:DN + DR, bass.ds(b, 1), :].rearrange("p a q -> p (a q)"))
            dve.tensor_copy(s_all[par][0:TN, PAGES, :], snew[0:TN, bass.ds(b, 1), :].rearrange("p a q -> p (a q)"))\
               .then_inc(q_lo, 1)

        def seq_act(act, b, par, tail, last):
            for i in range(PAGES):
                if i == 8 and not last:
                    query_act(act, b + 1, 1 - par, isinstance(b, int) and b == 0)
                if i < PAGES - 1:
                    hi_act(act, b, par, i + 1)
                elif not last:
                    hi_act(act, b + 1, 1 - par, 0)
                for j in range(3):
                    act.wait_ge(kb_mm, 3 * (b * PAGES + i) + j + 1)
                    if j == 0 and (i >= 2 or par or not isinstance(b, int)):
                        act.wait_ge(sq_ok, b * PAGES + i - 1)
                    if j < 2:
                        dst, src = sqk[:, i % 2, j * 384:(j + 1) * 384], ps[:, j, 0:384]
                    else:
                        dst, src = sqk[:, i % 2, 768:1024], ps[:, 2, P * par:P * par + 256]
                    act.activation(dst, src, ACT.Square).then_inc(kb_sq, 1)
                if i % 4 == 0 and (i or par or not isinstance(b, int)):
                    group_act(act, b if i else b - 1, i // 4 - 1 if i else 3)
                if tail and i == 7:
                    act.wait_ge(x_sub, b)
                    act.activation(s_all[1 - par].rearrange("p a b -> p (a b)"),
                                   s_all[1 - par].rearrange("p a b -> p (a b)"), ACT.Exp).then_inc(x_exp, 1)

        def lo_dve(dve, b, par, i):
            dve.wait_ge(t_hi, b * PAGES + i + 1)
            if i >= 2 or par or not isinstance(b, int):
                dve.wait_ge(b_mm, b * PAGES + i - 1)
            dve.tensor_copy(krT[DN:DN + DR, i % 2, :], ps[0:DR, 3 + i % 2, 2 * P:3 * P])
            dve.tensor_tensor(ct_lo[:, i % 2, :, :].rearrange("p a b -> p (a b)"), ps[:, 3 + i % 2, 0:KL],
                              f32(ct_hi[:, i % 2, :, :]).rearrange("p a b -> p (a b)"), ALU.subtract).then_inc(t_lo, 1)

        def group_dve(dve, b, par, g):
            n = b * 4 + g
            dve.wait_ge(g_rs, n + 1)
            dve.wait_ge(a_ev, b * PAGES + 4 * g + 4)
            dst = s_all[par][:, 4 * g:4 * g + 4, :].rearrange("p a (h t) -> p (a h) t", t=TS)
            dve.tensor_tensor(dst, a_sb[g % 2].rearrange("p a (h t) -> p (a h) t", t=TS),
                              ssq[:, g % 2, :].unsqueeze(2).to_broadcast([P, 4 * NH, TS]), ALU.mult).then_inc(g_s1, 1)
            dve.wait_ge(g_s1, n + 1)
            dve.wait_ge(b_mm, b * PAGES + 4 * g + 4)
            flat = s_all[par][:, 4 * g:4 * g + 4, :].rearrange("p a q -> p (a q)")
            dve.tensor_tensor(flat, flat, ps[:, 5 + g % 2, :], ALU.add).then_inc(g_s, 1)

        def tail_dve(dve, b, par, i):
            if i == 2:
                dve.wait_ge(g_s, 4 * b + 4)
                dve.wait_ge(q_lo, b + 1)
                dve.tensor_reduce(mx, s_all[par].rearrange("p k q -> p q k"), AX.X, ALU.max).then_inc(x_max, 1)
            if i == 4:
                dve.wait_ge(x_mt, b + 1)
                dve.tensor_reduce(cols[:, 12:13], ps[:, 7, 0:P], AX.X, ALU.max).then_inc(x_m, 1)
                dve.wait_ge(x_m, b + 1)
                dve.tensor_scalar(dg, ident, cols[:, 12:13], None, ALU.mult).then_inc(x_dg, 1)
            if i == 6:
                dve.wait_ge(x_mb, b + 1)
                dve.tensor_tensor(s_all[par], s_all[par],
                                  ps[:, 7, P:2 * P].unsqueeze(1).to_broadcast([P, SEQ_BLOCKS, HQ]), ALU.subtract)\
                   .then_inc(x_sub, 1)
            if i == 14:
                dve.wait_ge(x_ctx, b + 1)
                dve.reciprocal(cols[:, 13:14], ps[:, 7, KL:KL + 1]).then_inc(x_inv, 1)
                dve.wait_ge(x_inv, b + 1)
                dve.tensor_scalar(cx, ps[:, 7, 0:KL], cols[:, 13:14], None, ALU.mult).then_inc(x_cx, 1)
            if i == 15:
                dve.wait_ge(x_ct, b + 1)
                for k in range(2):
                    ins = dve.tensor_copy(ctxT[:, k, :, bass.ds(b * TS, TS)],
                                          ps[:, 7, k * P:(k + 1) * P].rearrange("p (h t) -> p h t", t=TS))
                ins.then_inc(x_cev, 1)

        def seq_dve(dve, b, par, tail, last):
            for i in range(PAGES):
                if i < PAGES - 1:
                    lo_dve(dve, b, par, i + 1)
                elif not last:
                    lo_dve(dve, b + 1, 1 - par, 0)
                n = b * PAGES + i
                q0 = 0 if par else 256
                dve.wait_ge(kb_sq, 3 * n + 3)
                dve.tensor_copy(a_sb[(i // 4) % 2][:, i % 4, :], ps[:, 2, q0:q0 + HQ]).then_inc(a_ev, 1)
                dve.tensor_reduce(ssq[:, (i // 4) % 2, (i % 4) * NH:(i % 4 + 1) * NH],
                                  sqk[:, i % 2, :].rearrange("p (h e) -> p h e", e=DN), AX.X, ALU.add)\
                   .then_inc(sq_ok, 1)
                if i % 4 == 1 and (i > 1 or par or not isinstance(b, int)):
                    if i == 1:
                        group_dve(dve, b - 1, 1 - par, 3)
                    else:
                        group_dve(dve, b, par, i // 4 - 1)
                if tail:
                    tail_dve(dve, b - 1, 1 - par, i)
                if i == 14 and not last:
                    query_dve(dve, b + 1, 1 - par, isinstance(b, int) and b == 0)

        LAST = NB - 1

        def sample_pe(pe):
            pe.wait_ge(p_oev, 8)
            pe.wait_ge(p_nev, 2)
            pe.wait_ge(s_init, 1)
            turn(pe, 0, 0, 0)
            seq_pe(pe, 0, 0, False, False)
            with pe.Fori(0, 3) as r:
                seq_pe(pe, r * 2 + 1, 1, True, False)
                seq_pe(pe, r * 2 + 2, 0, True, False)
            seq_pe(pe, LAST, 1, True, True)
            for i in range(PAGES):
                tail_pe(pe, LAST, 1, i)
            pe.wait_ge(s_uv, 32)
            pe.wait_ge(x_cev, NB + 1)
            for h in range(NH):
                r = slice(DV * (h % 2), DV * (h % 2) + DV)
                for k in range(2):
                    mm = pe.matmul(ps[r, 0, (h // 2) * TN:(h // 2 + 1) * TN], uv2[:, k, h * DV:(h + 1) * DV],
                                   ctxT[:, k, h, :], start=(k == 0), stop=(k == 1))
            mm.then_inc(o_mm, 1)

        uv2 = area(A_UK, 2, D)
        o_hi, o_lo = h_hi, h_lo
        o_mm, o_ev = sem("o_mm"), sem("o_ev")

        def sample_act(act):
            act.wait_ge(qa_lo, 4)
            query_act(act, 0, 0, True)
            hi_act(act, 0, 0, 0)
            seq_act(act, 0, 0, False, False)
            with act.Fori(0, 3) as r:
                seq_act(act, r * 2 + 1, 1, True, False)
                seq_act(act, r * 2 + 2, 0, True, False)
            seq_act(act, LAST, 1, True, True)
            group_act(act, LAST, 3)
            act.wait_ge(x_sub, NB)
            act.activation(s_all[1].rearrange("p a b -> p (a b)"), s_all[1].rearrange("p a b -> p (a b)"),
                           ACT.Exp).then_inc(x_exp, 1)
            split_hi(act, WO0)
            act.wait_ge(x_cev, NB + 1)
            for c in range(DC):
                if c == 0:
                    act.wait_ge(o_ev, 1)
                act.copy(o_hi[:, c, :], oT[:, c, :]).then_inc(d_hi, 1)

        def sample_dve(dve):
            dve.wait_ge(p_tev, UNITS)
            dve.wait_ge(p_o, NH)
            dve.memset(s_all[0][TN:P, PAGES, :], NEG).then_inc(x_cev, 1)
            dve.memset(s_all[1][TN:P, PAGES, :], NEG)
            dve.memset(cpg[:, :, KL:KL + 1], 1.0).then_inc(s_init, 1)
            query_dve(dve, 0, 0, True)
            lo_dve(dve, 0, 0, 0)
            seq_dve(dve, 0, 0, False, False)
            with dve.Fori(0, 3) as r:
                seq_dve(dve, r * 2 + 1, 1, True, False)
                seq_dve(dve, r * 2 + 2, 0, True, False)
            seq_dve(dve, LAST, 1, True, True)
            group_dve(dve, LAST, 1, 3)
            for i in range(PAGES):
                tail_dve(dve, LAST, 1, i)
            dve.wait_ge(o_mm, 1)
            dve.tensor_copy(oT[:, :, TP:T], ps[:, 0, :].rearrange("p (c t) -> p c t", c=DC)).then_inc(o_ev, 1)
            for c in range(DC):
                dve.wait_ge(d_hi, c + 7)
                if c >= DC - 2:
                    dve.wait_ge(d_lo, c + 1)
                dve.tensor_tensor(o_lo[:, c, :], oT[:, c, :], f32(o_hi[:, c, :]), ALU.subtract).then_inc(d_lo, 1)

        def sample_sp(sp):
            sp.wait_ge(s_pt, 16)
            sp.wait_ge(s_init, 1)
            for b in range(2):
                for i in range(PAGES):
                    page_load(sp, b, b % 2, i, False)
            with sp.Fori(0, 3) as r:
                for par in range(2):
                    for i in range(PAGES):
                        page_load(sp, r * 2 + 2 + par, par, i, True)
            sp.wait_ge(kb_mm, 3 * PAGES * NB)
            sp.dma_start(uv2, I["attn_w_uv"][0].rearrange("(k p) h d -> p k (h d)", p=P)).then_inc(s_uv, 16)

        def proj_src(name):
            w = I[name][0].rearrange("(k p) n -> p k n", p=P)
            return lambda d: w[:, :, d * P:(d + 1) * P]

        def proj_act(act, t0, i, split):
            for d in range(DC):
                if t0 + d + 1 > split:
                    split_hi(act, t0 + d + 1)
                x_added(act, t0 + d)
                norm_chunk_act(act, i, d)

        def proj_dve(dve, t0, i):
            for d in range(DC):
                add_x(dve, t0 + d, d)
                x_added(dve, t0 + d)
                norm_chunk_dve(dve, i, d)

        def proj_pool(pool, t0, i):
            for d in range(DC):
                split_lo(pool, t0 + d + 1)
                norm_add(pool, i, d)

        def attention_out_pe(pe):
            for d in range(DC):
                tile_product(pe, WO0 + d, WO0 + d + 6, o_hi, o_lo,
                             ready=(lambda k: pe.wait_ge(d_lo, k + 7)) if d == 0 else None).then_inc(w_used, 1)

        def rec_out_pe(pe):
            for part in (range(DC - 1), range(DC - 1, DC)):
                for d in range(2):
                    mm = tile_product(pe, OUT0 + d, OUT0 + d + 6, h_hi, h_lo, part=part,
                                      ready=(lambda k: pe.wait_ge(r_yl, k + 1)) if d == 0 else None)
                    if part[0]:
                        mm.then_inc(w_used, 1)
            states_pe(pe)
            for d in range(2, DC):
                tile_product(pe, OUT0 + d, OUT0 + d + 6, h_hi, h_lo).then_inc(w_used, 1)

        fnat = area(AP_, FF)
        frow = area(AP_, FF)
        FT = (FW - 1) * (1 + NB)
        ftail = snew[:].rearrange("p a b -> p (a b)")[:, 0:2 * FC * FT].rearrange("p (f t) -> p f t", f=FC)
        GB = TP + FW - 1
        gb = area(R1, 2, GB + NB * (FW - 1 + TS))
        CBN = GB + NB * (FW - 1 + TS) - (FW - 1)
        cb = area(R1 + 2 * 594, 2, CBN + FW - 1)
        hf = area(R1 + 4 * 594, 2, T)
        fpar = sb("fpar", [P, FC, F_ALL])
        SG = FW - 1 + TS
        S = {k: sem(f"f_{k}") for k in ("nat", "par", "parev", "conv", "silu", "h", "ch", "tail", "tailev", "store")}

        def gate_out(dve, pr_, buf, pad, w):
            dve.tensor_tensor(buf[:, pad:pad + HT], ps[:, 2 * pr_, 0:HT], rs[0][:, 0:HT], ALU.mult)
            dve.tensor_tensor(buf[:, pad + HT:pad + TP], ps[:, 2 * pr_ + 1, 0:TP - HT], rs[0][:, HT:TP], ALU.mult)
            dst = buf[:, TP + pad:TP + pad + NB * w].rearrange("p (b t) -> p b t", t=w)[:, :, pad:pad + TS]
            return dve.tensor_tensor(dst, ps[:, 2 * pr_ + 1, TP - HT:HT].rearrange("p (b t) -> p b t", t=TS),
                                     rs[0][:, TP:T].rearrange("p (b t) -> p b t", t=TS), ALU.mult)

        def ffn_load(sp, l, t0):
            for row, src in ((F_ST, I["state_ffn_conv"][l].rearrange("b w d -> (b w) d")),
                             (F_CW, I["ffn_conv_w"][l]), (F_CB, I["ffn_conv_b"][l:l + 1, :])):
                sp.dma_start(fnat[row:row + src.shape[0], :], src).then_inc(S["nat"], 16)
            up = I["ffn_w_up"][l].rearrange("(k p) n -> p k n", p=P)
            dn = I["ffn_w_down"][l].rearrange("(s k p) n -> s p k n", p=P, k=TF)
            with sp.Fori(0, THIRDS) as s:
                with sp.Fori(0, 4) as r:
                    for j in range(4):
                        col = (s * TF + r * 2 + j // 2) * P + (j % 2) * FF
                        load_tile(sp, t0 + j, up[:, :, bass.ds(col, P)], s * 6 + r)
                with sp.Fori(0, 2) as r:
                    for j in range(4):
                        src = dn[bass.ds(s, 1), :, :, bass.ds(r * 512 + j * P, P)]
                        load_tile(sp, t0 + 16 + j, src.rearrange("a p k n -> p (a k) n"), s * 6 + r)

        def ffn_pe(pe, l, t0, i):

            def up(s, r, first):
                for j in range(2):
                    t = t0 + 2 * j
                    it = s * 6 + r
                    tile_product(pe, t, t + 6, xn_hi, xn_lo, it,
                                 ready=norm_ready(pe, i) if first and j == 0 else None).then_inc(w_used, 1)
                    if first and j == 0:
                        norm_sum(pe, i)
                        pe.wait_ge(S["nat"], 48 * l + 48)
                        for c in range(FC):
                            mm = pe.transpose(ps[:, 4, c * F_ALL:(c + 1) * F_ALL],
                                              fnat[0:F_ALL, c * P:(c + 1) * P], ident[0:F_ALL, 0:F_ALL])
                        mm.then_inc(S["par"], 1)
                    tile_product(pe, t + 1, t + 7, xn_hi, xn_lo, it).then_inc(w_used, 1)

            def down(s, r, j):
                t = t0 + 16 + j
                tile_product(pe, t, t + 6, h_hi, h_lo, s * 6 + r,
                             ready=(lambda k: pe.wait_ge(S["h"], l * FC + s * TF + k + 1)) if j == 0 else None)\
                    .then_inc(w_used, 1)

            up(0, 0, True)
            with pe.Fori(1, 4) as r:
                up(0, r, False)
            with pe.Fori(0, 2) as r:
                for j in range(4):
                    down(0, r, j)
            with pe.Fori(0, 4) as r:
                up(1, r, False)
            with pe.Fori(0, 2) as r:
                for j in range(4):
                    down(1, r, j)
            with pe.Fori(0, 4) as r:
                up(2, r, False)
            for d in range(DC):
                down(2, d // 4, d % 4)
                if l == 1 and d in (1, 4):
                    tails_pe(pe, d == 4)

        def ffn_act(act, l, t0, i, nxt):

            def up(s, r, first):
                for j in range(2):
                    t, it = t0 + 2 * j, s * 6 + r
                    f = l * FC + s * TF + r * 2 + j
                    split_hi(act, t + 1, it)
                    if first and j == 0:
                        norm_root(act, i)
                    split_hi(act, t + 2, it)
                    act.wait_ge(S["conv"], f + 3)
                    act.activation(cb[:, j, 0:CBN], cb[:, j, 0:CBN], ACT.Silu).then_inc(S["silu"], 1)

            def down(s, r):
                for j in range(4):
                    split_hi(act, t0 + 17 + j, s * 6 + r)

            up(0, 0, True)
            with act.Fori(1, 4) as r:
                up(0, r, False)
            with act.Fori(0, 2) as r:
                down(0, r)
            with act.Fori(0, 4) as r:
                up(1, r, False)
            with act.Fori(0, 2) as r:
                down(1, r)
            with act.Fori(0, 4) as r:
                up(2, r, False)
            for d in range(DC):
                t, it = t0 + 16 + d % 4, (THIRDS - 1) * 6 + d // 4
                if t + 1 + 4 * it < TILES:
                    split_hi(act, t + 1, it)
                if nxt is not None:
                    x_added(act, t, it)
                    norm_chunk_act(act, nxt, d)
                elif d in (2, 5):
                    tails_act(act, d == 5)

        def ffn_pool(pool, t0, nxt):
            n = THIRDS * 6
            with pool.Fori(0, n - 2) as r:
                for j in range(4):
                    split_lo(pool, t0 + 1 + j, r)
            for d in range(DC):
                if nxt is not None or d < DC - 1:
                    split_lo(pool, t0 + 1 + d % 4, n - 2 + d // 4)
                if nxt is not None:
                    norm_add(pool, nxt, d)

        def ffn_dve(dve, l, t0, nxt):
            pad = dve.memset(gb[:, :, 0:FW - 1], 0.0)
            if l == 0:
                pad.then_inc(S["conv"], 2)
            dve.wait_ge(S["par"], l + 1)
            dve.tensor_copy(fpar[:].rearrange("p a b -> p (a b)"), ps[:, 4, 0:FC * F_ALL]).then_inc(S["parev"], 1)
            dve.wait_ge(S["parev"], l + 1)

            def up(s, r):
                for j in range(2):
                    t, it = t0 + 2 * j, s * 6 + r
                    f = s * TF + r * 2 + j
                    F = l * FC + f
                    ch = Chain(dve, S["ch"], F * 5)
                    par = fpar[:, bass.ds(f, 1), :].rearrange("p a b -> p (a b)")
                    dve.wait_ge(S["conv"], F + 1)
                    ch(dve.tensor_copy(gb_pad(j), par[:, F_ST:F_ST + 16].rearrange("p (b w) -> p b w", b=NB)))
                    dve.wait_ge(w_used, t + 1 + 4 * it)
                    gate_out(dve, t % 2, gb[:, j, :], FW - 1, SG).then_inc(acc_free[t % 2], 1)
                    dve.wait_ge(acc_free[t % 2], (t + 6) // 2 + 1 + 2 * it)
                    last = ftail[:, bass.ds(f, 1), l * FT:(l + 1) * FT].rearrange("p a b -> p (a b)")
                    dve.tensor_copy(last[:, 0:FW - 1], gb[:, j, TP:GB])
                    dve.tensor_copy(last[:, FW - 1:FT].rearrange("p (w b) -> p b w", b=NB),
                                    gb[:, j, GB:GB + NB * SG].rearrange("p (b t) -> p b t", t=SG)[:, :, TS:SG])
                    ch(dve.tensor_scalar(cb[:, j, 0:CBN], gb[:, j, 0:CBN], par[:, F_CW:F_CW + 1], par[:, F_CB:F_CB + 1],
                                         ALU.mult, ALU.add))
                    ch(dve.scalar_tensor_tensor(out=cb[:, j, 0:CBN], in0=gb[:, j, 1:1 + CBN],
                                                scalar=par[:, F_CW + 1:F_CW + 2], in1=cb[:, j, 0:CBN],
                                                op0=ALU.mult, op1=ALU.add))
                    dve.scalar_tensor_tensor(out=cb[:, j, 0:CBN], in0=gb[:, j, 2:2 + CBN],
                                             scalar=par[:, F_CW + 2:F_CW + 3], in1=cb[:, j, 0:CBN],
                                             op0=ALU.mult, op1=ALU.add).then_inc(S["conv"], 1)
                    dve.wait_ge(S["silu"], F + 1)
                    dve.wait_ge(w_used, t + 2 + 4 * it)
                    q = (t + 1) % 2
                    dve.tensor_tensor(hf[:, j, 0:HT], cb[:, j, 0:HT], ps[:, 2 * q, 0:HT], ALU.mult)
                    dve.tensor_tensor(hf[:, j, HT:TP], cb[:, j, HT:TP], ps[:, 2 * q + 1, 0:TP - HT], ALU.mult)
                    dve.tensor_tensor(hf[:, j, TP:T].rearrange("p (b t) -> p b t", t=TS),
                                      cb_new(j), ps[:, 2 * q + 1, TP - HT:HT].rearrange("p (b t) -> p b t", t=TS),
                                      ALU.mult).then_inc(acc_free[q], 1)
                    dve.wait_ge(acc_free[q], (t + 7) // 2 + 1 + 2 * it)
                    ch(dve.tensor_tensor(hf[:, j, :], hf[:, j, :], rs[0], ALU.mult))
                    hh = h_hi[:, bass.ds(r * 2 + j, 1), :].rearrange("p a b -> p (a b)")
                    hl = h_lo[:, bass.ds(r * 2 + j, 1), :].rearrange("p a b -> p (a b)")
                    ch(dve.tensor_copy(hh, hf[:, j, :]))
                    dve.tensor_tensor(hl, hf[:, j, :], f32(hh), ALU.subtract).then_inc(S["h"], 1)

            dve.wait_ge(n_rs, 2 * l + 2)
            with dve.Fori(0, THIRDS - 1) as s:
                with dve.Fori(0, 4) as r:
                    up(s, r)
                with dve.Fori(0, 2) as r:
                    for j in range(4):
                        add_x(dve, t0 + 16 + j, r * 4 + j, s * 6 + r)
            with dve.Fori(0, 4) as r:
                up(THIRDS - 1, r)
            for d in range(DC):
                t, it = t0 + 16 + d % 4, (THIRDS - 1) * 6 + d // 4
                add_x(dve, t, d, it)
                if nxt is not None:
                    x_added(dve, t, it)
                    norm_chunk_dve(dve, nxt, d)

        def gb_pad(j):
            return gb[:, j, TP + FW - 1:TP + FW - 1 + NB * SG].rearrange("p (b t) -> p b t", t=SG)[:, :, 0:FW - 1]

        def cb_new(j):
            return cb[:, j, GB:GB + NB * SG].rearrange("p (b t) -> p b t", t=SG)[:, :, 0:TS]

        def tails_pe(pe, second):
            if second:
                pe.wait_ge(S["tailev"], 4)
            else:
                pe.wait_ge(S["conv"], 2 + 2 * FC)
            for c in range(16, FC) if second else range(16):
                mm = pe.transpose(ps[0:2 * FT, 4 + c % 16 // 4, c % 4 * P:(c % 4 + 1) * P], ftail[:, c, :], ident)
                if c % 4 == 3:
                    mm.then_inc(S["tail"], 1)

        def tails_act(act, second):
            for c in range(4, FC // 4) if second else range(4):
                act.wait_ge(S["tail"], c + 1)
                act.copy(frow[0:2 * FT, c * 512:(c + 1) * 512], ps[0:2 * FT, 4 + c % 4, :]).then_inc(S["tailev"], 1)

        def ffn_store(sp):
            sp.wait_ge(S["tailev"], FC // 4)
            for l in range(2):
                r = l * FT
                sp.dma_start(O["ffn_conv_prompt"][l, 0], frow[r:r + FW - 1, :]).then_inc(S["store"], 16)
                for w in range(FW - 1):
                    q = r + FW - 1 + w * NB
                    sp.dma_start(O["ffn_conv_sample"][l, :, w, :], frow[q:q + NB, :]).then_inc(S["store"], 16)

        XP = RW - 1
        XW = TP + XP
        XS = XP + TS
        XB = XW + NB * XS
        XC = XB - XP
        xrb = area(R1, 2, XB)
        xcv = area(R1 + 2 * XB, 2, XB)
        o_ = R1 + (4 * XB + 7) // 8 * 8
        xch = area(o_, 2, T, dt=F32R)
        xcl = area(o_ + 2 * T, 2, T, dt=F32R)
        ri = area(o_ + 4 * T, T)
        gl = area(o_ + 5 * T, 2, T)
        ra, th, aa, mm_ = sq[0], sq[1], rs[1], rs[2]
        HL = (1 + NB) * (1 + XP)
        hl = area(A_P, DC, HL)
        gw = area(A_P + 1024, 2, 2, NB, P, dt=F32R)
        gw_raw = area(A_P + 5120, 2, D)
        hn = area(A_P + 5120, D)
        yh = area(A_P + 6144, T)
        spc = sb("spc", [P, 8, DC])
        c_abs, c_exp, c_ok = sem("c_abs"), sem("c_exp"), sem("c_ok")
        s_gw = sem("s_gw")
        r_conv, r_hi, r_lo, r_ga, r_gi, r_ta, r_ti, r_a, r_m, r_y, r_ge, r_yh, r_yl = (
            sem("r_conv"), sem("r_hi"), sem("r_lo"), sem("r_ga"), sem("r_gi"), sem("r_ta"), sem("r_ti"),
            sem("r_a"), sem("r_m"), sem("r_y"), sem("r_ge"), sem("r_yh"),
            sem("r_yl"))

        def lam(row):
            return rpar[:, :, row:row + 1].rearrange("p c a -> p (c a)")

        def decay_act(act):
            act.wait_ge(rp_ev, 1)
            act.activation(spc[:, 0, :], lam(R_LAM), ACT.Abs).then_inc(c_abs, 1)
            act.wait_ge(c_abs, 1)
            act.activation(spc[:, 1, :], spc[:, 0, :], ACT.Exp, scale=-1.0).then_inc(c_exp, 1)

        def decay_dve(dve, ch):
            e, z, z2, q = spc[:, 1, :], spc[:, 2, :], spc[:, 3, :], spc[:, 4, :]
            dve.wait_ge(c_exp, 1)
            ch(dve.tensor_scalar(z2, e, 2.0, None, ALU.add))
            ch(dve.reciprocal(q, z2))
            ch(dve.tensor_tensor(z, e, q, ALU.mult))
            ch(dve.tensor_tensor(z2, z, z, ALU.mult))
            ch(dve.tensor_scalar(q, z2, 1.0 / 19, None, ALU.mult))
            for k in range(17, 1, -2):
                ch(dve.scalar_tensor_tensor(out=q, in0=q, scalar=1.0 / k, in1=z2, op0=ALU.add, op1=ALU.mult))
            ch(dve.tensor_scalar(q, q, 1.0, 2.0, ALU.add, ALU.mult))
            ch(dve.tensor_tensor(q, q, z, ALU.mult))
            ch(dve.tensor_scalar(z, lam(R_LAM), -1.0, 0.0, ALU.mult, ALU.max))
            ch(dve.tensor_tensor(z, z, q, ALU.add))
            ch(dve.tensor_scalar(spc[:, 5, :], z, -4.0, None, ALU.mult))
            ch(dve.tensor_scalar(spc[:, 6, :], lam(R_BA), 0.5, None, ALU.mult))
            dve.tensor_scalar(spc[:, 7, :], lam(R_BI), 0.5, None, ALU.mult).then_inc(c_ok, 1)

        def xr_t(n):
            return REC0 + (2 * n - 1 if n else 0)

        def gb_t(n):
            return REC0 + (2 * n + 2 if n < DC - 1 else 2 * n + 1)

        def prompt_new(v, off):
            return v[:, 0:TP], v[:, XW:XB].rearrange("p (b t) -> p b t", t=XS)[:, :, off:off + TS]

        def rec_load(sp):
            w = I["rec_w_in"][0].rearrange("(k p) n -> p k n", p=P)
            for t in range(REC0, OUT0):
                for n in range(DC):
                    if t in (xr_t(n), gb_t(n)):
                        col = n * P + (D if t == gb_t(n) else 0)
                load_tile(sp, t, w[:, :, col:col + P])
                if t == REC0 + 1:
                    for g, name in enumerate(("rec_w_a", "rec_w_i")):
                        sp.dma_start(gw_raw[:, g, :].rearrange("p (n d) -> p n d", n=NB),
                                     I[name][0].rearrange("n c d -> c n d")).then_inc(s_gw, 16)

        def rec_gates(pe, n):
            pe.wait_ge(r_lo, n + 1)
            if n == 0:
                pe.wait_ge(res_l, 6)
            for g, (bank, free) in enumerate(((4, r_ta), (6, r_ti))):
                if n >= 1:
                    pe.wait_ge(free, n)
                out = [ps[:, bank, 0:HT], ps[:, bank + 1, 0:HT]]
                product(pe, out, gw[:, g, 0, n, :], gw[:, g, 1, n, :], halves(xch[:, n % 2, :]),
                        halves(xcl[:, n % 2, :]), True, True).then_inc((r_ga, r_gi)[g], 1)

        def rec_pe(pe):
            for n in range(DC + 1):
                if n < DC:
                    t = xr_t(n)
                    tile_product(pe, t, t + 6, xn_hi, xn_lo, ready=norm_ready(pe, 2) if n == 0 else None)\
                        .then_inc(w_used, 1)
                if n == 0:
                    norm_sum(pe, 2)
                    continue
                if n == 1:
                    pe.wait_ge(n_ln, 3)
                rec_gates(pe, n - 1)
                t = gb_t(n - 1)
                tile_product(pe, t, t + 6, xn_hi, xn_lo).then_inc(w_used, 1)

        def rec_finish_act(act, n):
            if n < DC - 1:
                split_hi(act, gb_t(n) + 1)
            act.wait_ge(r_ga, n + 1)
            if n:
                act.wait_ge(r_y, n)
            act.activation(two(ra), pair(2), ACT.Tanh, bias=spc[:, 6, n:n + 1], scale=0.5).then_inc(r_ta, 1)
            act.wait_ge(r_gi, n + 1)
            act.activation(two(ri), pair(3), ACT.Tanh, bias=spc[:, 7, n:n + 1], scale=0.5).then_inc(r_ti, 1)
            act.wait_ge(r_ta, n + 1)
            act.activation(aa, ra, ACT.Exp, bias=spc[:, 5, n:n + 1], scale=spc[:, 5, n:n + 1]).then_inc(r_a, 1)
            act.activation(th, ra, ACT.Tanh, bias=spc[:, 5, n:n + 1], scale=spc[:, 5, n:n + 1])
            act.wait_ge(r_a, 3 * n + 1)
            act.activation(mm_, aa, ACT.Square).then_inc(r_a, 1)
            split_hi(act, gb_t(n) + 2)
            act.wait_ge(r_m, n + 1)
            act.activation(mm_, mm_, ACT.Sqrt, scale=-1.0).then_inc(r_a, 1)

        def rec_high(act, n):
            act.wait_ge(r_y, n + 1)
            act.copy(h_hi[:, n, :], yh).then_inc(r_yh, 1)

        def rec_low(dve, n):
            dve.wait_ge(r_yh, n + 1)
            dve.tensor_tensor(h_lo[:, n, :], yh, f32(h_hi[:, n, :]), ALU.subtract).then_inc(r_yl, 1)

        def rec_act(act):
            act.wait_ge(s_gw, 32)
            for g in range(2):
                act.copy(gw[:, g, 0, :, :].rearrange("p a b -> p (a b)"), gw_raw[:, g, :]).then_inc(res_h, 1)
            for n in range(DC + 1):
                if n < 2:
                    split_hi(act, xr_t(n) + 1)
                if n < DC:
                    if n == 0:
                        norm_root(act, 2)
                    act.wait_ge(r_conv, n + 1)
                    src, dst = prompt_new(xcv[:, n % 2, :], 0), xch[:, n % 2, :]
                    act.copy(dst[:, 0:TP], src[0])
                    act.copy(dst[:, TP:T].rearrange("p (b t) -> p b t", t=TS), src[1]).then_inc(r_hi, 1)
                if n >= 2:
                    rec_high(act, n - 2)
                if n:
                    rec_finish_act(act, n - 1)
                    t = gb_t(n - 1)
                    act.wait_ge(acc_free[t % 2], (t + 6) // 2 + 1)
                    act.activation(gl[:, (n - 1) % 2, :], gl[:, (n - 1) % 2, :], ACT.Gelu_apprx_tanh)\
                       .then_inc(r_ge, 1)
            rec_high(act, DC - 1)

        def rec_finish_dve(dve, n, ch):
            dve.wait_ge(r_ti, n + 1)
            xp_, xs_ = prompt_new(xcv[:, n % 2, :], 0)
            new = lambda v: v[:, TP:T].rearrange("p (b t) -> p b t", t=TS)
            dve.scalar_tensor_tensor(out=ri[:, 0:TP], in0=ri[:, 0:TP], scalar=1.0, in1=xp_, op0=ALU.add, op1=ALU.mult)
            ch(dve.scalar_tensor_tensor(out=new(ri), in0=new(ri), scalar=1.0, in1=xs_, op0=ALU.add, op1=ALU.mult))
            dve.wait_ge(r_a, 3 * n + 2)
            dve.scalar_tensor_tensor(out=mm_, in0=mm_, scalar=1.0, in1=th, op0=ALU.add, op1=ALU.mult).then_inc(r_m, 1)
            t = gb_t(n)
            dve.wait_ge(w_used, t + 1)
            dve.tensor_tensor(two(gl[:, n % 2, :]), pair(t % 2), two(rs[0]), ALU.mult).then_inc(acc_free[t % 2], 1)
            dve.wait_ge(r_a, 3 * n + 3)
            ch(dve.scalar_tensor_tensor(out=ri, in0=ri, scalar=0.5, in1=mm_, op0=ALU.mult, op1=ALU.mult))
            a0, b0 = new(aa)[:, :, 0:1], new(ri)[:, :, 0:1]
            h0 = rpar[:, n, R_H:R_H + NB].unsqueeze(2)
            ch(dve.tensor_tensor(cols[:, 16:24].unsqueeze(2), a0, h0, ALU.mult))
            ch(dve.tensor_tensor(b0, b0, cols[:, 16:24].unsqueeze(2), ALU.add))
            ch(dve.memset(a0, 0.0))
            ch(dve.tensor_tensor_scan(mm_, aa, ri, 0.0, ALU.mult, ALU.add))
            dve.tensor_copy(hl[:, n, 0:1], mm_[:, TP - 1:TP])
            dve.tensor_copy(hl[:, n, 1:1 + NB].unsqueeze(2), new(mm_)[:, :, TS - 1:TS])
            dve.wait_ge(r_ge, n + 1)
            dve.tensor_tensor(yh, mm_, gl[:, n % 2, :], ALU.mult).then_inc(r_y, 1)

        def rec_dve(dve, ch):
            dve.memset(xrb[:, :, 0:XP], 0.0)
            for n in range(DC):
                t = xr_t(n)
                buf, out = xrb[:, n % 2, :], xcv[:, n % 2, 0:XC]
                if n == 0:
                    dve.wait_ge(n_rs, 3)
                ch(dve.tensor_copy(buf[:, XW:XB].rearrange("p (b t) -> p b t", t=XS)[:, :, 0:XP],
                                   rpar[:, n, R_CS:R_CS + NB * XP].rearrange("p (b w) -> p b w", b=NB)))
                dve.wait_ge(w_used, t + 1)
                gate_out(dve, t % 2, buf, XP, XS).then_inc(acc_free[t % 2], 1)
                dve.wait_ge(acc_free[t % 2], (t + 6) // 2 + 1)
                dve.tensor_copy(hl[:, n, 1 + NB:1 + NB + XP], buf[:, TP:XW])
                dve.tensor_copy(hl[:, n, 1 + NB + XP:HL].rearrange("p (w b) -> p b w", b=NB),
                                buf[:, XW:XB].rearrange("p (b t) -> p b t", t=XS)[:, :, TS:XS])
                ch(dve.tensor_scalar(out, buf[:, 0:XC], rpar[:, n, R_CW:R_CW + 1], rpar[:, n, R_CB:R_CB + 1],
                                     ALU.mult, ALU.add))
                for k in range(1, RW):
                    ins = dve.scalar_tensor_tensor(out=out, in0=buf[:, k:k + XC],
                                                   scalar=rpar[:, n, R_CW + k:R_CW + k + 1], in1=out,
                                                   op0=ALU.mult, op1=ALU.add)
                    if k < RW - 1:
                        ch(ins)
                ins.then_inc(r_conv, 1)
                dve.wait_ge(r_hi, n + 1)
                src, hi, lo = prompt_new(xcv[:, n % 2, :], 0), f32(xch[:, n % 2, :]), xcl[:, n % 2, :]
                dve.tensor_tensor(lo[:, 0:TP], src[0], hi[:, 0:TP], ALU.subtract)
                new = lambda v: v[:, TP:T].rearrange("p (b t) -> p b t", t=TS)
                dve.tensor_tensor(new(lo), src[1], new(hi), ALU.subtract).then_inc(r_lo, 1)
                if n >= 2:
                    rec_low(dve, n - 2)
                if n:
                    rec_finish_dve(dve, n - 1, ch)
            rec_low(dve, DC - 2)
            rec_finish_dve(dve, DC - 1, ch)
            rec_low(dve, DC - 1)

        def gw_pool(pool):
            for g in range(2):
                pool.wait_ge(res_h, g + 5)
                pool.tensor_tensor(gw[:, g, 1, :, :].rearrange("p a b -> p (a b)"), gw_raw[:, g, :],
                                   f32(gw[:, g, 0, :, :]).rearrange("p a b -> p (a b)"), ALU.subtract)\
                    .then_inc(res_l, 1)

        def states_pe(pe):
            for c in range(DC):
                mm = pe.transpose(ps[0:HL, 4 + c // 4, (c % 4) * P:(c % 4 + 1) * P], hl[:, c, :], ident)
            mm.then_inc(rp_ps, 1)

        def states_dve(dve):
            dve.wait_ge(rp_ps, 2)
            dve.tensor_copy(hn[0:HL, :].rearrange("p (a b) -> p a b", a=2), ps[0:HL, 4:6, :]).then_inc(rp_ev, 1)

        def rec_store(sp):
            sp.wait_ge(rp_ev, 2)
            sp.dma_start(O["lru_h_prompt"][0], hn[0:1, :]).then_inc(s_onat, 16)
            sp.dma_start(O["lru_h_sample"][0], hn[1:1 + NB, :]).then_inc(s_onat, 16)
            sp.dma_start(O["lru_conv_prompt"][0, 0], hn[1 + NB:1 + NB + XP, :]).then_inc(s_onat, 16)
            for w in range(XP):
                row = 1 + NB + XP + w * NB
                sp.dma_start(O["lru_conv_sample"][0, :, w, :], hn[row:row + NB, :]).then_inc(s_onat, 16)

        yn = area(R1, 2, D)
        s_y = [sem("s_y0"), sem("s_y1")]

        def out_pe(pe):
            last = TILES + 5
            pe.wait_ge(acc_free[last % 2], last // 2 + 1)
            pe.wait_ge(acc_free[1 - last % 2], (last - 1) // 2 + 1)
            for i in range(5):
                n = P if i < 4 else TN
                b = 2 * (i % 2)
                if i >= 2:
                    pe.wait_ge(xt_ev, DC + i - 1)
                for c in range(DC):
                    mm = pe.transpose(ps[0:n, b + c // 4, (c % 4) * P:(c % 4 + 1) * P], xT[:, c, i * P:i * P + n], ident)
                mm.then_inc(xt_ps, 1)

        def out_dve(dve):
            for i in range(5):
                n = P if i < 4 else TN
                b = 2 * (i % 2)
                dve.wait_ge(xt_ps, DC + i + 1)
                if i >= 2:
                    dve.wait_ge(s_y[i % 2], 16 * (i // 2))
                dve.tensor_copy(yn[0:n, i % 2, :].rearrange("p (a b) -> p a b", a=2), ps[0:n, b:b + 2, :])\
                   .then_inc(xt_ev, 1)

        def out_store(sp):
            for i in range(5):
                n = P if i < 4 else TN
                sp.wait_ge(xt_ev, DC + i + 1)
                dst = O["y_prompt"][0, i * P:(i + 1) * P, :] if i < 4 else O["y_sample"].rearrange("b t d -> (b t) d")
                sp.dma_start(dst, yn[0:n, i % 2, :]).then_inc(s_y[i % 2], 16)

        @block.sync
        def _(sp):
            load_inputs(sp)
            for t in range(4):
                load_tile(sp, t, down_src(t))
            load_gains(sp)
            for t in range(4, UQ0):
                load_tile(sp, t, down_src(t))
            for t in range(UQ0, UQ0 + 3):
                load_uq(sp, t)
            sp.wait_ge(kr_ok, 1)
            sp.dma_start(uk_raw, I["attn_w_uk"][0].rearrange("(k p) h d -> p k (h d)", p=P)).then_inc(s_uk, 16)
            sp.wait_ge(d_lo, 6)
            sp.dma_start(uv_raw, I["attn_w_uv"][0].rearrange("(k p) h d -> p k (h d)", p=P)).then_inc(s_uv, 16)
            for t in range(UQ0 + 3, WO0):
                load_uq(sp, t)
            down_store(sp)
            wo = proj_src("attn_w_o")
            for d in range(4):
                load_tile(sp, WO0 + d, wo(d))
            sample_sp(sp)
            for d in range(4, DC):
                load_tile(sp, WO0 + d, wo(d))
            sp.wait_ge(x_ctx, NB)
            ffn_load(sp, 0, FFN0)
            rec_load(sp)
            out = proj_src("rec_w_out")
            for d in range(DC):
                load_tile(sp, OUT0 + d, out(d))
                if d == 3:
                    rec_store(sp)
            sp.wait_ge(s_onat, 160)
            ffn_load(sp, 1, FFN1)
            ffn_store(sp)
            out_store(sp)
            sp.wait_ge(S["store"], 96)
            sp.wait_ge(s_y[0], 48)
            sp.wait_ge(s_y[1], 32)

        @block.gpsimd
        def _(pool):
            split_lo(pool, 0)
            for c in range(DC):
                norm_add(pool, 0, c)
            for t in range(1, WO0):
                split_lo(pool, t)
            uk_pool(pool)
            uv_pool(pool)
            split_lo(pool, WO0)
            proj_pool(pool, WO0, 1)
            ffn_pool(pool, FFN0, 2)
            gw_pool(pool)
            for t in range(REC0 + 1, OUT0 + 1):
                split_lo(pool, t)
            proj_pool(pool, OUT0, 3)
            ffn_pool(pool, FFN1, None)

        @block.scalar
        def _(act):
            act.preload_act_table_set("natural_log_exp_and_others")
            split_hi(act, 0)
            act.wait_ge(rp_ev, 1)
            for c in range(DC):
                act.wait_ge(xt_ev, c + 1)
                norm_chunk_act(act, 0, c)
            down_act(act)
            decay_act(act)
            uq_act(act)
            values_act(act)
            prompt_act(act)
            sample_act(act)
            proj_act(act, WO0, 1, WO0)
            ffn_act(act, 0, FFN0, 1, 2)
            rec_act(act)
            proj_act(act, OUT0, 3, OUT0 + 1)
            ffn_act(act, 1, FFN1, 3, None)

        @block.vector
        def _(dve):
            ch = Chain(dve, d_ch)
            keep_inputs(dve)
            down_dve(dve, ch)
            uq_dve(dve)
            values_dve(dve)
            prompt_dve(dve)
            sample_dve(dve)
            proj_dve(dve, WO0, 1)
            decay_dve(dve, ch)
            ffn_dve(dve, 0, FFN0, 2)
            rec_dve(dve, ch)
            states_dve(dve)
            proj_dve(dve, OUT0, 3)
            ffn_dve(dve, 1, FFN1, None)
            out_dve(dve)

        @block.tensor
        def _(pe):
            transpose_inputs(pe)
            down_pe(pe)
            uq_pe(pe)
            values_pe(pe)
            prompt_pe(pe)
            sample_pe(pe)
            attention_out_pe(pe)
            ffn_pe(pe, 0, FFN0, 1)
            rec_pe(pe)
            rec_out_pe(pe)
            ffn_pe(pe, 1, FFN1, 3)
            out_pe(pe)


_INS = ["x_prompt", "x_sample", "cache_ckv", "cache_krope", "page_table", "state_lru_h", "state_lru_conv",
        "state_ffn_conv", "norm_mix", "norm_ffn", "attn_w_down", "attn_g_q_lora", "attn_w_uq", "attn_g_kv_lora",
        "attn_g_qn", "attn_g_qr", "attn_g_kn", "attn_g_kr", "attn_w_uk", "attn_w_uv", "attn_w_o", "rec_w_in",
        "rec_conv_w", "rec_conv_b", "rec_w_a", "rec_b_a", "rec_w_i", "rec_b_i", "rec_lambda", "rec_w_out",
        "ffn_w_up", "ffn_conv_w", "ffn_conv_b", "ffn_w_down"]
_OUTS = [("y_prompt", (1, TP, D)), ("y_sample", (NB, TS, D)), ("ckv_prompt", (1, 1, TP, KL)),
         ("krope_prompt", (1, 1, TP, DR)), ("ckv_sample", (1, NB, TS, KL)), ("krope_sample", (1, NB, TS, DR)),
         ("lru_h_prompt", (1, 1, D)), ("lru_h_sample", (1, NB, D)), ("lru_conv_prompt", (1, 1, RW - 1, D)),
         ("lru_conv_sample", (1, NB, RW - 1, D)), ("ffn_conv_prompt", (2, 1, FW - 1, FF)),
         ("ffn_conv_sample", (2, NB, FW - 1, FF))]


def constants():
    import numpy as np

    c = np.zeros((P, C_ALL), np.float32)
    i = np.arange(P)
    c[:, C_ID:C_ID + P] = np.eye(P)
    c[:, C_ONE:C_ONE + P] = 1.0
    c[:, C_B64:C_B64 + P] = i[:, None] // 64 == i[None, :] // 64
    c[:, C_B32:C_B32 + P] = i[:, None] // 32 == i[None, :] // 32
    same = i[:, None] // DR == i[None, :] // DR
    k, m = i[:, None] % DR, i[None, :] % DR
    half = DR // 2
    c[:, C_ROT:C_ROT + P] = same * ((k == m - half) * 1.0 - (k == m + half) * 1.0)
    c[:, C_CM:C_CM + P] = np.where(i[None, :] <= i[:, None], 0.0, NEG)
    j = np.arange(TN)
    ok = (j[:, None] // TS == j[None, :] // TS) & (j[:, None] <= j[None, :])
    c[:TN, C_NM:C_NM + TN] = np.where(ok, 0.0, NEG)
    pos = np.concatenate([np.arange(TP), PAGES * PAGE + np.arange(TN) % TS]).astype(np.float32)
    inv = (np.float32(10000.0) ** (-np.arange(0, DR, 2, dtype=np.float32) / np.float32(DR))).astype(np.float32)
    ang = (pos[None, :] * inv[(i % half)][:, None]).astype(np.float32).astype(np.float64)
    c[:, C_COS:C_COS + T] = np.cos(ang)
    c[:, C_SIN:C_SIN + T] = np.sin(ang)
    return c


def kernel(**inputs):
    import numpy as _np
    import concourse.bacc as _bacc
    from concourse import mybir as _mybir
    from concourse.bass_utils import run_bass_kernel_spmd as _run

    nc = _bacc.Bacc("TRN2", target_bir_lowering=False, num_devices=1, dynamic_dma_scratch_size=1024)
    arrays, I, O = {}, {}, {}
    for name in _INS + ["consts"]:
        a = constants() if name == "consts" else _np.ascontiguousarray(inputs[name])
        arrays[f"in_{name}"] = a
        I[name] = nc.dram_tensor(f"in_{name}", a.shape, _mybir.dt.from_np(a.dtype), kind="ExternalInput").ap()
    for name, shape in _OUTS:
        O[name] = nc.dram_tensor(f"out_{name}", shape, F32, kind="ExternalOutput").ap()
    build(nc, I, O)
    r = _run(nc, [arrays], core_ids=[0])
    return tuple(r.results[0][f"out_{name}"] for name, _ in _OUTS)
```
